# Optimizing a Trainium2 kernel written in Bass

```python
import jax, jax.numpy as jnp
from jax import lax
import numpy as np
import math

D_MODEL = 1024
BATCH = 1
SEQ = 512
DEPTH = 1

MIX_WIDTH = D_MODEL
A_HEADS = 4
A_DV = MIX_WIDTH // 2 // A_HEADS
A_DK = A_DV // 2
B_HEADS = 4
B_DV = MIX_WIDTH // 2 // B_HEADS
B_DK = B_DV // 2
A_QK = A_HEADS * A_DK
A_V = A_HEADS * A_DV
B_QK = B_HEADS * B_DK
B_V = B_HEADS * B_DV
GLA_RANK = 16
GLA_GATE_TEMP = 16.0
CONV_W = 3
D_FF = 2816
CHUNK = 64
EPS = 1e-6
IN_WIDTHS = (2 * A_QK, A_V, A_V, 4 * A_HEADS, B_QK, B_QK, B_V, B_V, 2 * GLA_RANK)
IN_COLS = 2 * A_QK + A_V + A_V + 4 * A_HEADS + B_QK + B_QK + B_V + B_V + 2 * GLA_RANK


def rms_norm(x, g):
    xf = x.astype(jnp.float32)
    y = xf * lax.rsqrt(jnp.mean(xf * xf, axis=-1, keepdims=True) + EPS)
    return (y * g.astype(jnp.float32)).astype(x.dtype)

def head_rms_norm(y, g):
    y = y * lax.rsqrt(jnp.mean(y * y, axis=-1, keepdims=True) + EPS)
    return y * g.astype(jnp.float32)

def dwconv3(x, w, b):
    xp = jnp.pad(x, ((0, 0), (1, 1), (0, 0)))
    return xp[:, :-2] * w[0] + xp[:, 1:-1] * w[1] + xp[:, 2:] * w[2] + b

def flip(t):
    return t[:, ::-1]

def to_chunks(t):
    b, s, h = t.shape[:3]
    t = t.reshape((b, s // CHUNK, CHUNK, h) + t.shape[3:])
    return jnp.moveaxis(t, (1, 3), (0, 2))

def from_chunks(y):
    y = jnp.moveaxis(y, (0, 2), (1, 3))
    b, nc, l, h, d = y.shape
    return y.reshape(b, nc * l, h, d)

def mlstm_chunkwise(q, k, v, i_pre, log_f):
    bsz, _, h, dk = q.shape
    dv = v.shape[-1]
    causal = jnp.tril(jnp.ones((CHUNK, CHUNK), dtype=bool))

    def step(carry, inp):
        c_st, n_st, m_st = carry
        q_, k_, v_, i_, f_ = inp
        b = jnp.cumsum(f_, axis=-1)
        d_intra = jnp.where(causal, b[..., :, None] - b[..., None, :] + i_[..., None, :], -jnp.inf)
        m_inter = b + m_st[..., None]
        m_t = jnp.maximum(m_inter, jnp.max(d_intra, axis=-1))
        s = jnp.einsum('bhtd,bhsd->bhts', q_, k_) * jnp.exp(d_intra - m_t[..., None])
        inter = jnp.exp(m_inter - m_t)
        num = jnp.einsum('bhts,bhse->bhte', s, v_) + inter[..., None] * jnp.einsum('bhtd,bhde->bhte', q_, c_st)
        den = jnp.sum(s, axis=-1) + inter * jnp.einsum('bhtd,bhd->bht', q_, n_st)
        h_out = num / jnp.maximum(jnp.abs(den), jnp.exp(-m_t))[..., None]
        b_last = b[..., -1]
        g = b_last[..., None] - b + i_
        m_new = jnp.maximum(b_last + m_st, jnp.max(g, axis=-1))
        decay = jnp.exp(b_last + m_st - m_new)
        wk = jnp.exp(g - m_new[..., None])[..., None] * k_
        c_new = decay[..., None, None] * c_st + jnp.einsum('bhsd,bhse->bhde', wk, v_)
        n_new = decay[..., None] * n_st + jnp.sum(wk, axis=-2)
        return (c_new, n_new, m_new), h_out

    init = (jnp.zeros((bsz, h, dk, dv), jnp.float32),
            jnp.zeros((bsz, h, dk), jnp.float32),
            jnp.zeros((bsz, h), jnp.float32))
    _, hs = lax.scan(step, init, (to_chunks(q), to_chunks(k), to_chunks(v),
                                  to_chunks(i_pre), to_chunks(log_f)))
    return from_chunks(hs)

def gla_chunkwise(q, k, v, log_a):
    bsz, _, h, dk = q.shape
    dv = v.shape[-1]
    causal = jnp.tril(jnp.ones((CHUNK, CHUNK), dtype=bool))[..., None]

    def step(s_st, inp):
        q_, k_, v_, a_ = inp
        b = jnp.cumsum(a_, axis=-2)
        diff = b[..., :, None, :] - b[..., None, :, :]
        decay = jnp.exp(jnp.where(causal, diff, -jnp.inf))
        s = jnp.einsum('bhtd,bhsd,bhtsd->bhts', q_, k_, decay)
        o = jnp.einsum('bhts,bhse->bhte', s, v_) + jnp.einsum('bhtd,bhde->bhte', q_ * jnp.exp(b), s_st)
        b_last = b[..., -1:, :]
        k_dec = k_ * jnp.exp(b_last - b)
        s_new = jnp.exp(b_last[..., 0, :])[..., None] * s_st + jnp.einsum('bhsd,bhse->bhde', k_dec, v_)
        return s_new, o

    init = jnp.zeros((bsz, h, dk, dv), jnp.float32)
    _, os_ = lax.scan(step, init, (to_chunks(q), to_chunks(k), to_chunks(v), to_chunks(log_a)))
    return from_chunks(os_)

def hybrid_mixer(hn, w_in, mlstm_gate_b, mlstm_conv_w, mlstm_conv_b, mlstm_norm,
                 gla_w2, gla_b, gla_norm, w_out):
    bsz, s, _ = hn.shape
    proj = jnp.matmul(hn, w_in).astype(jnp.float32)
    idx = np.cumsum(np.array(IN_WIDTHS))[:-1].tolist()
    a_qk, a_v, a_o, a_gates, b_q, b_k, b_v, b_r, b_lr = jnp.split(proj, idx, axis=-1)

    qk = jax.nn.silu(dwconv3(a_qk, mlstm_conv_w.astype(jnp.float32), mlstm_conv_b.astype(jnp.float32)))
    q_a = qk[..., :A_QK].reshape(bsz, s, A_HEADS, A_DK)
    k_a = qk[..., A_QK:].reshape(bsz, s, A_HEADS, A_DK) * (A_DK ** -0.5)
    v_a = a_v.reshape(bsz, s, A_HEADS, A_DV)
    gates = a_gates + mlstm_gate_b.astype(jnp.float32)
    i_fw, f_fw, i_bw, f_bw = jnp.split(gates, 4, axis=-1)
    h_fw = mlstm_chunkwise(q_a, k_a, v_a, i_fw, jax.nn.log_sigmoid(f_fw))
    h_bw = flip(mlstm_chunkwise(flip(q_a), flip(k_a), flip(v_a), flip(i_bw), flip(jax.nn.log_sigmoid(f_bw))))
    y_a = jax.nn.sigmoid(a_o) * head_rms_norm(h_fw + h_bw, mlstm_norm).reshape(bsz, s, A_V)

    q_b = b_q.reshape(bsz, s, B_HEADS, B_DK) * (B_DK ** -0.5)
    k_b = b_k.reshape(bsz, s, B_HEADS, B_DK)
    v_b = b_v.reshape(bsz, s, B_HEADS, B_DV)
    lr_fw, lr_bw = jnp.split(b_lr, 2, axis=-1)
    w2 = gla_w2.astype(jnp.float32)
    gb = gla_b.astype(jnp.float32)
    la_fw = (jax.nn.log_sigmoid(lr_fw @ w2[0] + gb[0]) / GLA_GATE_TEMP).reshape(bsz, s, B_HEADS, B_DK)
    la_bw = (jax.nn.log_sigmoid(lr_bw @ w2[1] + gb[1]) / GLA_GATE_TEMP).reshape(bsz, s, B_HEADS, B_DK)
    o_fw = gla_chunkwise(q_b, k_b, v_b, la_fw)
    o_bw = flip(gla_chunkwise(flip(q_b), flip(k_b), flip(v_b), flip(la_bw)))
    y_b = jax.nn.silu(b_r) * head_rms_norm(o_fw + o_bw, gla_norm).reshape(bsz, s, B_V)

    y = jnp.concatenate([y_a, y_b], axis=-1).astype(hn.dtype)
    return jnp.matmul(y, w_out)

def conv_ffn(hn, w_gate, w_up, conv_w, conv_b, w_down):
    g = dwconv3(jnp.matmul(hn, w_gate), conv_w, conv_b)
    u = jnp.matmul(hn, w_up)
    return jnp.matmul(jax.nn.gelu(g, approximate=True) * u, w_down)

def first_inputs(seed: int = 0) -> dict:
    key = jax.random.key(seed)
    ks = jax.random.split(key, 20)
    f32 = jnp.float32

    def nrm(k, shape, scale):
        return jax.random.normal(k, shape, f32) * scale

    def gain(k, shape):
        return 1.0 + 0.05 * jax.random.normal(k, shape, f32)

    f_base = jnp.linspace(3.0, 6.0, A_HEADS, dtype=f32)
    i_base = jnp.zeros((A_HEADS,), f32)
    gate_base = jnp.concatenate([i_base, f_base, i_base, f_base])
    return {
        "x": nrm(ks[0], (BATCH, SEQ, D_MODEL), 1.0),
        "norm_mix_pre": gain(ks[1], (DEPTH, D_MODEL)),
        "norm_mix_post": gain(ks[2], (DEPTH, D_MODEL)),
        "norm_ffn_pre": gain(ks[3], (DEPTH, D_MODEL)),
        "norm_ffn_post": gain(ks[4], (DEPTH, D_MODEL)),
        "w_in": nrm(ks[5], (DEPTH, D_MODEL, IN_COLS), D_MODEL ** -0.5),
        "mlstm_gate_b": gate_base + nrm(ks[6], (DEPTH, 4 * A_HEADS), 0.1),
        "mlstm_conv_w": nrm(ks[7], (DEPTH, CONV_W, 2 * A_QK), CONV_W ** -0.5),
        "mlstm_conv_b": nrm(ks[8], (DEPTH, 2 * A_QK), 0.02),
        "mlstm_norm": gain(ks[9], (DEPTH, A_HEADS, A_DV)),
        "gla_w2": nrm(ks[10], (DEPTH, 2, GLA_RANK, B_QK), GLA_RANK ** -0.5),
        "gla_b": nrm(ks[11], (DEPTH, 2, B_QK), 0.02),
        "gla_norm": gain(ks[12], (DEPTH, B_HEADS, B_DV)),
        "w_out": nrm(ks[13], (DEPTH, MIX_WIDTH, D_MODEL), MIX_WIDTH ** -0.5),
        "ffn_w_gate": nrm(ks[14], (DEPTH, D_MODEL, D_FF), D_MODEL ** -0.5),
        "ffn_w_up": nrm(ks[15], (DEPTH, D_MODEL, D_FF), D_MODEL ** -0.5),
        "ffn_conv_w": nrm(ks[16], (DEPTH, CONV_W, D_FF), CONV_W ** -0.5),
        "ffn_conv_b": nrm(ks[17], (DEPTH, D_FF), 0.02),
        "ffn_w_down": nrm(ks[18], (DEPTH, D_FF, D_MODEL), D_FF ** -0.5),
    }

def first_block(x, norm_mix_pre, norm_mix_post, norm_ffn_pre, norm_ffn_post, w_in,
              mlstm_gate_b, mlstm_conv_w, mlstm_conv_b, mlstm_norm, gla_w2, gla_b, gla_norm,
              w_out, ffn_w_gate, ffn_w_up, ffn_conv_w, ffn_conv_b, ffn_w_down):
    for l in range(DEPTH):
        hn = rms_norm(x, norm_mix_pre[l])
        mix = hybrid_mixer(hn, w_in[l], mlstm_gate_b[l], mlstm_conv_w[l], mlstm_conv_b[l], mlstm_norm[l],
                           gla_w2[l], gla_b[l], gla_norm[l], w_out[l])
        x = x + rms_norm(mix, norm_mix_post[l])
        hn = rms_norm(x, norm_ffn_pre[l])
        ff = conv_ffn(hn, ffn_w_gate[l], ffn_w_up[l], ffn_conv_w[l], ffn_conv_b[l], ffn_w_down[l])
        x = x + rms_norm(ff, norm_ffn_post[l])
    return x


DEPTH_2 = 2

N_EVEN = (DEPTH_2 + 1) // 2
N_ODD = DEPTH_2 // 2

MEM_LEN = 256
XA_HEADS = 4
XA_HEAD_DIM = D_MODEL // XA_HEADS

POOL_W = D_MODEL // 2
POOL_WINDOWS = (2, 4, 8, 16)
N_POOL_GROUPS = len(POOL_WINDOWS)
POOL_GROUP = POOL_W // N_POOL_GROUPS
CONV_W_2 = D_MODEL // 2
CONV_K = 31

MLA_HEADS = 16
QK_NOPE = 64
QK_ROPE = 32
V_HEAD = 64
Q_LORA = 384
KV_LORA = 256
ROPE_THETA = 10000.0
Q_BLOCK = 128
MLA_SCALE = 1.0 / math.sqrt(QK_NOPE + QK_ROPE)

FFN_CONV_K = 3

NEG = -1e30


def rmsnorm(x, g):
    xf = x.astype(jnp.float32)
    y = xf * lax.rsqrt(jnp.mean(xf * xf, axis=-1, keepdims=True) + EPS)
    return (y * g.astype(jnp.float32)).astype(x.dtype)

def layernorm(x, g, b):
    xf = x.astype(jnp.float32)
    mu = jnp.mean(xf, axis=-1, keepdims=True)
    xc = xf - mu
    y = xc * lax.rsqrt(jnp.mean(xc * xc, axis=-1, keepdims=True) + EPS)
    return (y * g.astype(jnp.float32) + b.astype(jnp.float32)).astype(x.dtype)

def causal_dwconv(u, w):
    k = w.shape[0]
    return lax.conv_general_dilated(
        u, w[:, None, :], window_strides=(1,), padding=[(k - 1, 0)],
        dimension_numbers=("NWC", "WIO", "NWC"), feature_group_count=u.shape[-1])

def window_mean_minus_self(u, w):
    t = u.shape[1]
    uf = u.astype(jnp.float32)
    cs = jnp.cumsum(uf, axis=1)
    cs_lag = jnp.pad(cs, ((0, 0), (w, 0), (0, 0)))[:, :t]
    cnt = jnp.minimum(jnp.arange(t) + 1, w).astype(jnp.float32)
    return ((cs - cs_lag) / cnt[None, :, None] - uf).astype(u.dtype)

def rope_tables(positions):
    inv = 1.0 / (ROPE_THETA ** (jnp.arange(0, QK_ROPE, 2, dtype=jnp.float32) / QK_ROPE))
    ang = positions.astype(jnp.float32)[..., None] * inv
    return jnp.cos(ang), jnp.sin(ang)

def apply_rope(x, cos, sin):
    half = x.shape[-1] // 2
    c = cos.astype(x.dtype)
    s = sin.astype(x.dtype)
    x1, x2 = x[..., :half], x[..., half:]
    return jnp.concatenate([x1 * c - x2 * s, x1 * s + x2 * c], axis=-1)

def pool_conv_mixer(h, w_in, pool_w, pool_scale, dw_w, dw_b, ln_g, ln_b, w_out):
    b, t, _ = h.shape
    z = h @ w_in
    u, glu_a, glu_b = jnp.split(z, [POOL_W, POOL_W + CONV_W_2], axis=-1)
    ug = u.reshape(b, t, N_POOL_GROUPS, POOL_GROUP)
    pooled = jnp.stack([window_mean_minus_self(ug[:, :, i], w)
                        for i, w in enumerate(POOL_WINDOWS)], axis=2)
    ya = jnp.einsum("btgc,gcd->btgd", pooled, pool_w).reshape(b, t, POOL_W) * pool_scale
    gl = glu_a * jax.nn.sigmoid(glu_b)
    cv = causal_dwconv(gl, dw_w) + dw_b
    yb = jax.nn.silu(layernorm(cv, ln_g, ln_b))
    return jnp.concatenate([ya, yb], axis=-1) @ w_out

def mla_attention(h, cos, sin, w_dq_dkv, q_norm_g, w_uq, kv_norm_g, w_ukv, w_o):
    b, t, _ = h.shape
    c = h @ w_dq_dkv
    cq, ckv, k_pe = jnp.split(c, [Q_LORA, Q_LORA + KV_LORA], axis=-1)
    q = (rmsnorm(cq, q_norm_g) @ w_uq).reshape(b, t, MLA_HEADS, QK_NOPE + QK_ROPE)
    q_nope = q[..., :QK_NOPE]
    q_pe = apply_rope(q[..., QK_NOPE:], cos[:, :, None, :], sin[:, :, None, :])
    kv = (rmsnorm(ckv, kv_norm_g) @ w_ukv).reshape(b, t, MLA_HEADS, QK_NOPE + V_HEAD)
    k_nope, v = kv[..., :QK_NOPE], kv[..., QK_NOPE:]
    k_pe = apply_rope(k_pe, cos, sin)
    nb = t // Q_BLOCK
    kpos = jnp.arange(t)

    def block(args):
        qn, qp, i = args
        s = (jnp.einsum("bqhd,bkhd->bhqk", qn, k_nope)
             + jnp.einsum("bqhr,bkr->bhqk", qp, k_pe)).astype(jnp.float32) * MLA_SCALE
        qpos = i * Q_BLOCK + jnp.arange(Q_BLOCK)
        s = jnp.where(kpos[None, :] <= qpos[:, None], s, NEG)
        p = jax.nn.softmax(s, axis=-1).astype(v.dtype)
        return jnp.einsum("bhqk,bkhd->bqhd", p, v)

    qn_b = q_nope.reshape(b, nb, Q_BLOCK, MLA_HEADS, QK_NOPE).transpose(1, 0, 2, 3, 4)
    qp_b = q_pe.reshape(b, nb, Q_BLOCK, MLA_HEADS, QK_ROPE).transpose(1, 0, 2, 3, 4)
    o = lax.map(block, (qn_b, qp_b, jnp.arange(nb)))
    o = o.transpose(1, 0, 2, 3, 4).reshape(b, t, MLA_HEADS * V_HEAD)
    return o @ w_o

def memory_cross_attention(h, m, wq, wkv, wo):
    b, t, _ = h.shape
    q = (h @ wq).reshape(b, t, XA_HEADS, XA_HEAD_DIM)
    k, v = jnp.split(m @ wkv, 2, axis=-1)
    k = k.reshape(b, MEM_LEN, XA_HEADS, XA_HEAD_DIM)
    v = v.reshape(b, MEM_LEN, XA_HEADS, XA_HEAD_DIM)
    s = jnp.einsum("bthd,bmhd->bhtm", q, k).astype(jnp.float32) * (XA_HEAD_DIM ** -0.5)
    p = jax.nn.softmax(s, axis=-1).astype(v.dtype)
    o = jnp.einsum("bhtm,bmhd->bthd", p, v).reshape(b, t, D_MODEL)
    return o @ wo

def conv_ffn_2(h, w_up, conv_w, conv_b, w_down):
    a, g = jnp.split(h @ w_up, 2, axis=-1)
    g = causal_dwconv(g, conv_w) + conv_b
    return (jax.nn.silu(g) * a) @ w_down

def second_inputs(seed: int = 0) -> dict:
    key = jax.random.key(seed)
    ks = iter(jax.random.split(key, 40))
    f32 = jnp.float32

    def dense(shape, fan_in, scale=1.0):
        return jax.random.normal(next(ks), shape, f32) * (scale * fan_in ** -0.5)

    def gain(shape):
        return 1.0 + 0.02 * jax.random.normal(next(ks), shape, f32)

    def bias(shape):
        return 0.01 * jax.random.normal(next(ks), shape, f32)

    out_scale = 0.5
    x = jax.random.normal(next(ks), (BATCH, SEQ, D_MODEL), f32)
    mem = jax.random.normal(next(ks), (BATCH, MEM_LEN, D_MODEL), f32)
    offsets = jax.random.randint(next(ks), (BATCH, 1), 0, 4096, dtype=jnp.int32)
    positions = offsets + jnp.arange(SEQ, dtype=jnp.int32)[None, :]
    return {
        "x": x,
        "mem": mem,
        "positions": positions,
        "norm_mix_g": gain((DEPTH_2, D_MODEL)),
        "norm_xa_g": gain((DEPTH_2, D_MODEL)),
        "norm_mem_g": gain((DEPTH_2, D_MODEL)),
        "xa_wq": dense((DEPTH_2, D_MODEL, D_MODEL), D_MODEL),
        "xa_wkv": dense((DEPTH_2, D_MODEL, 2 * D_MODEL), D_MODEL),
        "xa_wo": dense((DEPTH_2, D_MODEL, D_MODEL), D_MODEL, out_scale),
        "norm_ffn_g": gain((DEPTH_2, D_MODEL)),
        "ffn_w_up": dense((DEPTH_2, D_MODEL, 2 * D_FF), D_MODEL),
        "ffn_conv_w": dense((DEPTH_2, FFN_CONV_K, D_FF), FFN_CONV_K),
        "ffn_conv_b": bias((DEPTH_2, D_FF)),
        "ffn_w_down": dense((DEPTH_2, D_FF, D_MODEL), D_FF, out_scale),
        "pc_w_in": dense((N_EVEN, D_MODEL, POOL_W + 2 * CONV_W_2), D_MODEL),
        "pool_w": dense((N_EVEN, N_POOL_GROUPS, POOL_GROUP, POOL_GROUP), POOL_GROUP),
        "pool_scale": gain((N_EVEN, POOL_W)),
        "conv_dw_w": dense((N_EVEN, CONV_K, CONV_W_2), CONV_K),
        "conv_dw_b": bias((N_EVEN, CONV_W_2)),
        "conv_ln_g": gain((N_EVEN, CONV_W_2)),
        "conv_ln_b": bias((N_EVEN, CONV_W_2)),
        "pc_w_out": dense((N_EVEN, POOL_W + CONV_W_2, D_MODEL), POOL_W + CONV_W_2, out_scale),
        "mla_w_dq_dkv": dense((N_ODD, D_MODEL, Q_LORA + KV_LORA + QK_ROPE), D_MODEL),
        "mla_q_norm_g": gain((N_ODD, Q_LORA)),
        "mla_w_uq": dense((N_ODD, Q_LORA, MLA_HEADS * (QK_NOPE + QK_ROPE)), Q_LORA),
        "mla_kv_norm_g": gain((N_ODD, KV_LORA)),
        "mla_w_ukv": dense((N_ODD, KV_LORA, MLA_HEADS * (QK_NOPE + V_HEAD)), KV_LORA),
        "mla_w_o": dense((N_ODD, MLA_HEADS * V_HEAD, D_MODEL), MLA_HEADS * V_HEAD, out_scale),
        "final_norm_g": gain((D_MODEL,)),
    }

def second_block(x, mem, positions, norm_mix_g, norm_xa_g, norm_mem_g, xa_wq, xa_wkv, xa_wo,
              norm_ffn_g, ffn_w_up, ffn_conv_w, ffn_conv_b, ffn_w_down,
              pc_w_in, pool_w, pool_scale, conv_dw_w, conv_dw_b, conv_ln_g, conv_ln_b, pc_w_out,
              mla_w_dq_dkv, mla_q_norm_g, mla_w_uq, mla_kv_norm_g, mla_w_ukv, mla_w_o,
              final_norm_g):
    cos, sin = rope_tables(positions)
    for l in range(DEPTH_2):
        h = rmsnorm(x, norm_mix_g[l])
        if l % 2 == 0:
            e = l // 2
            x = x + pool_conv_mixer(h, pc_w_in[e], pool_w[e], pool_scale[e], conv_dw_w[e],
                                    conv_dw_b[e], conv_ln_g[e], conv_ln_b[e], pc_w_out[e])
        else:
            o = l // 2
            x = x + mla_attention(h, cos, sin, mla_w_dq_dkv[o], mla_q_norm_g[o], mla_w_uq[o],
                                  mla_kv_norm_g[o], mla_w_ukv[o], mla_w_o[o])
        x = x + memory_cross_attention(rmsnorm(x, norm_xa_g[l]), rmsnorm(mem, norm_mem_g[l]),
                                       xa_wq[l], xa_wkv[l], xa_wo[l])
        x = x + conv_ffn_2(rmsnorm(x, norm_ffn_g[l]), ffn_w_up[l], ffn_conv_w[l], ffn_conv_b[l],
                         ffn_w_down[l])
    return rmsnorm(x, final_norm_g)


def setup_inputs(seed=0):
    out = dict(first_inputs(seed))
    for name, value in second_inputs(seed + 1).items():
        if name != "x":
            out[name + "_2"] = value
    return out


def reference(
    x, norm_mix_pre, norm_mix_post, norm_ffn_pre, norm_ffn_post, w_in, mlstm_gate_b,
    mlstm_conv_w, mlstm_conv_b, mlstm_norm, gla_w2, gla_b, gla_norm, w_out, ffn_w_gate,
    ffn_w_up, ffn_conv_w, ffn_conv_b, ffn_w_down, mem_2, positions_2, norm_mix_g_2, norm_xa_g_2,
    norm_mem_g_2, xa_wq_2, xa_wkv_2, xa_wo_2, norm_ffn_g_2, ffn_w_up_2, ffn_conv_w_2,
    ffn_conv_b_2, ffn_w_down_2, pc_w_in_2, pool_w_2, pool_scale_2, conv_dw_w_2, conv_dw_b_2,
    conv_ln_g_2, conv_ln_b_2, pc_w_out_2, mla_w_dq_dkv_2, mla_q_norm_g_2, mla_w_uq_2,
    mla_kv_norm_g_2, mla_w_ukv_2, mla_w_o_2, final_norm_g_2,
):
    x = first_block(
        x, norm_mix_pre, norm_mix_post, norm_ffn_pre, norm_ffn_post, w_in, mlstm_gate_b,
        mlstm_conv_w, mlstm_conv_b, mlstm_norm, gla_w2, gla_b, gla_norm, w_out, ffn_w_gate,
        ffn_w_up, ffn_conv_w, ffn_conv_b, ffn_w_down,
    )
    return second_block(
        x, mem_2, positions_2, norm_mix_g_2, norm_xa_g_2, norm_mem_g_2, xa_wq_2, xa_wkv_2,
        xa_wo_2, norm_ffn_g_2, ffn_w_up_2, ffn_conv_w_2, ffn_conv_b_2, ffn_w_down_2, pc_w_in_2,
        pool_w_2, pool_scale_2, conv_dw_w_2, conv_dw_b_2, conv_ln_g_2, conv_ln_b_2, pc_w_out_2,
        mla_w_dq_dkv_2, mla_q_norm_g_2, mla_w_uq_2, mla_kv_norm_g_2, mla_w_ukv_2, mla_w_o_2,
        final_norm_g_2,
    )


_drawn_inputs = setup_inputs


def setup_inputs(seed=0):
    import zlib

    import numpy as np

    out = dict(_drawn_inputs(seed))
    spreads = {}
    factors = {'mlstm_conv_b': 3.42,
     'gla_b': 8.0,
     'ffn_conv_b': 4.706,
     'norm_mix_g_2': 8.0,
     'norm_xa_g_2': 8.0,
     'norm_mem_g_2': 8.0,
     'norm_ffn_g_2': 8.0,
     'ffn_conv_b_2': 8.0,
     'pool_scale_2': 8.0,
     'conv_dw_b_2': 22.59,
     'conv_ln_g_2': 21.65,
     'conv_ln_b_2': 30.372,
     'mla_q_norm_g_2': 8.0,
     'mla_kv_norm_g_2': 8.0,
     'final_norm_g_2': 8.419}
    for name, (base, spread) in spreads.items():
        noise = np.random.default_rng([zlib.crc32(name.encode()), seed]).standard_normal(out[name].shape)
        drawn = base * np.exp(spread * noise) if base else spread * noise
        out[name] = __import__('jax').numpy.asarray(drawn.astype(out[name].dtype))
    for name, factor in factors.items():
        out[name] = (out[name] * factor).astype(out[name].dtype)
    return out
```

```python
import numpy as np
import concourse.bass as bass
from concourse import mybir
from contextlib import ExitStack

F32 = mybir.dt.float32
F32R = mybir.dt.float32r
I32 = mybir.dt.int32
ALU = mybir.AluOpType
ACT = mybir.ActivationFunctionType
AX = mybir.AxisListType

P = 128
S = 512
D = 1024
KD = D // P
NB = S // P
MEM = 256
FF = 2816
NF = FF // P
THIRDS = (8, 8, 6)
RING = 4
UNIT = 1024
BIG = 1e30
HALVES = (1, 2, 4, 8, 16, 32, 64)
POOL_WINDOWS = (2, 4, 8, 16)
CONV_K = 31
MLA_HEADS = 16
TWO_PI = 6.283185307179586
TWO_PI_A = 6.28125
TWO_PI_B = 0.0019350051879882812
TWO_PI_C = TWO_PI - TWO_PI_A - TWO_PI_B
ROUND = 12582912.0

VEC_SIZES = [("mix_pre", 8), ("mix_post", 8), ("ffn_pre", 8), ("ffn_post", 8), ("mix2_0", 8), ("mix2_1", 8),
             ("xa0", 8), ("xa1", 8), ("mem0", 8), ("mem1", 8), ("ffn2_0", 8), ("ffn2_1", 8), ("final", 8),
             ("mconv_w", 12), ("mconv_b", 4), ("mnorm", 4), ("gla_b", 4), ("gnorm", 4),
             ("fconv_w0", 66), ("fconv_b0", 22), ("fconv_w1", 66), ("fconv_b1", 22), ("fconv_w2", 66), ("fconv_b2", 22),
             ("pool_scale", 4), ("dw_w", 4 * CONV_K), ("dw_b", 4), ("ln_g", 4), ("ln_b", 4),
             ("q_norm", 3), ("kv_norm", 2), ("gate_b", 16), ("eps", 1), ("one", 1)]
VEC, _at = {}, 0
for _n, _w in VEC_SIZES:
    VEC[_n] = _at
    _at += _w
NVEC = _at

CONST_SIZES = [("ident", 128), ("ones", 128), ("past", 128), ("future", 128), ("upto", 128), ("since", 128),
               ("twice", 128), ("neg_future", 128), ("inv_count", 64), ("inv_freq", 16)]
CONST, _at = {}, 0
for _n, _w in CONST_SIZES:
    CONST[_n] = _at
    _at += _w
NCONST = _at

UNITS = [("lr_gates", 1, 8 * 48), ("a_qk", 4, 1024), ("b_qk", 4, 1024), ("a_v", 4, 1024), ("b_v", 4, 1024),
         ("a_o", 4, 1024), ("b_r", 4, 1024), ("w_out", 8, 1024)]
for _i in range(3):
    if _i == 1:
        UNITS += [("pc_in", 12, 1024), ("mem_k0", 8, 1024), ("mem_v0", 8, 1024), ("mem_k1", 8, 1024),
                  ("mem_v1", 8, 1024), ("pc_out", 8, 1024)]
    if _i == 2:
        UNITS += [("k_pe", 1, 256), ("w_dq", 5, 1024), ("q_nope", 4, 768), ("q_pe", 2, 1024),
                  ("k_nope", 2, 1024), ("mla_v", 2, 1024), ("mla_o", 8, 1024)]
    if _i > 0:
        UNITS += [(f"xq{_i - 1}", 8, 1024), (f"xo{_i - 1}", 8, 1024)]
    for _t, _c in enumerate(THIRDS):
        UNITS += [(f"ff{_i}_gu{_t}", 2 * _c, 1024), (f"ff{_i}_d{_t}", 8, _c * 128)]
UNIT0, _at = {}, 0
for _n, _c, _w in UNITS:
    UNIT0[_n] = _at
    _at += _c
NUNITS = _at

TILES = [("col_sum1", 1), ("row_sum1", 1), ("gates", 1), ("lr", 1), ("a_qk", 4), ("cum", 1), ("b_qk", 4),
         ("log_a", 4), ("gate_rows", 2), ("a_v", 4), ("b_v", 4), ("a_o", 4), ("b_r", 4)]
for _n in range(9):
    if _n < 8:
        TILES += ([(f"s{_n // 2}", 4)] if _n % 2 == 0 else []) + [(f"max{_n}", 1), (f"guard{_n}", 1)]
    if _n > 0:
        TILES += [(f"num{_n - 1}", 1), (f"den{_n - 1}", 1)]
TILES += [("norm_a", 4)]
for _c in range(2):
    TILES += [(f"lev{_c}_{_l}", 2) for _l in range(9)] + [(f"lev{_c}_9", 4), (f"o{_c}", 2)]
TILES += [("norm_b", 4), ("w_out", 8), ("post0", 1)]
for _i in range(3):
    if _i == 1:
        TILES += [("post1", 1), ("row_sum3", 1), ("pc_in", 12), ("mem_sums", 1), ("mem_k0", 8), ("mem_v0", 4), ("mem_k1", 8),
                  ("mem_v1", 4), ("pool", 4), ("ln_mean", 1), ("ln_var", 1), ("pc_out", 8)]
    if _i == 2:
        TILES += [("row_sum6", 1), ("col_sum6", 1), ("k_pe", 1), ("w_dq", 5), ("q_sum", 2), ("kv_sum", 2),
                  ("q_nope", 8), ("q_pe", 4), ("k_nope", 8), ("mla_v", 8), ("pe_turn", 5)]
        TILES += [("att", 9 * MLA_HEADS), ("mla_o", 8)]
    if _i > 0:
        TILES += [(f"row_sum_x{_i - 1}", 1), (f"xq{_i - 1}", 8), (f"xatt{_i - 1}", 24), (f"xo{_i - 1}", 8)]
    TILES += [(f"row_sum_f{_i}", 1)]
    for _t, _c in enumerate(THIRDS):
        TILES += [(f"ff{_i}_gu{_t}", 2 * _c), (f"ff{_i}_d{_t}", 8)]
TILES += [("row_sum_end", 1)]

TILE0, TILE_DONE, _at, _others = {}, [], 0, 0
_count = {n: k for n, k, _ in UNITS}
for _n, _c in TILES:
    TILE0[_n] = _at
    _at += _c
    for _i in range(_c):
        if _n in ("gates", "lr"):
            TILE_DONE.append(("unit", UNIT0["lr_gates"] + 1))
        elif _n in _count:
            _per = max(1, _c // _count[_n])
            if _n in ("a_v", "b_v", "q_pe"):
                TILE_DONE.append(("unit", UNIT0[_n] + _count[_n]))
            elif _n.startswith("mem_v"):
                TILE_DONE.append(("unit", UNIT0[_n] + 4 * (_i // 2) + 4))
            else:
                TILE_DONE.append(("unit", UNIT0[_n] + _i // _per + 1))
        else:
            _others += 1
            TILE_DONE.append(("tile", _others))

NORMS = ["mix_pre", "ffn_pre", "mix2_0", "mem0", "mem1", "xa0", "ffn2_0", "mix2_1", "xa1", "ffn2_1"]
SQ_END, _at = {}, 0
for _n in ("mix_pre", "post0", "ffn_pre", "post1", "mix2_0", "mem", "ln", "xa0", "ffn2_0", "mix2_1", "xa1", "ffn2_1",
           "final"):
    _at += 4 if _n == "ln" else KD
    SQ_END[_n] = _at


def xtile(base, kind, h, i):
    start = 0 if h == 0 else 6 * h - 4
    if kind == "s":
        return base + start + i
    return base + (6 * h + 4 if h < 3 else 20) + (2 if kind == "o" else 0) + i


def mtile(kind, h, b):
    if kind == "s":
        return TILE0["att"] + (0 if h == 0 else 9 * h - 5) + b
    start = 9 * h + (8 if h < MLA_HEADS - 1 else 4)
    return TILE0["att"] + start + (4 if kind == "o" else b)



def program(nc, x_t, mem_t, positions, weights, pool_w, gla_w2, vecs, consts, masks, out):
    ctx = ExitStack()
    with ctx:
        place = [1152]

        def at(name, shape, dt=F32, offset=None):
            size = int(np.prod(shape[1:])) * 4
            if offset is None:
                offset = place[0]
                place[0] += (size + 63) // 64 * 64
            return nc.alloc_sbuf_tensor_at(name, shape, dt, offset=offset)

        def sem(name):
            return ctx.enter_context(nc.semaphore(name))

        XT = at("XT", [P, KD, S])
        hn_at = place[0]
        hnH = at("hnH", [P, KD, S], F32R)
        hnL = at("hnL", [P, KD, S], F32R)
        act_at = place[0]
        actH = at("actH", [P, KD, S], F32R)
        actL = at("actL", [P, KD, S], F32R)
        mix_at = place[0]
        MIX = at("MIX", [P, KD, S])
        place[0] += 64
        raw = at("raw", [P, RING, UNIT])
        wH = at("wH", [P, RING, UNIT], F32R)
        wL = at("wL", [P, RING, UNIT], F32R)
        VT = at("VT", [P, NVEC])
        CT = at("CT", [P, NCONST])
        MASK = at("MASK", [P, len(HALVES), P], I32)
        zero = at("zero", [P, 16])
        rstd = at("rstd", [P, S])
        rcol = at("rcol", [P, NB])
        ssq = at("ssq", [P, S])
        sq = at("sq", [P, 2, S])
        lnb = at("lnb", [P, S])
        lncol = at("lncol", [P, NB])
        lnv = at("lnv", [P, S])
        tmpY = at("tmpY", [P, 1])
        scr = place[0]
        TOP = 229344
        KB2 = 4 * S
        gpad = at("gpad", [P, 2, S + 4], offset=scr)
        ups = at("ups", [P, 2, S], offset=scr + 4160)
        cva = at("cva", [P, 2, S], offset=scr + 8320)
        hval = at("hval", [P, 2, S], offset=scr + 12480)
        postb = at("postb", [P, 2, S], offset=scr + 16640)
        o = scr
        cpad = at("cpad", [P, 2, S + 4], offset=o)
        cvm = at("cvm", [P, 2, S], offset=o + 4160)
        Y = at("Y", [P, 4, S], offset=o)
        o += 8256
        qkA = at("qkA", [P, 4, S], offset=o); o += 4 * KB2
        qkB = at("qkB", [P, 2, 2, S], offset=o); o += 4 * KB2
        VA = at("VA", [P, NB, S], offset=o); o += 4 * KB2
        gateO = at("gateO", [P, 4, S], offset=o); o += 4 * KB2
        VB = at("VB", [P, NB, S], offset=o); o += 4 * KB2
        gate_in = at("gate_in", [P, NB, 16], offset=o); o += 256
        absf = at("absf", [P, NB, 8], offset=o); o += 128
        lnf = at("lnf", [P, NB, 8], offset=o); o += 128
        logf = at("logf", [P, NB, 8], offset=o); o += 128
        bN = at("bN", [P, NB, 8], offset=o); o += 128
        aN = at("aN", [P, NB, 8], offset=o); o += 128
        assert o <= TOP, (o, TOP)
        hr = at("hr", [P, 2, S], offset=scr + 8256)
        ht = at("ht", [P, 2, S], offset=scr + 8256 + 2 * KB2)
        gateR = at("gateR", [P, 4, S], offset=mix_at)
        cumF = at("cumF", [P, 4, S + 1], offset=mix_at + 4 * KB2)
        o = act_at
        rowA = at("rowA", [8, S], offset=o); o += KB2
        rowB = at("rowB", [8, S], offset=o); o += KB2
        rowM = at("rowM", [8, 2, S], offset=o); o += 2 * KB2
        rowG = at("rowG", [8, 2, S], offset=o); o += 2 * KB2
        zb = at("zb", [P, S], offset=o); o += KB2
        zc = at("zc", [P, S], offset=o); o += KB2
        tmpM = at("tmpM", [P, S], offset=o); o += KB2
        guard = at("guard", [P, 2, S], offset=o); o += 2 * KB2
        den = at("den", [P, S], offset=o); o += KB2
        yd = at("yd", [P, S], offset=o); o += KB2
        lrT = at("lrT", [32, S], offset=o); o += KB2
        W2 = at("W2", [32, 2, 256], offset=o); o += KB2
        ones512 = at("ones512", [P, S], offset=o); o += KB2
        assert o <= mix_at
        o = hn_at
        ST = at("ST", [P, NB, S], offset=o); o += 4 * KB2
        DT = at("DT", [P, NB, S], offset=o); o += 4 * KB2
        PM = at("PM", [P, 2, NB, S], offset=o); o += 8 * KB2
        assert o <= act_at
        o = hn_at
        arg = at("arg", [P, 2, 2, S], offset=o); o += 4 * KB2
        qkL = at("qkL", [P, 2, 2, S], offset=o); o += 4 * KB2
        Pd = at("Pd", [P, 2, NB, P], offset=o); o += 2 * KB2
        P1 = at("P1", [P, 2, NB, P], offset=o); o += 2 * KB2
        P2 = at("P2", [P, 2, NB, 2 * P], offset=o); o += 4 * KB2
        KT = [at("KT0", [P, KD, MEM], offset=mix_at), at("KT1", [P, KD, MEM], offset=scr + 22528)]
        VM = [at("VM0", [P, 2, D], offset=mix_at + 4 * KB2), at("VM1", [P, 2, D], offset=scr + 22528 + 4 * KB2)]
        up = scr + 22528 + 8 * KB2
        memT = at("memT", [P, KD, MEM], offset=up)
        up2 = up + 4 * KB2
        rmem = at("rmem", [P, MEM], offset=up2)
        cosT = at("cosT", [P, NB, 16], offset=up2 + 1088)
        sinT = at("sinT", [P, NB, 16], offset=up2 + 1344)
        posI = at("posI", [P, NB], I32, offset=up2 + 1600)
        posF = at("posF", [P, NB], offset=up2 + 1664)
        angA = at("angA", [P, NB, 16], offset=up2 + 1728)
        angB = at("angB", [P, NB, 16], offset=up2 + 1984)
        angC = at("angC", [P, NB, 16], offset=up2 + 2240)
        rcq = at("rcq", [P, 8], offset=up2 + 2496)
        kpn = at("kpn", [P, NB, 32], offset=up2 + 2560)
        kpr = at("kpr", [P, NB, 32], offset=up2 + 3072)
        assert up2 + 3584 + 2048 <= TOP, (up2, TOP)
        memH = [at(f"memH{i}", [P, KD, MEM], F32R, offset=act_at + 8 * i * KB2) for i in range(2)]
        memL = [at(f"memL{i}", [P, KD, MEM], F32R, offset=act_at + (8 * i + 4) * KB2) for i in range(2)]
        PADU = 16
        upad = at("upad", [P, 4, S + PADU], offset=scr)
        wina = at("wina", [P, S + PADU], offset=hn_at + 10 * KB2)
        winb = at("winb", [P, S + PADU], offset=hn_at + 12 * KB2)
        sigb = at("sigb", [P, 2, S], offset=scr + 17152)
        glp = at("glp", [P, 4, S + 32], offset=scr + 8448)
        cvb = at("cvb", [P, 4, S], offset=hn_at)
        pooled = at("pooled", [P, 4, S], offset=hn_at + 4 * KB2)
        pwt = at("pwt", [P, 4, P], offset=up2 + 3584)
        meanb = at("meanb", [P, S], offset=hn_at + 9 * KB2)
        ybuf = at("ybuf", [P, 2, S], offset=hn_at + 14 * KB2)
        qX = at("qX", [P, KD, S], offset=scr)
        EX = at("EX", [P, 2, 2, MEM], offset=scr + 8 * KB2)
        xst = at("xst", [P, 2, 8], offset=scr + 10 * KB2)
        PX = at("PX", [P, 2, 2, S], offset=hn_at)
        cH = at("cH", [P, 5, S], F32R, offset=scr)
        cL = at("cL", [P, 5, S], F32R, offset=scr + 5 * KB2)
        rq = at("rq", [P, S], offset=scr + 10 * KB2)
        QC = at("QC", [P, MLA_HEADS, S], offset=hn_at)
        KC = at("KC", [P, MLA_HEADS, S], offset=act_at)
        VL = at("VL", [P, NB, D], offset=mix_at)
        qpn = at("qpn", [P, 2, S], offset=up)
        qpr = at("qpr", [P, 2, S], offset=up + 2 * KB2)
        oHL = at("oHL", [P, MLA_HEADS, S], F32R, offset=act_at)
        EM = at("EM", [P, 4, S], offset=up)
        PX2 = at("PX2", [P, 2, NB, S], offset=scr)
        mst = at("mst", [P, 2, 16], offset=scr + 10 * KB2)

        def v(name, i=0):
            return VT[:, VEC[name] + i:VEC[name] + i + 1]

        def c(name, w=P):
            return CT[:, CONST[name]:CONST[name] + w]
        ident, ones, past, future = c("ident"), c("ones"), c("past"), c("future")
        upto, since, twice, neg_future = c("upto"), c("since"), c("twice"), c("neg_future")
        bank = [ctx.enter_context(nc.psum_tensor(f"bank{i}", [P, S], F32)) for i in range(8)]

        loaded = [sem(f"loaded{i}") for i in range(RING)]
        hi_split = sem("hi_split")
        split = sem("split")
        unit_done = sem("unit_done")
        tile_done = sem("tile_done")
        evacuated = [sem(f"evacuated{i}") for i in range(8)]
        tables_in = sem("tables_in")
        x_in = sem("x_in")
        mem_in = sem("mem_in")
        sq_ready, sq_used = sem("sq_ready"), sem("sq_used")
        hi_ready, hn_ready = sem("hi_ready"), sem("hn_ready")
        rstd_ready = sem("rstd_ready")
        v_step, a_step = sem("v_step"), sem("a_step")
        out_done = sem("out_done")
        named = {}

        def sig(name):
            if name not in named:
                named[name] = sem(name)
            return named[name]

        def tile_wait(eng, n):
            kind, count = TILE_DONE[n]
            eng.wait_ge(unit_done if kind == "unit" else tile_done, count)

        def gone_wait(eng, n):
            eng.wait_ge(evacuated[n % 8], n // 8 + 1)

        def free(ins, n):
            ins.then_inc(evacuated[n % 8], 1)

        def psum(n):
            return bank[n % 8]

        NORM = {n: i for i, n in enumerate(NORMS)}
        WIDTH = {n: w for n, _, w in UNITS}
        COUNT = {n: k for n, k, _ in UNITS}
        LAST = {n: UNIT0[n] + k for n, k, _ in UNITS}

        block = ctx.enter_context(nc.Block())

        runs, u = [], 0
        for n, k, w in UNITS:
            if runs and runs[-1][2] == w:
                runs[-1][1] += k
            else:
                runs.append([u, k, w])
            u += k

        @block.sync
        def _(sp):
            def load(u, slot, turn, w):
                sp.dma_start(raw[:, slot, 0:w], weights[u, :, 0:w]).then_inc(loaded[slot], 16)

            for u0, n, w in runs:
                i0 = 0
                while i0 < n and (u0 + i0 < RING or (n - i0) % RING):
                    if u0 + i0 >= RING:
                        sp.wait_ge(split, u0 + i0 - RING + 1)
                    load(u0 + i0, (u0 + i0) % RING, 0, w)
                    i0 += 1
                if i0 < n:
                    with sp.Fori(0, (n - i0) // RING) as i:
                        for j in range(RING):
                            u = u0 + i0 + j
                            sp.wait_ge(split, i * RING + (u - RING + 1))
                            load(i * RING + u, u % RING, 0, w)
            sp.wait_ge(out_done, 16 * KD)

        @block.gpsimd
        def _(pool):
            nc.gpsimd.memset(zero[:, :], 0.0).then_inc(sig("zero_set"), 1)
            pool.wait_ge(sig("zero_set"), 1)
            nothing = zero[:, 0:1]

            def split_unit(u, slot, turn, w):
                pool.wait_ge(loaded[slot], turn * 16 + 16)
                nc.gpsimd.tensor_tensor(wH[:, slot, 0:w], raw[:, slot, 0:w], nothing.broadcast_to([P, w]), ALU.add)\
                    .then_inc(hi_split, 1)
                pool.wait_ge(hi_split, u + 1)
                nc.gpsimd.tensor_tensor(wL[:, slot, 0:w], raw[:, slot, 0:w], wH[:, slot, 0:w].bitcast(F32),
                                        ALU.subtract).then_inc(split, 1)

            for u0, n, w in runs:
                i0 = 0
                while i0 < n and (u0 + i0 < RING or (n - i0) % RING):
                    u = u0 + i0
                    if u >= RING:
                        pool.wait_ge(unit_done, u - RING + 1)
                    split_unit(u, u % RING, u // RING, w)
                    i0 += 1
                if i0 < n:
                    with pool.Fori(0, (n - i0) // RING) as i:
                        for j in range(RING):
                            u = u0 + i0 + j
                            pool.wait_ge(unit_done, i * RING + (u - RING + 1))
                            split_unit(i * RING + u, u % RING, i + u // RING, w)

        @block.tensor
        def _(pe):
            mm = nc.tensor.matmul

            def claim(n):
                if n >= 8:
                    pe.wait_ge(evacuated[n % 8], n // 8)

            def three(out_, aH, aL, bH, bL, first, last):
                mm(out_, aH, bH, start=first, stop=False)
                mm(out_, aH, bL, start=False, stop=False)
                return mm(out_, aL, bH, start=False, stop=last)

            def wait_hn(norm, k):
                pe.wait_ge(hn_ready, KD * NORM[norm] + k + 1)

            def project(name, bH, bL, kd=KD, cols=S, ready=None, after={}):
                for i in range(COUNT[name]):
                    u, n = UNIT0[name] + i, TILE0[name] + i
                    pe.wait_ge(split, u + 1)
                    claim(n)
                    for k in range(kd):
                        if ready and i == 0:
                            ready(k)
                        cut = slice(k * P, k * P + P)
                        last = three(psum(n)[:, 0:cols], wH[:, u % RING, cut], wL[:, u % RING, cut],
                                     bH[:, k, :], bL[:, k, :], k == 0, k == kd - 1)
                    last.then_inc(unit_done, 1)
                    if i in after:
                        after[i]()

            def project_natural(name, aH, aL, kd, blocks, tile0, u0, units, ready=None):
                for i in range(units):
                    u = u0 + i
                    pe.wait_ge(split, u + 1)
                    ks = [k for k in (2 * i, 2 * i + 1) if k < kd]
                    for b in range(blocks):
                        n = tile0 + b
                        if i == 0:
                            claim(n)
                        tok = slice(b * P, b * P + P)
                        for k in ks:
                            cut = slice((k - 2 * i) * S, (k - 2 * i) * S + S)
                            last = three(psum(n)[:, :], aH[:, k, tok], aL[:, k, tok], wH[:, u % RING, cut],
                                         wL[:, u % RING, cut], k == 0, k == kd - 1)
                    last.then_inc(unit_done, 1)

            def row_sums(n, norm, cols=S):
                pe.wait_ge(sq_used, SQ_END[norm])
                claim(n)
                mm(psum(n)[:, 0:cols], ones, ssq[:, 0:cols], start=True, stop=True).then_inc(tile_done, 1)

            def col_sums(n, norm, blocks=NB):
                pe.wait_ge(sq_used, SQ_END[norm])
                claim(n)
                for b in range(blocks):
                    last = mm(psum(n)[:, b:b + 1], ssq[:, b * P:b * P + P], ones[:, 0:1], start=True, stop=True)
                last.then_inc(tile_done, 1)

            def feed_forward(f, norm):
                for t, chunks in enumerate(THIRDS):
                    if t == 0:
                        project(f"ff{f}_gu0", hnH, hnL, ready=lambda k: wait_hn(norm, k),
                                after={0: lambda: row_sums(TILE0[f"row_sum_f{f}"], norm)})
                    else:
                        project(f"ff{f}_gu{t}", hnH, hnL)
                    base = f * NF + sum(THIRDS[:t])
                    project(f"ff{f}_d{t}", actH, actL, kd=chunks,
                            ready=lambda k: pe.wait_ge(sig("hid_ready"), base + k + 1))

            pe.wait_ge(tables_in, 16 * 4)
            col_sums(TILE0["col_sum1"], "mix_pre")
            row_sums(TILE0["row_sum1"], "mix_pre")
            n, u = TILE0["gates"], UNIT0["lr_gates"]
            pe.wait_ge(split, u + 1)
            claim(n)
            for b in range(NB):
                for k in range(KD):
                    wait_hn("mix_pre", k)
                    tok = slice(b * P, b * P + P)
                    cut = slice(k * 48, k * 48 + 16)
                    three(psum(n)[:, b * 16:b * 16 + 16], hnH[:, k, tok], hnL[:, k, tok], wH[:, u % RING, cut],
                          wL[:, u % RING, cut], k == 0, k == KD - 1)
            claim(n + 1)
            for k in range(KD):
                cut = slice(k * 48 + 16, k * 48 + 48)
                last = three(psum(n + 1)[0:32, :], wH[:, u % RING, cut], wL[:, u % RING, cut], hnH[:, k, :],
                             hnL[:, k, :], k == 0, k == KD - 1)
            last.then_inc(unit_done, 1)
            project("a_qk", hnH, hnL)
            n = TILE0["cum"]
            pe.wait_ge(sig("logf_ready"), 1)
            claim(n)
            for b in range(NB):
                for d, (heads, others, tri) in enumerate(((slice(0, 4), range(0, b), upto),
                                                          (slice(4, 8), range(b + 1, NB), since))):
                    to = psum(n)[:, b * 8 + 4 * d:b * 8 + 4 * d + 4]
                    for i, q in enumerate(others):
                        mm(to, ones, logf[:, q, heads], start=(i == 0), stop=False)
                    last = mm(to, tri, logf[:, b, heads], start=(len(others) == 0), stop=True)
            last.then_inc(tile_done, 1)
            project("b_qk", hnH, hnL)
            gone_wait(pe, TILE0["lr"])
            for i in range(4):
                n = TILE0["log_a"] + i
                claim(n)
                mm(psum(n)[:, :], W2[:, i // 2, (i % 2) * P:(i % 2) * P + P], lrT[:, :], start=True, stop=True)\
                    .then_inc(tile_done, 1)
            gone_wait(pe, TILE0["cum"])
            for i, src in enumerate((aN, bN)):
                n = TILE0["gate_rows"] + i
                claim(n)
                for b in range(NB):
                    last = nc.tensor.transpose(psum(n)[0:8, b * P:b * P + P], src[:, b, :], ident)
                last.then_inc(tile_done, 1)
            project_natural("a_v", hnH, hnL, KD, NB, TILE0["a_v"], UNIT0["a_v"], 4)
            project_natural("b_v", hnH, hnL, KD, NB, TILE0["b_v"], UNIT0["b_v"], 4)
            project("a_o", hnH, hnL)
            project("b_r", hnH, hnL)

            def score_tiles(h):
                rows = slice(64 * (h % 2), 64 * (h % 2) + 64)
                for j in range(NB):
                    n = TILE0[f"s{h}"] + j
                    claim(n)
                    mm(psum(n)[:, :], qkA[rows, 2 + h // 2, j * P:j * P + P], qkA[rows, h // 2, :], start=True,
                       stop=True).then_inc(tile_done, 1)

            def spread_rows(i):
                h, d = i // 2, i % 2
                pick = ident[0:8, h + 4 * d:h + 4 * d + 1].broadcast_to([8, P])
                for name, src in (("max", rowM), ("guard", rowG)):
                    n = TILE0[f"{name}{i}"]
                    claim(n)
                    mm(psum(n)[:, :], pick, src[:, d, :], start=True, stop=True).then_inc(tile_done, 1)

            def weigh(i):
                h, d = i // 2, i % 2
                pe.wait_ge(sig("weights_m"), i + 1)
                for name in ("num", "den"):
                    n = TILE0[f"{name}{i}"]
                    claim(n)
                    for q, j in enumerate(range(NB) if d == 0 else range(NB - 1, -1, -1)):
                        cols = slice(j * P, S) if d == 0 else slice(0, j * P + P)
                        lhs = VA[:, j, h * P:h * P + P] if name == "num" else ones
                        last = mm(psum(n)[:, cols], lhs, PM[:, i % 2, j, cols], start=(q == 0), stop=(q == NB - 1))
                    last.then_inc(tile_done, 1)

            pe.wait_ge(sig("qk_ready"), 4)
            pe.wait_ge(sig("rows_ready"), 1)
            for i in range(9):
                if i < 8:
                    if i % 2 == 0:
                        score_tiles(i // 2)
                    spread_rows(i)
                if i > 0:
                    weigh(i - 1)

            def head_sums(name, stage):
                for h in range(4):
                    n = TILE0[name] + h
                    claim(n)
                    pe.wait_ge(sig("head_sq"), 4 * stage + h + 1)
                    mm(psum(n)[:, :], ones, sq[:, h % 2, :], start=True, stop=True).then_inc(tile_done, 1)
            head_sums("norm_a", 0)

            for cc in range(2):
                for lev in range(10):
                    if lev > 0:
                        pe.wait_ge(sig("level_qk"), cc * 9 + lev)
                    for hh in range(2):
                        rows = slice(64 * hh, 64 * hh + 64)
                        q_, k_ = (qkB[rows, 0, cc], qkB[rows, 1, cc]) if lev == 0 else \
                            (qkL[rows, lev % 2, 0], qkL[rows, lev % 2, 1])
                        for half in range(2 if lev == 9 else 1):
                            n = TILE0[f"lev{cc}_{lev}"] + (2 * hh + half if lev == 9 else hh)
                            claim(n)
                            if lev == 9:
                                for j in (2 * half, 2 * half + 1):
                                    last = mm(psum(n)[:, (j % 2) * 256:(j % 2) * 256 + 256], k_[:, j * P:j * P + P],
                                              q_[:, 256 * (1 - half):256 * (1 - half) + 256], start=True, stop=True)
                            else:
                                for j in range(NB):
                                    i = j ^ 1 if lev == 8 else j
                                    last = mm(psum(n)[:, j * P:j * P + P], k_[:, j * P:j * P + P],
                                              q_[:, i * P:i * P + P], start=True, stop=True)
                            last.then_inc(tile_done, 1)
                for hh in range(2):
                    n = TILE0[f"o{cc}"] + hh
                    claim(n)
                    gone_wait(pe, TILE0[f"lev{cc}_7"] + hh)
                    gone_wait(pe, TILE0[f"lev{cc}_8"] + hh)
                    gone_wait(pe, TILE0[f"lev{cc}_9"] + 2 * hh)
                    gone_wait(pe, TILE0[f"lev{cc}_9"] + 2 * hh + 1)
                    val = [VB[:, j, (2 * cc + hh) * P:(2 * cc + hh) * P + P] for j in range(NB)]
                    for j in range(NB):
                        mm(psum(n)[:, j * P:j * P + P], val[j], Pd[:, hh, j, :], start=(j == 0), stop=False)
                    for j in range(NB):
                        mm(psum(n)[:, (j ^ 1) * P:(j ^ 1) * P + P], val[j], P1[:, hh, j, :], start=False, stop=False)
                    for j in range(NB):
                        to = slice(256, 512) if j < 2 else slice(0, 256)
                        last = mm(psum(n)[:, to], val[j], P2[:, hh, j, :], start=False, stop=(j == NB - 1))
                    last.then_inc(tile_done, 1)
            head_sums("norm_b", 1)
            project("w_out", actH, actL, ready=lambda k: pe.wait_ge(sig("y_ready"), k + 1))

            row_sums(TILE0["post0"], "post0")
            feed_forward(0, "ffn_pre")
            row_sums(TILE0["post1"], "post1")

            def cross_attention(l):
                norm = f"xa{l}"
                project(f"xq{l}", hnH, hnL, ready=lambda k: wait_hn(norm, k),
                        after={0: lambda: row_sums(TILE0[f"row_sum_x{l}"], norm)})
                base = TILE0[f"xatt{l}"]

                def scores(h):
                    for pair in range(2):
                        n = xtile(base, "s", h, pair)
                        claim(n)
                        gone_wait(pe, TILE0[f"xq{l}"] + 2 * h + 1)
                        for q in range(2):
                            tok = slice((2 * pair + q) * P, (2 * pair + q) * P + P)
                            for k in range(2):
                                last = mm(psum(n)[:, q * MEM:q * MEM + MEM], qX[:, 2 * h + k, tok],
                                          KT[l][:, 2 * h + k, :], start=(k == 0), stop=(k == 1))
                        last.then_inc(tile_done, 1)

                def turn(h):
                    for pair in range(2):
                        n = xtile(base, "t", h, pair)
                        claim(n)
                        pe.wait_ge(sig("x_probs"), 8 * l + 2 * h + pair + 1)
                        for m in range(2):
                            for q in range(2):
                                last = nc.tensor.transpose(psum(n)[:, m * MEM + q * P:m * MEM + q * P + P],
                                                           EX[:, pair, q, m * P:m * P + P], ident)
                        last.then_inc(tile_done, 1)

                def values(h):
                    gone_wait(pe, xtile(base, "t", h, 1))
                    for f in range(2):
                        n = xtile(base, "o", h, f)
                        claim(n)
                        for m in range(2):
                            last = mm(psum(n)[:, :], VM[l][:, m, h * 256 + f * P:h * 256 + f * P + P],
                                      PX[:, h % 2, m, :], start=(m == 0), stop=(m == 1))
                        last.then_inc(tile_done, 1)
                scores(0)
                for h in range(4):
                    if h < 3:
                        scores(h + 1)
                    turn(h)
                    values(h)
                project(f"xo{l}", actH, actL, ready=lambda k: gone_wait(pe, xtile(base, "o", k // 2, k % 2)))

            project("pc_in", hnH, hnL, ready=lambda k: wait_hn("mix2_0", k),
                    after={0: lambda: row_sums(TILE0["row_sum3"], "mix2_0"),
                           6: lambda: row_sums(TILE0["mem_sums"], "mem", MEM)})
            for l in range(2):
                project(f"mem_k{l}", memH[l], memL[l], cols=MEM, ready=lambda k: wait_hn(f"mem{l}", k))
                for g in range(2):
                    project_natural(f"mem_v{l}", memH[l], memL[l], KD, 2, TILE0[f"mem_v{l}"] + 2 * g,
                                    UNIT0[f"mem_v{l}"] + 4 * g, 4)
            for g in range(4):
                n = TILE0["pool"] + g
                pe.wait_ge(sig("pooled"), g + 1)
                claim(n)
                mm(psum(n)[:, :], pwt[:, g, :], pooled[:, g, :], start=True, stop=True).then_inc(tile_done, 1)
            n = TILE0["ln_mean"]
            pe.wait_ge(sig("ln_sum"), 1)
            claim(n)
            mm(psum(n)[:, :], ones, ssq[:, :], start=True, stop=True).then_inc(tile_done, 1)
            row_sums(TILE0["ln_var"], "ln")
            project("pc_out", actH, actL, ready=lambda k: pe.wait_ge(sig("pc_ready"), k + 1))
            cross_attention(0)
            feed_forward(1, "ffn2_0")

            n, u = TILE0["k_pe"], UNIT0["k_pe"]
            pe.wait_ge(split, u + 1)
            claim(n)
            for b in range(NB):
                for k in range(KD):
                    wait_hn("mix2_1", k)
                    tok = slice(b * P, b * P + P)
                    cut = slice(k * 32, k * 32 + 32)
                    last = three(psum(n)[:, b * 32:b * 32 + 32], hnH[:, k, tok], hnL[:, k, tok], wH[:, u % RING, cut],
                                 wL[:, u % RING, cut], k == 0, k == KD - 1)
            last.then_inc(unit_done, 1)
            row_sums(TILE0["row_sum6"], "mix2_1")
            col_sums(TILE0["col_sum6"], "mix2_1")
            project("w_dq", hnH, hnL)
            for i, name in enumerate(("q_sum", "kv_sum")):
                n = TILE0[name]
                pe.wait_ge(sig("lora_added"), (3, 5)[i])
                claim(n)
                mm(psum(n)[:, :], ones, sq[:, i, :], start=True, stop=True).then_inc(tile_done, 1)
                claim(n + 1)
                for b in range(NB):
                    last = mm(psum(n + 1)[:, b:b + 1], sq[:, i, b * P:b * P + P], ones[:, 0:1], start=True, stop=True)
                last.then_inc(tile_done, 1)
            pe.wait_ge(sig("c_ready"), 5)
            for name, per, kd, c0 in (("q_nope", 2, 3, 0), ("q_pe", 0, 3, 0), ("k_nope", 4, 2, 3), ("mla_v", 0, 2, 3)):
                if name == "q_pe":
                    project_natural(name, cH, cL, kd, NB, TILE0[name], UNIT0[name], 2)
                    continue
                if name == "mla_v":
                    for g in range(2):
                        project_natural(name, cH[:, c0:c0 + 2, :], cL[:, c0:c0 + 2, :], kd, NB, TILE0[name] + 4 * g,
                                        UNIT0[name] + g, 1)
                    continue
                for i in range(COUNT[name]):
                    u = UNIT0[name] + i
                    pe.wait_ge(split, u + 1)
                    for q in range(per):
                        n = TILE0[name] + per * i + q
                        claim(n)
                        for k in range(kd):
                            cut = slice((q * kd + k) * P, (q * kd + k) * P + P)
                            last = three(psum(n)[:, :], wH[:, u % RING, cut], wL[:, u % RING, cut],
                                         cH[:, c0 + k, :], cL[:, c0 + k, :], k == 0, k == kd - 1)
                    last.then_inc(unit_done, 1)
            for b in range(NB):
                n = TILE0["pe_turn"] + b
                pe.wait_ge(sig("q_rotated"), b + 1)
                claim(n)
                for g in range(4):
                    last = nc.tensor.transpose(psum(n)[:, g * P:g * P + P], qpr[:, b % 2, g * P:g * P + P], ident)
                last.then_inc(tile_done, 1)
            n = TILE0["pe_turn"] + 4
            pe.wait_ge(sig("k_rotated"), 1)
            claim(n)
            for b in range(NB):
                last = nc.tensor.transpose(psum(n)[0:32, b * P:b * P + P], kpr[:, b, :], ident)
            last.then_inc(tile_done, 1)
            pe.wait_ge(sig("k_rows"), 1)
            gone_wait(pe, TILE0["pe_turn"] + 4)
            gone_wait(pe, TILE0["pe_turn"] + 3)

            def att_scores(h):
                for b in range(NB):
                    n = mtile("s", h, b)
                    claim(n)
                    w = (b + 1) * P
                    mm(psum(n)[:, 0:w], QC[0:96, h, b * P:b * P + P], KC[0:96, h, 0:w], start=True, stop=False)
                    mm(psum(n)[:, b * P:w], ident, neg_future, start=False, stop=True).then_inc(tile_done, 1)

            def att_turn(h):
                for b in range(NB):
                    n = mtile("t", h, b)
                    claim(n)
                    pe.wait_ge(sig("m_probs"), 4 * h + b + 1)
                    for j in range(b + 1):
                        last = nc.tensor.transpose(psum(n)[:, j * P:j * P + P], EM[:, b, j * P:j * P + P], ident)
                    last.then_inc(tile_done, 1)

            def att_values(h):
                n = mtile("o", h, 0)
                claim(n)
                for b in (0, 1, 2, 3):
                    gone_wait(pe, mtile("t", h, b))
                rows = slice(64 * (h % 2), 64 * (h % 2) + 64)
                for j in range(NB):
                    last = mm(psum(n)[rows, j * P:], VL[:, j, h * 64:h * 64 + 64], PX2[:, h % 2, j, j * P:],
                              start=(j == 0), stop=(j == NB - 1))
                last.then_inc(tile_done, 1)

            for i in range(MLA_HEADS):
                att_scores(i)
                if i > 0:
                    att_turn(i - 1)
                    att_values(i - 1)
            att_turn(MLA_HEADS - 1)
            att_values(MLA_HEADS - 1)
            oH_, oL_ = (oHL[:, :, :].rearrange("p (a two) s -> p a two s", two=2)[:, :, i, :] for i in range(2))
            project("mla_o", oH_, oL_, ready=lambda k: gone_wait(pe, mtile("o", 2 * k + 1, 0)))
            cross_attention(1)
            feed_forward(2, "ffn2_1")
            row_sums(TILE0["row_sum_end"], "final")

        @block.scalar
        def _(act):
            step, nsq, nhi = [0], [0], [0]
            run = nc.scalar.activation

            def link(ins):
                step[0] += 1
                ins.then_inc(a_step, 1)
                act.wait_ge(a_step, step[0])

            def square(src, cols=S):
                if nsq[0] >= 2:
                    act.wait_ge(sq_used, nsq[0] - 1)
                run(sq[:, nsq[0] % 2, 0:cols], src, ACT.Square).then_inc(sq_ready, 1)
                nsq[0] += 1

            def high(dst, src, gain):
                run(dst, src, ACT.Copy, scale=gain).then_inc(hi_ready, 1)
                nhi[0] += 1

            def norm_chunk(gain, c_):
                square(XT[:, c_, :])
                high(hnH[:, c_, :], XT[:, c_, :], v(gain, c_))

            def inverse_root(n, dst, tmp, width, cols=S, signal=None, rows=P):
                tile_wait(act, n)
                free(run(tmp, psum(n)[0:rows, 0:cols], ACT.Ln, bias=v("eps"), scale=1.0 / width), n)
                gone_wait(act, n)
                run(dst, tmp, ACT.Exp, scale=-0.5).then_inc(signal, 1)

            def row_root(n, width=D):
                inverse_root(n, rstd[:, :], lnb[:, :], width, signal=rstd_ready)

            def feed_forward(f):
                base = TILE0[f"row_sum_f{f}"]
                row_root(base)
                for t, chunks in enumerate(THIRDS):
                    for j in range(chunks):
                        q = sum(THIRDS[:t]) + j
                        i, s_ = f * NF + q, q % 2
                        g = 4 + i
                        gone_wait(act, TILE0[f"ff{f}_gu{t}"] + 2 * j)
                        mid = 2 if f == 0 else 1
                        run(cva[:, s_, :], gpad[:, s_, mid:mid + S], ACT.Identity, bias=v(f"fconv_b{f}", q),
                            scale=v(f"fconv_w{f}", 3 * q + 1)).then_inc(sig("conv_mid"), 1)
                        act.wait_ge(sig("conv_done"), g + 1)
                        run(cva[:, s_, :], cva[:, s_, :], ACT.Gelu_apprx_tanh if f == 0 else ACT.Silu)\
                            .then_inc(sig("gate_done"), 1)
                        if j == 0 and t > 0:
                            act.wait_ge(unit_done, LAST[f"ff{f}_d{t - 1}"])
                        act.wait_ge(sig("hval_ready"), i + 1)
                        run(actH[:, j, :], hval[:, s_, :], ACT.Copy).then_inc(sig("hid_hi"), 1)
                    if t == 0 and f == 0:
                        for m in range(KD):
                            n = TILE0["ff0_d0"] + m
                            tile_wait(act, n)
                            free(run(MIX[:, m, :], psum(n)[:, :], ACT.Copy), n)

            act.dma_start(VT[:, :], vecs).then_inc(tables_in, 16)
            act.dma_start(CT[:, :], consts).then_inc(tables_in, 16)
            for c_ in range(KD):
                act.dma_start(XT[:, c_, :], x_t[c_ * P:c_ * P + P, :]).then_inc(x_in, 16)
            act.dma_start(MASK[:, :, :], masks).then_inc(tables_in, 16)
            act.dma_start(W2[:, :, :], gla_w2).then_inc(tables_in, 16)
            act.wait_ge(tables_in, 16 * 4)
            act.wait_ge(x_in, 16 * KD)

            for c_ in range(KD):
                norm_chunk("mix_pre", c_)
            inverse_root(TILE0["col_sum1"], rcol[:, :], lncol[:, :], D, NB, sig("rcol_ready"))
            row_root(TILE0["row_sum1"])
            act.wait_ge(sig("gates_in"), 1)
            link(run(absf[:, :, :], gate_in[:, :, 8:16], ACT.Abs))
            link(run(lnf[:, :, :], absf[:, :, :], ACT.Exp, scale=-1.0))
            run(lnf[:, :, :], lnf[:, :, :], ACT.Ln, bias=v("one")).then_inc(sig("softplus_f"), 1)
            for i in range(4):
                gone_wait(act, TILE0["a_qk"] + i)
                run(cvm[:, i % 2, :], cpad[:, i % 2, 2:2 + S], ACT.Identity, bias=v("mconv_b", i),
                    scale=v("mconv_w", 3 * i + 1)).then_inc(sig("conv_mid"), 1)
                act.wait_ge(sig("conv_done"), i + 1)
                run(qkA[:, i, :], cvm[:, i % 2, :], ACT.Silu).then_inc(sig("qk_ready"), 1)
            for i in range(4):
                n = TILE0["log_a"] + i
                tile_wait(act, n)
                if i > 0:
                    act.wait_ge(sig("log_a_used"), i)
                free(run(zb[:, :], psum(n)[:, :], ACT.Identity, bias=v("gla_b", i)), n)
                gone_wait(act, n)
                link(run(zc[:, :], zb[:, :], ACT.Abs))
                link(run(zc[:, :], zc[:, :], ACT.Exp, scale=-1.0))
                run(zc[:, :], zc[:, :], ACT.Ln, bias=v("one")).then_inc(sig("softplus_a"), 1)
            for i, dst in enumerate((rowA, rowB)):
                n = TILE0["gate_rows"] + i
                tile_wait(act, n)
                free(run(dst[:, :], psum(n)[0:8, :], ACT.Copy), n)
            for name, dst in (("a_v", VA), ("b_v", VB)):
                for b in range(NB):
                    n = TILE0[name] + b
                    tile_wait(act, n)
                    free(run(dst[:, b, :], psum(n)[:, :], ACT.Copy, scale=rcol[:, b:b + 1]), n)
            for i in range(4):
                gone_wait(act, TILE0["a_o"] + i)
                run(gateO[:, i, :], gateO[:, i, :], ACT.Sigmoid).then_inc(sig("gate_act"), 1)
            for i in range(4):
                gone_wait(act, TILE0["b_r"] + i)
                run(gateR[:, i, :], gateR[:, i, :], ACT.Silu).then_inc(sig("gate_act"), 1)

            for i in range(8):
                h, d = i // 2, i % 2
                if d == 0:
                    if i > 0:
                        act.wait_ge(sig("weights_m"), i)
                    for j in range(NB):
                        n = TILE0[f"s{h}"] + j
                        tile_wait(act, n)
                        free(run(ST[:, j, :], psum(n)[:, :], ACT.Copy, scale=0.125), n)
                n = TILE0[f"max{i}"]
                if i > 0:
                    act.wait_ge(sig("weights_m"), i)
                act.wait_ge(sig("masked"), i + 1)
                for j in (range(NB - 1, -1, -1) if d == 0 else range(NB)):
                    diag = slice(j * P, j * P + P)
                    rest = slice(j * P + P, S) if d == 0 else slice(0, j * P)
                    own = aN[:, j, h + 4 * d:h + 4 * d + 1]
                    run(DT[:, j, diag], tmpM[:, diag], ACT.Exp, bias=own, scale=-1.0)
                    if rest.start < rest.stop:
                        last = run(DT[:, j, rest], psum(n)[:, rest], ACT.Exp, bias=own, scale=-1.0)
                free(last, n)
                n = TILE0[f"guard{i}"]
                tile_wait(act, n)
                if i >= 2:
                    gone_wait(act, TILE0[f"den{i - 2}"])
                free(run(guard[:, i % 2, :], psum(n)[:, :], ACT.Exp, scale=-1.0), n)

            def head_norms(name, stage, chunk0):
                def finish(h):
                    act.wait_ge(sig("head_out"), 4 * stage + h + 1)
                    run(actH[:, chunk0 + h, :], ht[:, h % 2, :], ACT.Copy).then_inc(sig("y_hi"), 1)
                for h in range(4):
                    act.wait_ge(sig("head_ready"), 4 * stage + h + 1)
                    if h >= 2:
                        tile_wait(act, TILE0[name] + h - 2)
                    run(sq[:, h % 2, :], Y[:, h, :], ACT.Square).then_inc(sig("head_sq"), 1)
                    if h >= 2:
                        act.wait_ge(sig("head_out"), 4 * stage + h - 1)
                    inverse_root(TILE0[name] + h, hr[:, h % 2, :], lnb[:, :], P, signal=sig("head_root"))
                    if h >= 1:
                        finish(h - 1)
                finish(3)
            head_norms("norm_a", 0, 0)

            for cc in range(2):
                for lev in range(1, 10):
                    i = cc * 9 + lev
                    act.wait_ge(sig("level_arg"), i)
                    run(arg[:, lev % 2, :, :], arg[:, lev % 2, :, :], ACT.Exp, scale=1.0 / 16)\
                        .then_inc(sig("level_exp"), 1)
                if cc > 0:
                    tile_wait(act, TILE0[f"o{cc - 1}"] + 1)
                for hh in range(2):
                    n = TILE0[f"lev{cc}_8"] + hh
                    tile_wait(act, n)
                    free(run(P1[:, hh, :, :], psum(n)[:, :], ACT.Copy), n)
                for q in range(4):
                    n = TILE0[f"lev{cc}_9"] + q
                    tile_wait(act, n)
                    free(run(P2[:, q // 2, 2 * (q % 2):2 * (q % 2) + 2, :], psum(n)[:, :], ACT.Copy), n)
            head_norms("norm_b", 1, 4)

            def post_chunk(c_):
                square(MIX[:, c_, :])
            for m in range(KD):
                n = TILE0["w_out"] + m
                tile_wait(act, n)
                free(run(MIX[:, m, :], psum(n)[:, :], ACT.Copy), n)
                gone_wait(act, n)
                post_chunk(m)
            row_root(TILE0["post0"])
            for c_ in range(KD):
                act.wait_ge(sig("x_new"), c_ + 1)
                norm_chunk("ffn_pre", c_)
            act.dma_start(memT[:, :, :], mem_t.rearrange("(k p) m -> p k m", p=P)).then_inc(mem_in, 16)
            act.dma_start(posI[:, :], positions).then_inc(mem_in, 16)
            act.dma_start(pwt[:, :, :], pool_w.rearrange("g c d -> c g d")).then_inc(mem_in, 16)
            feed_forward(0)
            for m in range(KD):
                gone_wait(act, TILE0["ff0_d2"] + m)
                post_chunk(m)
            row_root(TILE0["post1"])
            for c_ in range(KD):
                act.wait_ge(sig("x_new"), KD + c_ + 1)
                norm_chunk("mix2_0", c_)

            act.wait_ge(mem_in, 48)
            row_root(TILE0["row_sum3"])
            for c_ in range(KD):
                square(memT[:, c_, :], MEM)
            for i in range(4):
                gone_wait(act, TILE0["pc_in"] + 8 + i)
                run(sigb[:, i % 2, :], sigb[:, i % 2, :], ACT.Sigmoid).then_inc(sig("glu_gate"), 1)
                if i == 0:
                    inverse_root(TILE0["mem_sums"], rmem[:, :], lnb[:, 0:MEM], D, MEM, sig("mem_root"))
            for l in range(2):
                for c_ in range(KD):
                    act.wait_ge(sig("mem_normed"), c_ + 1)
                    high(memH[l][:, c_, :], memT[:, c_, :], v(f"mem{l}", c_))
            for l in range(2):
                for i in range(KD):
                    n = TILE0[f"mem_k{l}"] + i
                    tile_wait(act, n)
                    free(run(KT[l][:, i, :], psum(n)[:, 0:MEM], ACT.Copy), n)
                for i in range(4):
                    n = TILE0[f"mem_v{l}"] + i
                    tile_wait(act, n)
                    free(run(VM[l][:, i % 2, (i // 2) * S:(i // 2) * S + S], psum(n)[:, :], ACT.Copy), n)
            act.wait_ge(unit_done, LAST["mem_v1"])

            def pc_high(i, chunk):
                run(actH[:, chunk, :], ybuf[:, i % 2, :], ACT.Copy).then_inc(sig("pc_hi"), 1)
            for g in range(4):
                n = TILE0["pool"] + g
                tile_wait(act, n)
                if g >= 2:
                    act.wait_ge(sig("pc_ready"), g - 1)
                free(run(ybuf[:, g % 2, :], psum(n)[:, :], ACT.Copy, scale=v("pool_scale", g)), n)
                gone_wait(act, n)
                pc_high(g, g)
            for c_ in range(4):
                act.wait_ge(sig("centred"), c_ + 1)
                square(cvb[:, c_, :])
            row_root(TILE0["ln_var"], S)
            for c_ in range(4):
                act.wait_ge(sig("scaled"), c_ + 1)
                act.wait_ge(sig("pc_ready"), 4 + c_ - 1)
                link(run(ybuf[:, c_ % 2, :], cvb[:, c_, :], ACT.Silu, bias=v("ln_b", c_), scale=v("ln_g", c_)))
                pc_high(4 + c_, 4 + c_)
            for c_ in range(KD):
                gone_wait(act, TILE0["pc_out"] + c_)
                norm_chunk("xa0", c_)

            def cross_attention(l, next_norm):
                base = TILE0[f"xatt{l}"]
                row_root(TILE0[f"row_sum_x{l}"])

                def outputs(h):
                    for pair in range(2):
                        n = xtile(base, "t", h, pair)
                        tile_wait(act, n)
                        if h >= 2:
                            tile_wait(act, xtile(base, "o", h - 2, 1))
                        free(run(PX[:, h % 2, :, pair * MEM:pair * MEM + MEM],
                                 psum(n)[:, :].rearrange("p (m q) -> p m q", m=2), ACT.Copy), n)
                    for f in range(2):
                        tile_wait(act, xtile(base, "o", h, f))
                        run(actH[:, 2 * h + f, :], psum(xtile(base, "o", h, f))[:, :], ACT.Copy)\
                            .then_inc(sig("x_hi"), 1)
                for h in range(4):
                    for pair in range(2):
                        n = xtile(base, "s", h, pair)
                        act.wait_ge(sig("x_max"), 8 * l + 2 * h + pair + 1)
                        if h >= 1:
                            tile_wait(act, xtile(base, "t", h - 1, pair))
                        for q in range(2):
                            last = run(EX[:, pair, q, :], psum(n)[:, q * MEM:q * MEM + MEM], ACT.Exp,
                                       bias=xst[:, pair, 2 + q:3 + q], scale=1.0 / 16,
                                       accum_out=xst[:, pair, 4 + q:5 + q])
                        free(last, n)
                    if h > 0:
                        outputs(h - 1)
                outputs(3)
                for c_ in range(KD):
                    gone_wait(act, TILE0[f"xo{l}"] + c_)
                    norm_chunk(next_norm, c_)

            cross_attention(0, "ffn2_0")
            feed_forward(1)
            for c_ in range(KD):
                gone_wait(act, TILE0["ff1_d2"] + c_)
                norm_chunk("mix2_1", c_)

            act.wait_ge(sig("angle"), 1)
            run(sinT[:, :, :], angB[:, :, :], ACT.Sin).then_inc(sig("turned"), 1)
            act.wait_ge(sig("angle"), 2)
            run(cosT[:, :, :], angC[:, :, :], ACT.Sin).then_inc(sig("turned"), 1)
            row_root(TILE0["row_sum6"])
            inverse_root(TILE0["col_sum6"], rcol[:, :], lncol[:, :], D, NB, sig("rcol_ready"))
            act.wait_ge(sig("rcol_ready"), 2)
            n = TILE0["k_pe"]
            tile_wait(act, n)
            for b in range(NB):
                last = run(kpn[:, b, :], psum(n)[:, b * 32:b * 32 + 32], ACT.Copy, scale=rcol[:, b:b + 1])
            free(last, n)
            for i in range(5):
                gone_wait(act, TILE0["w_dq"] + i)
                if i >= 2:
                    act.wait_ge(sig("lora_added"), i - 1)
                run(qpr[:, i % 2, :], qpn[:, i % 2, :], ACT.Square).then_inc(sig("lora_sq"), 1)
                run(cH[:, i, :], qpn[:, i % 2, :], ACT.Copy, scale=v("q_norm", i) if i < 3 else v("kv_norm", i - 3))\
                    .then_inc(sig("c_hi"), 1)
            inverse_root(TILE0["q_sum"], rq[:, :], lnb[:, :], 384, signal=sig("lora_root"))
            inverse_root(TILE0["q_sum"] + 1, rcq[:, 0:4], lncol[:, :], 384, NB, sig("lora_root"))
            inverse_root(TILE0["kv_sum"], rstd[:, :], lnb[:, :], 256, signal=rstd_ready)
            inverse_root(TILE0["kv_sum"] + 1, rcq[:, 4:8], lncol[:, :], 256, NB, sig("lora_root"))
            act.wait_ge(sig("lora_root"), 3)
            for b in range(NB):
                n = TILE0["q_pe"] + b
                tile_wait(act, n)
                if b >= 2:
                    act.wait_ge(sig("q_rotated"), b - 1)
                else:
                    act.wait_ge(sig("c_ready"), 5)
                free(run(qpn[:, b % 2, :], psum(n)[:, :], ACT.Copy, scale=rcq[:, b:b + 1]), n)
            for i in range(8):
                n = TILE0["mla_v"] + i
                tile_wait(act, n)
                b = i % 4
                free(run(VL[:, b, (i // 4) * S:(i // 4) * S + S], psum(n)[:, :], ACT.Copy, scale=rcq[:, 4 + b:5 + b]), n)
            for b in range(NB):
                n = TILE0["pe_turn"] + b
                tile_wait(act, n)
                for j in range(4):
                    last = run(QC[64:96, j:MLA_HEADS:4, b * P:b * P + P],
                               psum(n)[32 * j:32 * j + 32, :].rearrange("p (g t) -> p g t", g=4), ACT.Copy)
                free(last, n)
            n = TILE0["pe_turn"] + 4
            tile_wait(act, n)
            run(KC[64:96, 8:16, :], psum(n)[0:32, :].unsqueeze(1).broadcast_to([32, 8, S]), ACT.Copy)\
                .then_inc(sig("k_rows"), 1)

            scale = (64 + 32) ** -0.5

            def att_out(h):
                for b in (0, 2):
                    n = mtile("t", h, b)
                    tile_wait(act, n)
                    if h >= 2:
                        tile_wait(act, mtile("o", h - 2, 0))
                    free(run(PX2[:, h % 2, 0:b + 1, b * P:b * P + P],
                             psum(n)[:, 0:(b + 1) * P].rearrange("p (j q) -> p j q", q=P), ACT.Copy), n)
                n = mtile("o", h, 0)
                tile_wait(act, n)
                rows = slice(64 * (h % 2), 64 * (h % 2) + 64)
                run(oHL[rows, h // 2 * 2, :], psum(n)[rows, :], ACT.Copy).then_inc(sig("m_hi"), 1)

            for i in range(MLA_HEADS):
                act.wait_ge(sig("m_max"), i + 1)
                for b in range(NB):
                    n = mtile("s", i, b)
                    if i > 0:
                        tile_wait(act, mtile("t", i - 1, b))
                    w = (b + 1) * P
                    free(run(EM[:, b, 0:w], psum(n)[:, 0:w], ACT.Exp, bias=mst[:, i % 2, 4 + b:5 + b], scale=scale,
                             accum_out=mst[:, i % 2, 8 + b:9 + b]), n)
                if i > 0:
                    att_out(i - 1)
            att_out(MLA_HEADS - 1)
            for c_ in range(KD):
                gone_wait(act, TILE0["mla_o"] + c_)
                norm_chunk("xa1", c_)
            cross_attention(1, "ffn2_1")
            feed_forward(2)
            for c_ in range(KD):
                gone_wait(act, TILE0["ff2_d2"] + c_)
                square(XT[:, c_, :])
            row_root(TILE0["row_sum_end"])
            for c_ in range(KD):
                act.wait_ge(sig("final"), c_ + 1)
                act.dma_start(out[c_ * P:c_ * P + P, :], MIX[:, c_, :]).then_inc(out_done, 16)

        @block.vector
        def _(dve):
            step, nsq, nhn, nroot, nconv = [0], [0], [0], [0], [0]
            tt, ts, stt = nc.vector.tensor_tensor, nc.vector.tensor_scalar, nc.vector.scalar_tensor_tensor

            def link(ins):
                step[0] += 1
                ins.then_inc(v_step, 1)
                dve.wait_ge(v_step, step[0])

            def add_squares(first, cols=S):
                dve.wait_ge(sq_ready, nsq[0] + 1)
                s_ = sq[:, nsq[0] % 2, 0:cols]
                if first:
                    ins = nc.vector.tensor_copy(ssq[:, 0:cols], s_)
                else:
                    ins = tt(ssq[:, 0:cols], ssq[:, 0:cols], s_, ALU.add)
                ins.then_inc(sq_used, 1)
                nsq[0] += 1
                dve.wait_ge(sq_used, nsq[0])

            def low(dst, src, gain, hi):
                dve.wait_ge(hi_ready, nhn[0] + 1)
                stt(dst, src, gain, hi.bitcast(F32), ALU.mult, ALU.subtract).then_inc(hn_ready, 1)
                nhn[0] += 1

            def norm_chunk(gain, c_):
                add_squares(c_ == 0)
                if gain != "final":
                    low(hnL[:, c_, :], XT[:, c_, :], v(gain, c_), hnH[:, c_, :])

            def root_wait():
                nroot[0] += 1
                dve.wait_ge(rstd_ready, nroot[0])

            def scaled(dst, n, rows=slice(0, P)):
                tile_wait(dve, n)
                free(tt(dst, psum(n)[rows, :], rstd[rows, :], ALU.mult), n)

            def convolve(pad, acc, left, right, w, q):
                nconv[0] += 1
                dve.wait_ge(sig("conv_mid"), nconv[0])
                link(stt(acc, pad[:, left:left + S], v(w, 3 * q), acc, ALU.mult, ALU.add))
                stt(acc, pad[:, right:right + S], v(w, 3 * q + 2), acc, ALU.mult, ALU.add).then_inc(sig("conv_done"), 1)

            def norm_next(f, next_norm, c_):
                if f == 0:
                    add_squares(c_ == 0)
                else:
                    norm_chunk(next_norm, c_)

            def feed_forward(f, next_norm):
                root_wait()
                left, right = (1, 3) if f == 0 else (0, 2)
                for s_ in range(2):
                    nc.vector.memset(gpad[:, s_, 0:2], 0.0)
                    link(nc.vector.memset(gpad[:, s_, 2 + S:4 + S], 0.0))
                for t, chunks in enumerate(THIRDS):
                    for j in range(chunks):
                        q = sum(THIRDS[:t]) + j
                        i, s_ = f * NF + q, q % 2
                        n = TILE0[f"ff{f}_gu{t}"] + 2 * j
                        scaled(gpad[:, s_, 2:2 + S], n)
                        scaled(ups[:, s_, :], n + 1)
                        convolve(gpad[:, s_, :], cva[:, s_, :], left, right, f"fconv_w{f}", q)
                        dve.wait_ge(sig("gate_done"), i + 1)
                        tt(hval[:, s_, :], cva[:, s_, :], ups[:, s_, :], ALU.mult).then_inc(sig("hval_ready"), 1)
                        dve.wait_ge(sig("hid_hi"), i + 1)
                        tt(actL[:, j, :], hval[:, s_, :], actH[:, j, :].bitcast(F32), ALU.subtract)\
                            .then_inc(sig("hid_ready"), 1)
                    acc = MIX if f == 0 else XT
                    for m in range(KD):
                        n = TILE0[f"ff{f}_d{t}"] + m
                        if f == 0 and t == 0:
                            continue
                        tile_wait(dve, n)
                        if f == 0 and t == 1:
                            gone_wait(dve, TILE0["ff0_d0"] + m)
                        free(tt(acc[:, m, :], psum(n)[:, :], acc[:, m, :], ALU.add), n)
                        if t == 2 and m > 0:
                            norm_next(f, next_norm, m - 1)
                norm_next(f, next_norm, KD - 1)

            def post_norm(gain, next_norm):
                root_wait()
                for c_ in range(KD):
                    link(tt(postb[:, c_ % 2, :], MIX[:, c_, :], rstd[:, :], ALU.mult))
                    stt(XT[:, c_, :], postb[:, c_ % 2, :], v(gain, c_), XT[:, c_, :], ALU.mult, ALU.add)\
                        .then_inc(sig("x_new"), 1)
                    if c_ > 0:
                        norm_chunk(next_norm, c_ - 1)
                norm_chunk(next_norm, KD - 1)

            link(nc.vector.memset(ones512[:, :], 1.0))
            for s_ in range(2):
                link(nc.vector.memset(cpad[:, s_, 0:2], 0.0))
                link(nc.vector.memset(cpad[:, s_, 2 + S:4 + S], 0.0))
            link(nc.vector.memset(cumF[:, :, 0:1], 0.0))
            dve.wait_ge(tables_in, 16 * 4)
            dve.wait_ge(x_in, 16 * KD)
            for c_ in range(KD):
                norm_chunk("mix_pre", c_)
            dve.wait_ge(sig("rcol_ready"), 1)
            n = TILE0["gates"]
            tile_wait(dve, n)
            for b in range(NB):
                last = stt(gate_in[:, b, :], psum(n)[:, b * 16:b * 16 + 16], rcol[:, b:b + 1],
                           VT[:, VEC["gate_b"]:VEC["gate_b"] + 16], ALU.mult, ALU.add)
            free(last, n)
            gone_wait(dve, n)
            nc.vector.tensor_copy(bN[:, :, :], gate_in[:, :, 0:8]).then_inc(sig("gates_in"), 1)
            root_wait()
            scaled(lrT[:, :], TILE0["lr"], slice(0, 32))
            gone_wait(dve, TILE0["lr"])
            dve.wait_ge(sig("softplus_f"), 1)
            stt(logf[:, :, :], gate_in[:, :, 8:16], 0.0, lnf[:, :, :], ALU.min, ALU.subtract)\
                .then_inc(sig("logf_ready"), 1)
            for i in range(4):
                n = TILE0["a_qk"] + i
                scaled(cpad[:, i % 2, 2:2 + S], n)
                convolve(cpad[:, i % 2, :], cvm[:, i % 2, :], 1, 3, "mconv_w", i)
            n = TILE0["cum"]
            tile_wait(dve, n)
            link(nc.vector.tensor_copy(bN[:, :, :], psum(n)[:, 0:32].rearrange("p (b h) -> p b h", b=NB)))
            free(tt(aN[:, :, :], gate_in[:, :, 0:8], bN[:, :, :], ALU.subtract), n)
            for i in range(4):
                n = TILE0["b_qk"] + i
                tile_wait(dve, n)
                free(stt(qkB[:, i // 2, i % 2, :], psum(n)[:, :], 0.125 if i < 2 else 1.0, rstd[:, :], ALU.mult,
                         ALU.mult), n)
            for i in range(4):
                dve.wait_ge(sig("softplus_a"), i + 1)
                stt(zc[:, :], zb[:, :], 0.0, zc[:, :], ALU.min, ALU.subtract).then_inc(sig("log_a_made"), 1)
                dve.wait_ge(sig("log_a_made"), i + 1)
                nc.vector.tensor_tensor_scan(cumF[:, i, 1:1 + S], ones512[:, :], zc[:, :], 0.0, ALU.mult, ALU.add)\
                    .then_inc(sig("log_a_used"), 1)
            for i in range(2):
                gone_wait(dve, TILE0["gate_rows"] + i)
            scan = nc.vector.tensor_tensor_scan
            link(scan(rowM[:, 0, :], rowA[:, :], rowA[:, :], 0.0, ALU.max, ALU.max))
            link(scan(rowM[:, 1, ::-1], rowA[:, ::-1], rowA[:, ::-1], 0.0, ALU.max, ALU.max))
            tt(rowG[:, :, :], rowM[:, :, :], rowB[:, :].unsqueeze(1).broadcast_to([8, 2, S]), ALU.add)\
                .then_inc(sig("rows_ready"), 1)
            for i in range(4):
                scaled(gateO[:, i, :], TILE0["a_o"] + i)
            for i in range(4):
                scaled(gateR[:, i, :], TILE0["b_r"] + i)

            def finish_m(i):
                h, d = i // 2, i % 2
                n = TILE0[f"den{i}"]
                tile_wait(dve, n)
                gone_wait(dve, TILE0[f"guard{i}"])
                link(tt(den[:, :], psum(n)[:, :], guard[:, i % 2, :], ALU.max))
                free(stt(den[:, :], psum(n)[:, :], -1.0, den[:, :], ALU.mult, ALU.max), n)
                gone_wait(dve, n)
                link(nc.vector.reciprocal(den[:, :], den[:, :]))
                n = TILE0[f"num{i}"]
                free(tt(yd[:, :] if d else Y[:, h, :], psum(n)[:, :], den[:, :], ALU.mult), n)
                gone_wait(dve, n)
                if d:
                    tt(Y[:, h, :], Y[:, h, :], yd[:, :], ALU.add).then_inc(sig("head_ready"), 1)

            for i in range(9):
                if i < 8:
                    h, d = i // 2, i % 2
                    n = TILE0[f"max{i}"]
                    tile_wait(dve, n)
                    mask = past if d == 0 else future
                    tt(tmpM[:, :].rearrange("p (b t) -> p b t", b=NB), psum(n)[:, :].rearrange("p (b t) -> p b t", b=NB),
                       mask.unsqueeze(1).broadcast_to([P, NB, P]), ALU.add).then_inc(sig("masked"), 1)
                    gone_wait(dve, n)
                    gone_wait(dve, TILE0[f"s{h}"] + 3)
                    for j in range(NB):
                        cols = slice(j * P, S) if d == 0 else slice(0, j * P + P)
                        last = tt(PM[:, i % 2, j, cols], ST[:, j, cols], DT[:, j, cols], ALU.mult)
                    last.then_inc(sig("weights_m"), 1)
                if i > 0:
                    finish_m(i - 1)

            def head_norms(stage, chunk0, gain, gate):
                def finish(h):
                    dve.wait_ge(sig("y_hi"), 4 * stage + h + 1)
                    tt(actL[:, chunk0 + h, :], ht[:, h % 2, :], actH[:, chunk0 + h, :].bitcast(F32), ALU.subtract)\
                        .then_inc(sig("y_ready"), 1)
                for h in range(4):
                    dve.wait_ge(sig("head_root"), 4 * stage + h + 1)
                    if h >= 2:
                        dve.wait_ge(sig("y_ready"), 4 * stage + h - 1)
                    link(stt(ht[:, h % 2, :], Y[:, h, :], v(gain, h), hr[:, h % 2, :], ALU.mult, ALU.mult))
                    dve.wait_ge(sig("gate_act"), 4 * stage + h + 1)
                    tt(ht[:, h % 2, :], ht[:, h % 2, :], gate[:, h, :], ALU.mult).then_inc(sig("head_out"), 1)
                    if h >= 1:
                        finish(h - 1)
                finish(3)
            head_norms(0, 0, "mnorm", gateO)

            for cc in range(2):
                fw, bw = cumF[:, cc], cumF[:, 2 + cc]

                def level_arg(lev):
                    half = 2 ** (lev - 1)
                    s_ = lev % 2
                    used = cc * 9 + (lev - 2 if lev > 2 else 0)
                    if used > 0:
                        dve.wait_ge(sig("level_qk"), used)

                    def halves(a):
                        return a.rearrange("p (n two h) -> p n two h", two=2, h=half)
                    at_, after = halves(fw[:, 0:S]), halves(fw[:, 1:1 + S])
                    bat = halves(bw[:, 0:S])
                    q_, k_ = halves(arg[:, s_, 0, :]), halves(arg[:, s_, 1, :])
                    wide = [P, S // (2 * half), half]
                    mid, bmid = at_[:, :, 1, 0:1].broadcast_to(wide), bat[:, :, 1, 0:1].broadcast_to(wide)
                    tt(q_[:, :, 1, :], after[:, :, 1, :], mid, ALU.subtract)
                    tt(k_[:, :, 0, :], mid, after[:, :, 0, :], ALU.subtract)
                    tt(q_[:, :, 0, :], bmid, bat[:, :, 0, :], ALU.subtract)
                    tt(k_[:, :, 1, :], bat[:, :, 1, :], bmid, ALU.subtract).then_inc(sig("level_arg"), 1)

                def level_apply(lev):
                    dve.wait_ge(sig("level_exp"), cc * 9 + lev)
                    tt(qkL[:, lev % 2, :, :], arg[:, lev % 2, :, :], qkB[:, :, cc, :], ALU.mult)\
                        .then_inc(sig("level_qk"), 1)

                def level_take(lev):
                    for hh in range(2):
                        n = TILE0[f"lev{cc}_{lev}"] + hh
                        tile_wait(dve, n)
                        src = psum(n)[:, :].rearrange("p (b t) -> p b t", b=NB)
                        if lev == 0:
                            free(tt(Pd[:, hh, :, :], src, twice.unsqueeze(1).broadcast_to([P, NB, P]), ALU.mult), n)
                        elif lev < 8:
                            gone_wait(dve, TILE0[f"lev{cc}_{lev - 1}"] + hh)
                            free(nc.vector.copy_predicated(
                                Pd[:, hh, :, :], MASK[:, lev - 1, :].unsqueeze(1).broadcast_to([P, NB, P]), src), n)
                if cc > 0:
                    tile_wait(dve, TILE0[f"o{cc - 1}"] + 1)
                level_arg(1)
                for lev in range(1, 10):
                    if lev < 9:
                        level_arg(lev + 1)
                    if lev >= 2:
                        level_take(lev - 2)
                    level_apply(lev)
                for hh in range(2):
                    n = TILE0[f"o{cc}"] + hh
                    tile_wait(dve, n)
                    free(nc.vector.tensor_copy(Y[:, 2 * cc + hh, :], psum(n)[:, :]), n)
                    gone_wait(dve, n)
                    nc.vector.tensor_copy(tmpY[:, :], Y[:, 2 * cc + hh, 0:1]).then_inc(sig("head_ready"), 1)
            head_norms(1, 4, "gnorm", gateR)
            for c_ in range(KD):
                add_squares(c_ == 0)
            post_norm("mix_post", "ffn_pre")
            feed_forward(0, None)
            post_norm("ffn_post", "mix2_0")

            root_wait()
            for i in range(4):
                nc.vector.memset(upad[:, i, 0:PADU], 0.0)
                nc.vector.memset(glp[:, i, 0:32], 0.0)
            scaled(upad[:, 0, PADU:], TILE0["pc_in"])
            gone_wait(dve, TILE0["pc_in"])
            dve.wait_ge(mem_in, 48)
            for c_ in range(KD):
                add_squares(c_ == 0, MEM)
            for i in range(1, 4):
                scaled(upad[:, i, PADU:], TILE0["pc_in"] + i)
            for i in range(4):
                scaled(glp[:, i, 30:30 + S], TILE0["pc_in"] + 4 + i)
            for i in range(4):
                if i >= 2:
                    dve.wait_ge(sig("glu_gate"), i - 1)
                scaled(sigb[:, i % 2, :], TILE0["pc_in"] + 8 + i)
                if i > 0:
                    dve.wait_ge(sig("glu_gate"), i)
                    link(tt(glp[:, i - 1, 30:30 + S], glp[:, i - 1, 30:30 + S], sigb[:, (i - 1) % 2, :], ALU.mult))
            dve.wait_ge(sig("glu_gate"), 4)
            link(tt(glp[:, 3, 30:30 + S], glp[:, 3, 30:30 + S], sigb[:, 1, :], ALU.mult))
            dve.wait_ge(sig("mem_root"), 1)
            for c_ in range(KD):
                tt(memT[:, c_, :], memT[:, c_, :], rmem[:, :], ALU.mult).then_inc(sig("mem_normed"), 1)
            for l in range(2):
                for c_ in range(KD):
                    low(memL[l][:, c_, :], memT[:, c_, :], v(f"mem{l}", c_), memH[l][:, c_, :])
            dve.wait_ge(unit_done, LAST["pc_in"])
            for g, w in enumerate(POOL_WINDOWS):
                src, shift, bufs = upad[:, g, :], 1, [wina, winb]
                while shift < w:
                    dst = bufs[0]
                    lo = 2 * shift - 1
                    link(tt(dst[:, lo:], src[:, lo:], src[:, lo - shift:S + PADU - shift], ALU.add))
                    src, shift, bufs = dst, 2 * shift, bufs[::-1]
                link(stt(pooled[:, g, :], src[:, PADU:], 1.0 / w, upad[:, g, PADU:], ALU.mult, ALU.subtract))
                link(tt(meanb[:, 0:16], src[:, PADU:PADU + 16], CT[:, CONST["inv_count"] + 16 * g:
                        CONST["inv_count"] + 16 * g + 16], ALU.mult))
                tt(pooled[:, g, 0:16], meanb[:, 0:16], upad[:, g, PADU:PADU + 16], ALU.subtract)\
                    .then_inc(sig("pooled"), 1)
            for k in range(CONV_K):
                for c_ in range(4):
                    tap = glp[:, c_, k:k + S]
                    w = v("dw_w", c_ * CONV_K + k)
                    if k == 0:
                        ins = ts(cvb[:, c_, :], tap, w, v("dw_b", c_), ALU.mult, ALU.add)
                    else:
                        dve.wait_ge(sig("conv31"), 4 * (k - 1) + c_ + 1)
                        ins = stt(cvb[:, c_, :], tap, w, cvb[:, c_, :], ALU.mult, ALU.add)
                    ins.then_inc(sig("conv31"), 1)
            dve.wait_ge(sig("conv31"), 4 * CONV_K)
            link(tt(ssq[:, :], cvb[:, 0, :], cvb[:, 1, :], ALU.add))
            link(tt(ssq[:, :], ssq[:, :], cvb[:, 2, :], ALU.add))
            tt(ssq[:, :], ssq[:, :], cvb[:, 3, :], ALU.add).then_inc(sig("ln_sum"), 1)

            def pc_low(i, chunk):
                dve.wait_ge(sig("pc_hi"), i + 1)
                tt(actL[:, chunk, :], ybuf[:, i % 2, :], actH[:, chunk, :].bitcast(F32), ALU.subtract)\
                    .then_inc(sig("pc_ready"), 1)
            for g in range(4):
                pc_low(g, g)
            n = TILE0["ln_mean"]
            tile_wait(dve, n)
            free(ts(meanb[:, :], psum(n)[:, :], 1.0 / S, None, ALU.mult), n)
            gone_wait(dve, n)
            for c_ in range(4):
                tt(cvb[:, c_, :], cvb[:, c_, :], meanb[:, :], ALU.subtract).then_inc(sig("centred"), 1)
            for c_ in range(4):
                add_squares(c_ == 0)
            root_wait()
            for c_ in range(4):
                tt(cvb[:, c_, :], cvb[:, c_, :], rstd[:, :], ALU.mult).then_inc(sig("scaled"), 1)
            for c_ in range(4):
                pc_low(4 + c_, 4 + c_)

            def add_to_x(name, next_norm):
                for m in range(KD):
                    n = TILE0[name] + m
                    tile_wait(dve, n)
                    free(tt(XT[:, m, :], psum(n)[:, :], XT[:, m, :], ALU.add), n)
                    if m > 0:
                        norm_chunk(next_norm, m - 1)
                norm_chunk(next_norm, KD - 1)
            add_to_x("pc_out", "xa0")

            def cross_attention(l, next_norm):
                base = TILE0[f"xatt{l}"]
                root_wait()
                for i in range(KD):
                    scaled(qX[:, i, :], TILE0[f"xq{l}"] + i)

                def output_low(h):
                    for f in range(2):
                        dve.wait_ge(sig("x_hi"), 8 * l + 2 * h + f + 1)
                        n = xtile(base, "o", h, f)
                        free(tt(actL[:, 2 * h + f, :], psum(n)[:, :], actH[:, 2 * h + f, :].bitcast(F32),
                                ALU.subtract), n)
                for h in range(4):
                    for pair in range(2):
                        n = xtile(base, "s", h, pair)
                        tile_wait(dve, n)
                        link(nc.vector.reduce_max(xst[:, pair, 0:2], psum(n)[:, :].rearrange("p (q m) -> p q m", q=2),
                                                  AX.X))
                        ts(xst[:, pair, 2:4], xst[:, pair, 0:2], -1.0 / 16, None, ALU.mult).then_inc(sig("x_max"), 1)
                    for pair in range(2):
                        gone_wait(dve, xtile(base, "s", h, pair))
                        link(nc.vector.reciprocal(xst[:, pair, 6:8], xst[:, pair, 4:6]))
                        for q in range(2):
                            last = ts(EX[:, pair, q, :], EX[:, pair, q, :], xst[:, pair, 6 + q:7 + q], None, ALU.mult)
                        last.then_inc(sig("x_probs"), 1)
                    if h > 0:
                        output_low(h - 1)
                output_low(3)
                add_to_x(f"xo{l}", next_norm)

            cross_attention(0, "ffn2_0")
            feed_forward(1, "mix2_1")

            link(nc.vector.tensor_copy(posF[:, :], posI[:, :]))
            freq = CT[:, CONST["inv_freq"]:CONST["inv_freq"] + 16].unsqueeze(1).broadcast_to([P, NB, 16])
            link(tt(angA[:, :, :], freq, posF[:, :].unsqueeze(2).broadcast_to([P, NB, 16]), ALU.mult))
            link(ts(angB[:, :, :], angA[:, :, :], 1.0 / TWO_PI, ROUND, ALU.mult, ALU.add))
            link(ts(angB[:, :, :], angB[:, :, :], ROUND, None, ALU.subtract))
            for part in (TWO_PI_A, TWO_PI_B, TWO_PI_C):
                link(stt(angA[:, :, :], angB[:, :, :], -part, angA[:, :, :], ALU.mult, ALU.add))
            link(ts(angC[:, :, :], angA[:, :, :], TWO_PI / 4, TWO_PI / 2, ALU.add, ALU.is_gt))
            link(stt(angC[:, :, :], angC[:, :, :], -TWO_PI, angA[:, :, :], ALU.mult, ALU.add))
            link(ts(angC[:, :, :], angC[:, :, :], TWO_PI / 4, None, ALU.add))
            ts(angB[:, :, :], angA[:, :, :], 3.1415925, -3.1415925, ALU.min, ALU.max).then_inc(sig("angle"), 1)
            ts(angC[:, :, :], angC[:, :, :], 3.1415925, -3.1415925, ALU.min, ALU.max).then_inc(sig("angle"), 1)
            root_wait()
            for i in range(5):
                g_ = v("q_norm", i) if i < 3 else v("kv_norm", i - 3)
                n = TILE0["w_dq"] + i
                scaled(qpn[:, i % 2, :], n)
                gone_wait(dve, n)
                dve.wait_ge(sig("lora_sq"), i + 1)
                dst, src = sq[:, i // 3, :], qpr[:, i % 2, :]
                if i in (0, 3):
                    ins = nc.vector.tensor_copy(dst, src)
                else:
                    ins = tt(dst, dst, src, ALU.add)
                ins.then_inc(sig("lora_added"), 1)
                dve.wait_ge(sig("lora_added"), i + 1)
                dve.wait_ge(sig("c_hi"), i + 1)
                stt(cL[:, i, :], qpn[:, i % 2, :], g_, cH[:, i, :].bitcast(F32), ALU.mult, ALU.subtract)\
                    .then_inc(sig("c_ready"), 1)

            def contents(name, dst, root):
                for i in range(8):
                    n = TILE0[name] + i
                    tile_wait(dve, n)
                    tt(dst[0:64, 2 * i, :], psum(n)[0:64, :], root[0:64, :], ALU.mult)
                    free(tt(dst[0:64, 2 * i + 1, :], psum(n)[64:P, :], root[64:P, :], ALU.mult), n)
            dve.wait_ge(sig("lora_root"), 1)
            contents("q_nope", QC, rq)

            def rotate(dst, src, b, heads):
                w = [P, heads, 16]
                cos, sin = cosT[:, b:b + 1, :].broadcast_to(w), sinT[:, b:b + 1, :].broadcast_to(w)
                x1, x2 = src[:, :, 0:16], src[:, :, 16:32]
                t = [z.rearrange("p (h c) -> p h c", c=16) for z in
                     (ssq[:, 0:16 * heads], ssq[:, 256:256 + 16 * heads], lnv[:, 0:16 * heads],
                      lnv[:, 256:256 + 16 * heads])]
                tt(t[0], x1, cos, ALU.mult)
                tt(t[1], x2, sin, ALU.mult)
                tt(t[2], x1, sin, ALU.mult)
                link(tt(t[3], x2, cos, ALU.mult))
                tt(dst[:, :, 0:16], t[0], t[1], ALU.subtract)
                return tt(dst[:, :, 16:32], t[2], t[3], ALU.add)
            dve.wait_ge(sig("turned"), 2)
            gone_wait(dve, TILE0["k_pe"])
            for b in range(NB):
                last = rotate(kpr[:, b:b + 1, :], kpn[:, b:b + 1, :], b, 1)
                if b < NB - 1:
                    link(last)
            last.then_inc(sig("k_rotated"), 1)
            dve.wait_ge(sig("k_rotated"), 1)
            for b in range(NB):
                gone_wait(dve, TILE0["q_pe"] + b)
                if b == 2:
                    root_wait()
                    contents("k_nope", KC, rstd)
                if b >= 2:
                    tile_wait(dve, TILE0["pe_turn"] + b - 2)
                rotate(qpr[:, b % 2, :].rearrange("p (h c) -> p h c", c=32),
                       qpn[:, b % 2, :].rearrange("p (h c) -> p h c", c=32), b, MLA_HEADS).then_inc(sig("q_rotated"), 1)
                dve.wait_ge(sig("q_rotated"), b + 1)
            n = TILE0["pe_turn"] + 4
            tile_wait(dve, n)
            dve.wait_ge(sig("k_rows"), 1)
            free(nc.vector.tensor_copy(KC[64:96, 0:8, :], psum(n)[0:32, :].unsqueeze(1).broadcast_to([32, 8, S])), n)

            scale = (64 + 32) ** -0.5

            def att_low(h):
                dve.wait_ge(sig("m_hi"), h + 1)
                n = mtile("o", h, 0)
                rows = slice(64 * (h % 2), 64 * (h % 2) + 64)
                free(tt(oHL[rows, h // 2 * 2 + 1, :], psum(n)[rows, :], oHL[rows, h // 2 * 2, :].bitcast(F32),
                        ALU.subtract), n)

            def att_rows(h):
                for b in (1, 3):
                    n = mtile("t", h, b)
                    tile_wait(dve, n)
                    if h >= 2:
                        tile_wait(dve, mtile("o", h - 2, 0))
                    free(nc.vector.tensor_copy(PX2[:, h % 2, 0:b + 1, b * P:b * P + P],
                                               psum(n)[:, 0:(b + 1) * P].rearrange("p (j q) -> p j q", q=P)), n)

            for i in range(MLA_HEADS):
                s_ = i % 2
                for b in range(NB):
                    n = mtile("s", i, b)
                    tile_wait(dve, n)
                    last = nc.vector.reduce_max(mst[:, s_, b:b + 1], psum(n)[:, 0:(b + 1) * P], AX.X)
                link(last)
                ts(mst[:, s_, 4:8], mst[:, s_, 0:4], -scale, None, ALU.mult).then_inc(sig("m_max"), 1)
                if i > 0:
                    att_rows(i - 1)
                for b in range(NB):
                    gone_wait(dve, mtile("s", i, b))
                link(nc.vector.reciprocal(mst[:, s_, 12:16], mst[:, s_, 8:12]))
                for b in range(NB):
                    w = (b + 1) * P
                    ts(EM[:, b, 0:w], EM[:, b, 0:w], mst[:, s_, 12 + b:13 + b], None, ALU.mult)\
                        .then_inc(sig("m_probs"), 1)
                if i > 0:
                    att_low(i - 1)
            att_rows(MLA_HEADS - 1)
            att_low(MLA_HEADS - 1)
            add_to_x("mla_o", "xa1")
            cross_attention(1, "ffn2_1")
            feed_forward(2, "final")
            root_wait()
            for c_ in range(KD):
                stt(MIX[:, c_, :], XT[:, c_, :], v("final", c_), rstd[:, :], ALU.mult, ALU.mult)\
                    .then_inc(sig("final"), 1)


def columns(a):
    return a.reshape(-1, P).T


def stationary(w):
    k, n = w.shape
    return w.reshape(k // P, P, n // P, P).transpose(2, 1, 0, 3).reshape(n // P, P, k)


def moving(w):
    k, n = w.shape
    units = []
    for g in range(n // S):
        chunks = [w[c * P:c * P + P, g * S:g * S + S] for c in range(k // P)]
        for i in range(0, len(chunks), 2):
            units.append(np.concatenate(chunks[i:i + 2], axis=1))
    return units


def lay_weights(a):
    w_in = a["w_in"][0]
    widths = (512, 512, 512, 16, 256, 256, 512, 512, 32)
    a_qk, a_v, a_o, gates, b_q, b_k, b_v, b_r, b_lr = np.split(w_in, np.cumsum(widths)[:-1], axis=1)
    gates = gates.reshape(D, 4, 4)[:, [0, 2, 1, 3]].reshape(D, 16)
    small = np.concatenate([gates, b_lr], axis=1)
    kpe = a["mla_w_dq_dkv_2"][0][:, 640:672]
    uq = a["mla_w_uq_2"][0].reshape(384, MLA_HEADS, 96)
    ukv = a["mla_w_ukv_2"][0].reshape(256, MLA_HEADS, 128)

    def narrow(w):
        return [w.reshape(KD, P, -1).transpose(1, 0, 2).reshape(P, -1)]

    def grouped(w, per):
        st = stationary(w)
        return [np.concatenate(list(st[i:i + per]), axis=1) for i in range(0, len(st), per)]
    groups = {
        "lr_gates": narrow(small), "a_qk": stationary(a_qk), "b_qk": stationary(np.concatenate([b_q, b_k], axis=1)),
        "a_v": moving(a_v), "b_v": moving(b_v), "a_o": stationary(a_o), "b_r": stationary(b_r),
        "w_out": stationary(a["w_out"][0]), "pc_in": stationary(a["pc_w_in_2"][0]),
        "pc_out": stationary(a["pc_w_out_2"][0]), "k_pe": narrow(kpe),
        "w_dq": stationary(a["mla_w_dq_dkv_2"][0][:, :640]),
        "q_nope": grouped(uq[:, :, :64].reshape(384, 1024), 2), "q_pe": moving(uq[:, :, 64:].reshape(384, 512)),
        "k_nope": grouped(ukv[:, :, :64].reshape(256, 1024), 4), "mla_v": moving(ukv[:, :, 64:].reshape(256, 1024)),
        "mla_o": stationary(a["mla_w_o_2"][0]),
    }
    for l in range(2):
        groups[f"mem_k{l}"] = stationary(a["xa_wkv_2"][l][:, :D])
        groups[f"mem_v{l}"] = moving(a["xa_wkv_2"][l][:, D:])
        groups[f"xq{l}"] = stationary(a["xa_wq_2"][l])
        groups[f"xo{l}"] = stationary(a["xa_wo_2"][l])
    layers = [(a["ffn_w_gate"][0], a["ffn_w_up"][0], a["ffn_w_down"][0])]
    for l in range(2):
        up = a["ffn_w_up_2"][l]
        layers.append((up[:, FF:], up[:, :FF], a["ffn_w_down_2"][l]))
    for i, (gate, up, down) in enumerate(layers):
        pairs = np.stack([stationary(gate), stationary(up)], axis=1).reshape(2 * NF, P, D)
        at = 0
        for t, c in enumerate(THIRDS):
            groups[f"ff{i}_gu{t}"] = pairs[2 * at:2 * (at + c)]
            groups[f"ff{i}_d{t}"] = stationary(down[at * P:(at + c) * P])
            at += c
    laid = np.zeros((NUNITS, P, UNIT), np.float32)
    for name, count, width in UNITS:
        assert len(groups[name]) == count, name
        for i, w in enumerate(groups[name]):
            laid[UNIT0[name] + i, :, :w.shape[1]] = w
    return laid


def lay_vectors(a):
    cols = {
        "mix_pre": a["norm_mix_pre"][0], "mix_post": a["norm_mix_post"][0], "ffn_pre": a["norm_ffn_pre"][0],
        "ffn_post": a["norm_ffn_post"][0], "mix2_0": a["norm_mix_g_2"][0], "mix2_1": a["norm_mix_g_2"][1],
        "xa0": a["norm_xa_g_2"][0], "xa1": a["norm_xa_g_2"][1], "mem0": a["norm_mem_g_2"][0],
        "mem1": a["norm_mem_g_2"][1], "ffn2_0": a["norm_ffn_g_2"][0], "ffn2_1": a["norm_ffn_g_2"][1],
        "final": a["final_norm_g_2"], "mconv_b": a["mlstm_conv_b"][0], "mnorm": a["mlstm_norm"][0],
        "gla_b": a["gla_b"][0], "gnorm": a["gla_norm"][0], "fconv_b0": a["ffn_conv_b"][0],
        "fconv_b1": a["ffn_conv_b_2"][0], "fconv_b2": a["ffn_conv_b_2"][1], "pool_scale": a["pool_scale_2"][0],
        "dw_b": a["conv_dw_b_2"][0], "ln_g": a["conv_ln_g_2"][0], "ln_b": a["conv_ln_b_2"][0],
        "q_norm": a["mla_q_norm_g_2"][0], "kv_norm": a["mla_kv_norm_g_2"][0],
    }
    laid = np.zeros((P, NVEC), np.float32)
    for name, w in cols.items():
        c = columns(w)
        laid[:, VEC[name]:VEC[name] + c.shape[1]] = c
    for name, w in (("mconv_w", a["mlstm_conv_w"][0]), ("fconv_w0", a["ffn_conv_w"][0]),
                    ("fconv_w1", a["ffn_conv_w_2"][0]), ("fconv_w2", a["ffn_conv_w_2"][1]),
                    ("dw_w", a["conv_dw_w_2"][0])):
        taps, width = w.shape
        c = w.reshape(taps, width // P, P).transpose(2, 1, 0).reshape(P, -1)
        laid[:, VEC[name]:VEC[name] + c.shape[1]] = c
    laid[:, VEC["gate_b"]:VEC["gate_b"] + 16] = a["mlstm_gate_b"][0].reshape(4, 4)[[0, 2, 1, 3]].reshape(16)
    laid[:, VEC["eps"]] = 1e-6
    laid[:, VEC["one"]] = 1.0
    return laid


def constants():
    p, f = np.arange(P)[:, None], np.arange(P)[None, :]
    laid = np.zeros((P, NCONST), np.float32)

    def put(name, w):
        laid[:, CONST[name]:CONST[name] + w.shape[1]] = w
    put("ident", (p == f) * 1.0)
    put("ones", np.ones((P, P)))
    put("past", (f < p) * BIG)
    put("future", (f > p) * BIG)
    put("upto", (p <= f) * 1.0)
    put("since", (p >= f) * 1.0)
    put("twice", (p == f) * 2.0)
    put("neg_future", (f > p) * -BIG)
    counts = [np.minimum(np.arange(16) + 1, w).astype(np.float32) for w in POOL_WINDOWS]
    put("inv_count", np.tile(np.concatenate([np.float32(1.0) / c for c in counts]), (P, 1)))
    inv = np.float32(1.0) / (np.float32(10000.0) ** (np.arange(0, 32, 2, dtype=np.float32) / np.float32(32)))
    put("inv_freq", np.tile(inv.astype(np.float32), (P, 1)))
    masks = np.stack([((p // (2 * h) == f // (2 * h)) & (p // h != f // h)) for h in HALVES], axis=1).astype(np.int32)
    return laid, masks


def kernel(**inputs):
    import concourse.bacc as bacc
    from concourse.bass_utils import run_bass_kernel_spmd

    a = {k: np.asarray(w) for k, w in inputs.items()}
    consts, masks = constants()
    w2 = np.zeros((32, 2, 256), np.float32)
    w2[0:16, 0], w2[16:32, 1] = a["gla_w2"][0, 0], a["gla_w2"][0, 1]
    arrays = {
        "x_t": np.ascontiguousarray(a["x"][0].T), "mem_t": np.ascontiguousarray(a["mem_2"][0].T),
        "positions": np.ascontiguousarray(a["positions_2"][0].reshape(NB, P).T),
        "weights": lay_weights(a), "pool_w": np.ascontiguousarray(a["pool_w_2"][0]), "gla_w2": w2,
        "vecs": lay_vectors(a), "consts": consts, "masks": masks,
    }
    nc = bacc.Bacc("TRN2", target_bir_lowering=False, num_devices=1, dynamic_dma_scratch_size=1024)
    args = {n: nc.dram_tensor(n, w.shape, mybir.dt.from_np(w.dtype), kind="ExternalInput").ap()
            for n, w in arrays.items()}
    out = nc.dram_tensor("out", (D, S), F32, kind="ExternalOutput").ap()
    program(nc, out=out, **args)
    result = run_bass_kernel_spmd(nc, [arrays], core_ids=[0])
    return np.ascontiguousarray(result.results[0]["out"].T).reshape(1, S, D)
```

```python
import numpy as np
import concourse.bass as bass
from concourse import mybir
from contextlib import ExitStack

F32 = mybir.dt.float32
F32R = mybir.dt.float32r
I32 = mybir.dt.int32
ALU = mybir.AluOpType
ACT = mybir.ActivationFunctionType
AX = mybir.AxisListType

P = 128
S = 512
D = 1024
KD = D // P
NB = S // P
MEM = 256
FF = 2816
NF = FF // P
THIRDS = (8, 8, 6)
RING = 4
UNIT = 1024
BIG = 1e30
HALVES = (1, 2, 4, 8, 16, 32, 64)
POOL_WINDOWS = (2, 4, 8, 16)
CONV_K = 31
POOL_LOW_AT = (11, 13, 15, 17)
MLA_HEADS = 16
TWO_PI = 6.283185307179586
TWO_PI_A = 6.28125
TWO_PI_B = 0.0019350051879882812
TWO_PI_C = TWO_PI - TWO_PI_A - TWO_PI_B
ROUND = 12582912.0

VEC_SIZES = [("mix_pre", 8), ("mix_post", 8), ("ffn_pre", 8), ("ffn_post", 8), ("mix2_0", 8), ("mix2_1", 8),
             ("xa0", 8), ("xa1", 8), ("mem0", 8), ("mem1", 8), ("ffn2_0", 8), ("ffn2_1", 8), ("final", 8),
             ("mconv_w", 12), ("mconv_b", 4), ("mnorm", 4), ("gla_b", 4), ("gnorm", 4),
             ("fconv_w0", 66), ("fconv_b0", 22), ("fconv_w1", 66), ("fconv_b1", 22), ("fconv_w2", 66), ("fconv_b2", 22),
             ("pool_scale", 4), ("dw_w", 4 * CONV_K), ("dw_b", 4), ("ln_g", 4), ("ln_b", 4),
             ("q_norm", 3), ("kv_norm", 2), ("gate_b", 16), ("eps", 1), ("one", 1)]
VEC, _at = {}, 0
for _n, _w in VEC_SIZES:
    VEC[_n] = _at
    _at += _w
NVEC = _at

CONST_SIZES = [("ident", 128), ("ones", 128), ("past", 128), ("future", 128), ("upto", 128), ("since", 128),
               ("twice", 128), ("neg_future", 128), ("inv_count", 64), ("inv_freq", 16)]
CONST, _at = {}, 0
for _n, _w in CONST_SIZES:
    CONST[_n] = _at
    _at += _w
NCONST = _at

UNITS = [("lr_gates", 1, 8 * 48), ("a_qk", 4, 1024), ("b_qk", 4, 1024), ("a_v", 4, 1024), ("b_v", 4, 1024),
         ("a_o", 4, 1024), ("b_r", 4, 1024), ("w_out", 8, 1024)]
for _i in range(3):
    if _i == 1:
        UNITS += [("pc_in", 12, 1024), ("mem_k0", 8, 1024), ("mem_v0", 8, 1024), ("mem_k1", 8, 1024),
                  ("mem_v1", 8, 1024), ("pc_out", 8, 1024)]
    if _i == 2:
        UNITS += [("k_pe", 1, 256), ("w_dq", 5, 1024), ("q_nope", 4, 768), ("q_pe", 2, 1024),
                  ("k_nope", 2, 1024), ("mla_v", 2, 1024), ("mla_o", 8, 1024)]
    if _i > 0:
        UNITS += [(f"xq{_i - 1}", 8, 1024), (f"xo{_i - 1}", 8, 1024)]
    for _t, _c in enumerate(THIRDS):
        UNITS += [(f"ff{_i}_gu{_t}", 2 * _c, 1024), (f"ff{_i}_d{_t}", 8, _c * 128)]
UNIT0, _at = {}, 0
for _n, _c, _w in UNITS:
    UNIT0[_n] = _at
    _at += _c
NUNITS = _at

TILES = [("col_sum1", 1), ("row_sum1", 1), ("gates", 1), ("lr", 1), ("a_qk", 4), ("cum", 1), ("b_qk", 4),
         ("log_a", 4), ("gate_rows", 2), ("a_v", 4), ("b_v", 4), ("a_o", 4), ("b_r", 4)]
OWN_BANKS = {}
for _n in range(9):
    if _n < 8:
        TILES += [(f"max{_n}", 1), (f"guard{_n}", 1)] + ([(f"s{_n // 2}a", 2)] if _n % 2 == 0 else [])
        OWN_BANKS.update({f"max{_n}": 2, f"guard{_n}": 3, f"s{_n // 2}a": 0, f"s{_n // 2}b": 0})
    if _n > 0:
        TILES += [(f"num{_n - 1}", 1), (f"den{_n - 1}", 1)]
        OWN_BANKS.update({f"num{_n - 1}": 4 + 2 * (_n % 2), f"den{_n - 1}": 5 + 2 * (_n % 2)})
    if _n < 8 and _n % 2 == 0:
        TILES += [(f"s{_n // 2}b", 2)]
TILES += [("norm_a", 4)]
for _c in range(2):
    TILES += [(f"lev{_c}_{_l}", 2) for _l in range(9)] + [(f"lev{_c}_9", 4), (f"o{_c}", 2)]
TILES += [("norm_b", 4), ("w_out", 8), ("post0", 1)]
for _i in range(3):
    if _i == 1:
        TILES += [("post1", 1), ("row_sum3", 1), ("pc_in", 12), ("mem_sums", 1), ("mem_k0", 8), ("mem_v0", 4), ("pool", 4), ("mem_k1", 8),
                  ("mem_v1", 4), ("pc_out", 6), ("ln_mean", 1), ("ln_var", 1), ("pc_out_end", 2)]
    if _i == 2:
        TILES += [("row_sum6", 1), ("col_sum6", 1), ("k_pe", 1), ("w_dq", 5), ("q_sum", 2), ("kv_sum", 2),
                  ("q_nope", 8), ("q_pe", 4), ("k_nope", 8), ("k_turn", 1), ("q_turn01", 2), ("mla_v", 8), ("q_turn23", 2)]
        TILES += [("att", 9 * MLA_HEADS), ("mla_o", 8)]
    if _i > 0:
        TILES += [(f"row_sum_x{_i - 1}", 1), (f"xq{_i - 1}", 8), (f"xatt{_i - 1}", 24), (f"xo{_i - 1}", 8)]
    TILES += [(f"row_sum_f{_i}", 1)]
    for _t, _c in enumerate(THIRDS):
        TILES += [(f"ff{_i}_gu{_t}", 2 * _c), (f"ff{_i}_d{_t}", 8)]
TILES += [("row_sum_end", 1)]

TILE0, TILE_DONE, _at, _others = {}, [], 0, 0
BANK, TURN, _next, _uses = [], [], 0, [0] * 8
_count = {n: k for n, k, _ in UNITS}
for _n, _c in TILES:
    TILE0[_n] = _at
    _at += _c
    for _i in range(_c):
        BANK.append(OWN_BANKS[_n] + _i if _n in OWN_BANKS else _next % 8)
        _next = BANK[-1] + 1
        TURN.append(_uses[BANK[-1]])
        _uses[BANK[-1]] += 1
        if _n in ("gates", "lr"):
            TILE_DONE.append(("unit", UNIT0["lr_gates"] + 1))
        elif _n.startswith("pc_out"):
            TILE_DONE.append(("unit", UNIT0["pc_out"] + (4 + _i // 2 if _n == "pc_out" else 7 + _i)))
        elif _n in _count:
            _per = max(1, _c // _count[_n])
            if _n in ("a_v", "b_v", "q_pe"):
                TILE_DONE.append(("unit", UNIT0[_n] + _count[_n]))
            elif _n.startswith("mem_v"):
                TILE_DONE.append(("unit", UNIT0[_n] + 4 * (_i // 2) + 4))
            else:
                TILE_DONE.append(("unit", UNIT0[_n] + _i // _per + 1))
        else:
            _others += 1
            TILE_DONE.append(("tile", _others))

NORMS = ["mix_pre", "ffn_pre", "mix2_0", "mem0", "mem1", "xa0", "ffn2_0", "mix2_1", "xa1", "ffn2_1"]
SQ_END, _at = {}, 0
for _n in ("mix_pre", "post0", "ffn_pre", "post1", "mix2_0", "mem", "ln", "xa0", "ffn2_0", "mix2_1", "xa1", "ffn2_1",
           "final"):
    _at += 4 if _n == "ln" else KD
    SQ_END[_n] = _at


def xtile(base, kind, h, i):
    return base + {"s": (0, 2, 6, 12), "t": (4, 10, 16, 20), "o": (8, 14, 18, 22)}[kind][h] + i


def s_tile(h, j):
    return TILE0[f"s{h}a"] + j if j < 2 else TILE0[f"s{h}b"] + j - 2


def mtile(kind, h, b):
    i = h + {"s": 0, "t": 1, "o": 2}[kind]
    start = (0, 4)[i] if i < 2 else 9 * i - 6 if i <= MLA_HEADS else 9 * MLA_HEADS - 1
    if kind == "t":
        start += (4 if i < MLA_HEADS else 0) + (1 if i >= 2 else 0)
    elif kind == "o":
        start += 4 if i < MLA_HEADS else 0
    return TILE0["att"] + start + b



def pc_tile(m):
    return TILE0["pc_out"] + m if m < 6 else TILE0["pc_out_end"] + m - 6


def turn_tile(b):
    return TILE0["q_turn01"] + b if b < 2 else TILE0["q_turn23"] + b - 2


def program(nc, x_t, mem_t, positions, weights, pool_w, gla_w2, vecs, consts, masks, out):
    ctx = ExitStack()
    with ctx:
        place = [1152]

        def at(name, shape, dt=F32, offset=None):
            size = int(np.prod(shape[1:])) * 4
            if offset is None:
                offset = place[0]
                place[0] += (size + 63) // 64 * 64
            return nc.alloc_sbuf_tensor_at(name, shape, dt, offset=offset)

        def sem(name):
            return ctx.enter_context(nc.semaphore(name))

        XT = at("XT", [P, KD, S])
        hn_at = place[0]
        hnH = at("hnH", [P, KD, S], F32R)
        hnL = at("hnL", [P, KD, S], F32R)
        act_at = place[0]
        actH = at("actH", [P, KD, S], F32R)
        actL = at("actL", [P, KD, S], F32R)
        mix_at = place[0]
        MIX = at("MIX", [P, KD, S])
        place[0] += 64
        raw = at("raw", [P, RING, UNIT])
        wH = at("wH", [P, RING, UNIT], F32R)
        wL = at("wL", [P, RING, UNIT], F32R)
        VT = at("VT", [P, NVEC])
        CT = at("CT", [P, NCONST])
        MASK = at("MASK", [P, len(HALVES), P], I32)
        zero = at("zero", [P, 16])
        identR = at("identR", [P, P], F32R)
        neg_futureR = at("neg_futureR", [P, P], F32R)
        rstd = at("rstd", [P, S])
        rcol = at("rcol", [P, NB])
        ssq = at("ssq", [P, S])
        sq = at("sq", [P, 2, S])
        lnb = at("lnb", [P, S])
        lncol = at("lncol", [P, NB])
        lnv = at("lnv", [P, S])
        tmpY = at("tmpY", [P, 1])
        scr = place[0]
        TOP = 229344
        KB2 = 4 * S
        gpad = at("gpad", [P, 2, S + 4], offset=scr)
        ups = at("ups", [P, 2, S], offset=scr + 4160)
        cva = at("cva", [P, 2, S], offset=scr + 8320)
        hval = at("hval", [P, 2, S], offset=scr + 12480)
        o = scr
        cpad = at("cpad", [P, 2, S + 4], offset=o)
        cvm = at("cvm", [P, 2, S], offset=o + 4160)
        Y = at("Y", [P, 4, S], offset=o)
        o += 8256
        qkA = at("qkA", [P, 4, S], offset=o); o += 4 * KB2
        qkB = at("qkB", [P, 2, 2, S], offset=o); o += 4 * KB2
        VA = at("VA", [P, NB, S], offset=o); o += 4 * KB2
        gateO = at("gateO", [P, 4, S], offset=o); o += 4 * KB2
        VB = at("VB", [P, NB, S], offset=o); o += 4 * KB2
        gate_in = at("gate_in", [P, NB, 16], offset=o); o += 256
        absf = at("absf", [P, NB, 8], offset=o); o += 128
        lnf = at("lnf", [P, NB, 8], offset=o); o += 128
        logf = at("logf", [P, NB, 8], offset=o); o += 128
        bN = at("bN", [P, NB, 8], offset=o); o += 128
        aN = at("aN", [P, NB, 8], offset=o); o += 128
        assert o <= TOP, (o, TOP)
        hr = at("hr", [P, 2, S], offset=scr + 8256)
        ht = at("ht", [P, 2, S], offset=scr + 8256 + 2 * KB2)
        gateR = at("gateR", [P, 4, S], offset=mix_at)
        cumF = at("cumF", [P, 4, S + 1], offset=mix_at + 4 * KB2)
        o = act_at
        rowA = at("rowA", [8, S], offset=o); o += KB2
        rowB = at("rowB", [8, S], offset=o); o += KB2
        rowM = at("rowM", [8, 2, S], offset=o); o += 2 * KB2
        rowG = at("rowG", [8, 2, S], offset=o); o += 2 * KB2
        zb = at("zb", [P, S], offset=o); o += KB2
        zc = at("zc", [P, S], offset=o); o += KB2
        tmpM = at("tmpM", [P, S], offset=o); o += KB2
        guard = at("guard", [P, 2, S], offset=o); o += 2 * KB2
        o += KB2
        yd = at("yd", [P, S], offset=o); o += KB2
        lrT = at("lrT", [32, S], offset=o); o += KB2
        W2 = at("W2", [32, 2, 256], offset=o)
        den = at("den", [P, 2, S], offset=o); o += KB2
        ones512 = at("ones512", [P, S], offset=o); o += KB2
        assert o <= mix_at
        o = hn_at
        ST = at("ST", [P, NB, S], offset=o); o += 4 * KB2
        DT = at("DT", [P, NB, S], offset=o); o += 4 * KB2
        PM = at("PM", [P, 2, NB, S], offset=o); o += 8 * KB2
        assert o <= act_at
        o = hn_at
        arg = at("arg", [P, 2, 2, S], offset=o); o += 4 * KB2
        qkL = at("qkL", [P, 2, 2, S], offset=o); o += 4 * KB2
        Pd = at("Pd", [P, 2, NB, P], offset=o); o += 2 * KB2
        P1 = at("P1", [P, 2, NB, P], offset=o); o += 2 * KB2
        P2 = at("P2", [P, 2, NB, 2 * P], offset=o); o += 4 * KB2
        KT = [at("KT0", [P, KD, MEM], offset=mix_at), at("KT1", [P, KD, MEM], offset=scr + 22528)]
        VM = [at("VM0", [P, 2, D], offset=mix_at + 4 * KB2), at("VM1", [P, 2, D], offset=scr + 22528 + 4 * KB2)]
        up = scr + 22528 + 8 * KB2
        memT = at("memT", [P, KD, MEM], offset=up)
        up2 = up + 4 * KB2
        rmem = at("rmem", [P, MEM], offset=up2)
        cosT = at("cosT", [P, NB, 16], offset=up2 + 1088)
        sinT = at("sinT", [P, NB, 16], offset=up2 + 1344)
        posI = at("posI", [P, NB], I32, offset=up2 + 1600)
        posF = at("posF", [P, NB], offset=up2 + 1664)
        angA = at("angA", [P, NB, 16], offset=up2 + 1728)
        angB = at("angB", [P, NB, 16], offset=up2 + 1984)
        angC = at("angC", [P, NB, 16], offset=up2 + 2240)
        rcq = at("rcq", [P, 8], offset=up2 + 2496)
        kpn = at("kpn", [P, NB, 32], offset=up2 + 2560)
        kpr = at("kpr", [P, NB, 32], offset=up2 + 3072)
        assert up2 + 3584 + 2048 <= TOP, (up2, TOP)
        memH = [at(f"memH{i}", [P, KD, MEM], F32R, offset=act_at + 8 * i * KB2) for i in range(2)]
        memL = [at(f"memL{i}", [P, KD, MEM], F32R, offset=act_at + (8 * i + 4) * KB2) for i in range(2)]
        PADU = 16
        upad = at("upad", [P, 4, S + PADU], offset=scr)
        wina = at("wina", [P, S + PADU], offset=hn_at + 10 * KB2)
        winb = at("winb", [P, S + PADU], offset=hn_at + 12 * KB2)
        sigb = at("sigb", [P, 2, S], offset=scr + 17152)
        glp = at("glp", [P, 4, S + 32], offset=scr + 8448)
        cvb = at("cvb", [P, 4, S], offset=hn_at)
        pooled = at("pooled", [P, 4, S], offset=hn_at + 4 * KB2)
        pwt = at("pwt", [P, 4, P], offset=up2 + 3584)
        poolL = at("poolL", [P, 4, S], F32R, offset=scr)
        meanb = at("meanb", [P, S], offset=hn_at + 9 * KB2)
        ybuf = at("ybuf", [P, 2, S], offset=hn_at + 14 * KB2)
        qX = at("qX", [P, KD, S], offset=scr)
        EX = at("EX", [P, 2, 2, MEM], offset=scr + 8 * KB2)
        xst = at("xst", [P, 2, 8], offset=scr + 10 * KB2)
        PX = at("PX", [P, 2, 2, S], offset=hn_at)
        cH = at("cH", [P, 5, S], F32R, offset=scr)
        cL = at("cL", [P, 5, S], F32R, offset=scr + 5 * KB2)
        rq = at("rq", [P, S], offset=scr + 10 * KB2)
        QC = at("QC", [P, MLA_HEADS, S], offset=hn_at)
        KC = at("KC", [P, MLA_HEADS, S], offset=act_at)
        VL = at("VL", [P, NB, D], offset=mix_at)
        qpn = at("qpn", [P, 2, S], offset=up)
        qpr = at("qpr", [P, 2, S], offset=up + 2 * KB2)
        oHL = at("oHL", [P, MLA_HEADS, S], F32R, offset=act_at)
        EM = at("EM", [P, 2, NB, S], offset=up)
        assert up + 8 * KB2 <= TOP
        PX2 = at("PX2", [P, 2, NB, S], offset=scr)
        mst = at("mst", [P, 2, 16], offset=scr + 10 * KB2)

        def v(name, i=0):
            return VT[:, VEC[name] + i:VEC[name] + i + 1]

        def c(name, w=P):
            return CT[:, CONST[name]:CONST[name] + w]
        ident, ones, past, future = c("ident"), c("ones"), c("past"), c("future")
        upto, since, twice, neg_future = c("upto"), c("since"), c("twice"), c("neg_future")
        bank = [ctx.enter_context(nc.psum_tensor(f"bank{i}", [P, S], F32)) for i in range(8)]

        loaded = [sem(f"loaded{i}") for i in range(RING)]
        hi_split = sem("hi_split")
        split = sem("split")
        unit_done = sem("unit_done")
        tile_done = sem("tile_done")
        evacuated = [sem(f"evacuated{i}") for i in range(8)]
        tables_in = sem("tables_in")
        vecs_in = sem("vecs_in")
        x_in = [sem(f"x_in{i}") for i in range(KD)]
        mem_in = sem("mem_in")
        sq_ready, sq_used = sem("sq_ready"), sem("sq_used")
        hi_ready, hn_ready = sem("hi_ready"), sem("hn_ready")
        rstd_ready = sem("rstd_ready")
        v_step, a_step = sem("v_step"), sem("a_step")
        out_done = sem("out_done")
        named = {}

        def sig(name):
            if name not in named:
                named[name] = sem(name)
            return named[name]

        def tile_wait(eng, n):
            kind, count = TILE_DONE[n]
            eng.wait_ge(unit_done if kind == "unit" else tile_done, count)

        def gone_wait(eng, n):
            eng.wait_ge(evacuated[BANK[n]], TURN[n] + 1)

        def free(ins, n):
            ins.then_inc(evacuated[BANK[n]], 1)

        def psum(n):
            return bank[BANK[n]]

        NORM = {n: i for i, n in enumerate(NORMS)}
        WIDTH = {n: w for n, _, w in UNITS}
        COUNT = {n: k for n, k, _ in UNITS}
        LAST = {n: UNIT0[n] + k for n, k, _ in UNITS}

        block = ctx.enter_context(nc.Block())

        runs, u = [], 0
        for n, k, w in UNITS:
            if n.startswith("mem_"):
                parts = [("memory", k)]
            elif n in ("ff0_gu0", "pc_in"):
                parts = [("", RING), ("post_norm", k - RING)]
            else:
                parts = [("", k)]
            for kind, k_ in parts:
                if runs and runs[-1][2:] == [w, kind]:
                    runs[-1][1] += k_
                else:
                    runs.append([u, k_, w, kind])
                u += k_

        @block.sync
        def _(sp):
            def load(u, slot, turn, w):
                sp.dma_start(raw[:, slot, 0:w], weights[u, :, 0:w]).then_inc(loaded[slot], 16)

            for u0, n, w, kind in runs:
                i0 = 0
                while i0 < n and (u0 + i0 < RING or (n - i0) % RING):
                    if u0 + i0 >= RING:
                        sp.wait_ge(split, u0 + i0 - RING + 1)
                    load(u0 + i0, (u0 + i0) % RING, 0, w)
                    if u0 + i0 < 2:
                        for c_ in range((u0 + i0) * KD // 2, (u0 + i0 + 1) * KD // 2):
                            sp.dma_start(XT[:, c_, :], x_t[c_ * P:c_ * P + P, :]).then_inc(x_in[c_], 16)
                    i0 += 1
                if i0 < n:
                    with sp.Fori(0, (n - i0) // RING) as i:
                        for j in range(RING):
                            u = u0 + i0 + j
                            sp.wait_ge(split, i * RING + (u - RING + 1))
                            load(i * RING + u, u % RING, 0, w)
            sp.wait_ge(out_done, 16 * KD)

        @block.gpsimd
        def _(pool):
            nc.gpsimd.memset(zero[:, :], 0.0).then_inc(sig("zero_set"), 1)
            pool.wait_ge(sig("zero_set"), 1)
            nothing = zero[:, 0:1]
            skipped = [0]
            posts = [0]

            def post_scale(i):
                pool.wait_ge(rstd_ready, 2 * i + 2)
                for c_ in range(KD):
                    nc.gpsimd.tensor_tensor(MIX[:, c_, :], MIX[:, c_, :], rstd[:, :], ALU.mult)\
                        .then_inc(sig("post_scaled"), 1)

            def split_unit(u, slot, turn, w):
                pool.wait_ge(loaded[slot], turn * 16 + 16)
                nc.gpsimd.tensor_tensor(wH[:, slot, 0:w], raw[:, slot, 0:w], nothing.broadcast_to([P, w]), ALU.add)\
                    .then_inc(hi_split, 1)
                pool.wait_ge(hi_split, u - skipped[0] + 1)
                nc.gpsimd.tensor_tensor(wL[:, slot, 0:w], raw[:, slot, 0:w], wH[:, slot, 0:w].bitcast(F32),
                                        ALU.subtract).then_inc(split, 1)

            for u0, n, w, kind in runs:
                i0 = 0
                if kind == "post_norm":
                    post_scale(posts[0])
                    posts[0] += 1
                if kind == "memory":
                    with pool.Fori(0, n // RING) as i:
                        for j in range(RING):
                            slot = (u0 + j) % RING
                            pool.wait_ge(sig("memory_hi"), i * RING + (j + 1))
                            nc.gpsimd.tensor_tensor(wL[:, slot, 0:w], raw[:, slot, 0:w],
                                                    wH[:, slot, 0:w].bitcast(F32), ALU.subtract).then_inc(split, 1)
                    skipped[0] += n
                    continue
                while i0 < n and (u0 + i0 < RING or (n - i0) % RING):
                    u = u0 + i0
                    if u >= RING:
                        pool.wait_ge(unit_done, u - RING + 1)
                    split_unit(u, u % RING, u // RING, w)
                    i0 += 1
                if i0 < n:
                    with pool.Fori(0, (n - i0) // RING) as i:
                        for j in range(RING):
                            u = u0 + i0 + j
                            pool.wait_ge(unit_done, i * RING + (u - RING + 1))
                            split_unit(i * RING + u, u % RING, i + u // RING, w)

        @block.tensor
        def _(pe):
            mm = nc.tensor.matmul

            def claim(n):
                if TURN[n] > 0:
                    pe.wait_ge(evacuated[BANK[n]], TURN[n])

            def three(out_, aH, aL, bH, bL, first, last):
                mm(out_, aH, bH, start=first, stop=False)
                mm(out_, aH, bL, start=False, stop=False)
                return mm(out_, aL, bH, start=False, stop=last)

            def wait_hn(norm, k):
                pe.wait_ge(hn_ready, KD * NORM[norm] + k + 1)

            def project(name, bH, bL, kd=KD, cols=S, ready=None, after={}):
                for i in range(COUNT[name]):
                    u, n = UNIT0[name] + i, TILE0[name] + i
                    pe.wait_ge(split, u + 1)
                    claim(n)
                    for k in range(kd):
                        if ready and i == 0:
                            ready(k)
                        cut = slice(k * P, k * P + P)
                        last = three(psum(n)[:, 0:cols], wH[:, u % RING, cut], wL[:, u % RING, cut],
                                     bH[:, k, :], bL[:, k, :], k == 0, k == kd - 1)
                    last.then_inc(unit_done, 1)
                    if i in after:
                        after[i]()

            def project_natural(name, aH, aL, kd, blocks, tile0, u0, units, ready=None):
                for i in range(units):
                    u = u0 + i
                    pe.wait_ge(split, u + 1)
                    ks = [k for k in (2 * i, 2 * i + 1) if k < kd]
                    for b in range(blocks):
                        n = tile0 + b
                        if i == 0:
                            claim(n)
                        tok = slice(b * P, b * P + P)
                        for k in ks:
                            cut = slice((k - 2 * i) * S, (k - 2 * i) * S + S)
                            last = three(psum(n)[:, :], aH[:, k, tok], aL[:, k, tok], wH[:, u % RING, cut],
                                         wL[:, u % RING, cut], k == 0, k == kd - 1)
                    last.then_inc(unit_done, 1)

            def row_sums(n, norm, cols=S):
                pe.wait_ge(sq_used, SQ_END[norm])
                claim(n)
                mm(psum(n)[:, 0:cols], ones, ssq[:, 0:cols], start=True, stop=True).then_inc(tile_done, 1)

            def col_sums(n, norm, blocks=NB):
                pe.wait_ge(sq_used, SQ_END[norm])
                claim(n)
                for b in range(blocks):
                    last = mm(psum(n)[:, b:b + 1], ssq[:, b * P:b * P + P], ones[:, 0:1], start=True, stop=True)
                last.then_inc(tile_done, 1)

            def feed_forward(f, norm):
                for t, chunks in enumerate(THIRDS):
                    if t == 0:
                        project(f"ff{f}_gu0", hnH, hnL, ready=lambda k: wait_hn(norm, k),
                                after={1 if f == 0 else 0: lambda: row_sums(TILE0[f"row_sum_f{f}"], norm)})
                    else:
                        project(f"ff{f}_gu{t}", hnH, hnL)
                    base = f * NF + sum(THIRDS[:t])
                    project(f"ff{f}_d{t}", actH, actL, kd=chunks,
                            ready=lambda k: pe.wait_ge(sig("hid_ready"), base + k + 1))

            n, u = TILE0["lr"], UNIT0["lr_gates"]
            pe.wait_ge(split, u + 1)
            claim(n)
            for k in range(KD):
                wait_hn("mix_pre", k)
                cut = slice(k * 48 + 16, k * 48 + 48)
                three(psum(n)[0:32, :], wH[:, u % RING, cut], wL[:, u % RING, cut], hnH[:, k, :], hnL[:, k, :],
                      k == 0, k == KD - 1)
            n = TILE0["gates"]
            claim(n)
            for b in range(NB):
                for k in range(KD):
                    tok = slice(b * P, b * P + P)
                    cut = slice(k * 48, k * 48 + 16)
                    last = three(psum(n)[:, b * 16:b * 16 + 16], hnH[:, k, tok], hnL[:, k, tok],
                                 wH[:, u % RING, cut], wL[:, u % RING, cut], k == 0, k == KD - 1)
            last.then_inc(unit_done, 1)
            pe.wait_ge(tables_in, 16 * 3)
            col_sums(TILE0["col_sum1"], "mix_pre")
            row_sums(TILE0["row_sum1"], "mix_pre")
            project("a_qk", hnH, hnL)
            n = TILE0["cum"]
            pe.wait_ge(sig("logf_ready"), 1)
            claim(n)
            for b in range(NB):
                for d, (heads, others, tri) in enumerate(((slice(0, 4), range(0, b), upto),
                                                          (slice(4, 8), range(b + 1, NB), since))):
                    to = psum(n)[:, b * 8 + 4 * d:b * 8 + 4 * d + 4]
                    for i, q in enumerate(others):
                        mm(to, ones, logf[:, q, heads], start=(i == 0), stop=False)
                    last = mm(to, tri, logf[:, b, heads], start=(len(others) == 0), stop=True)
            last.then_inc(tile_done, 1)
            project("b_qk", hnH, hnL)
            gone_wait(pe, TILE0["lr"])
            for i in range(4):
                n = TILE0["log_a"] + i
                claim(n)
                mm(psum(n)[:, :], W2[:, i // 2, (i % 2) * P:(i % 2) * P + P], lrT[:, :], start=True, stop=True)\
                    .then_inc(tile_done, 1)
            gone_wait(pe, TILE0["cum"])
            for i, src in enumerate((aN, bN)):
                n = TILE0["gate_rows"] + i
                claim(n)
                for b in range(NB):
                    last = nc.tensor.transpose(psum(n)[0:8, b * P:b * P + P], src[:, b, :], ident)
                last.then_inc(tile_done, 1)
            project_natural("a_v", hnH, hnL, KD, NB, TILE0["a_v"], UNIT0["a_v"], 4)
            project_natural("b_v", hnH, hnL, KD, NB, TILE0["b_v"], UNIT0["b_v"], 4)
            project("a_o", hnH, hnL)
            project("b_r", hnH, hnL)

            def score_tiles(h, js):
                rows = slice(64 * (h % 2), 64 * (h % 2) + 64)
                for j in js:
                    n = s_tile(h, j)
                    claim(n)
                    mm(psum(n)[:, :], qkA[rows, 2 + h // 2, j * P:j * P + P], qkA[rows, h // 2, :], start=True,
                       stop=True).then_inc(tile_done, 1)

            def spread_rows(i):
                h, d = i // 2, i % 2
                pick = ident[0:8, h + 4 * d:h + 4 * d + 1].broadcast_to([8, P])
                for name, src in (("max", rowM), ("guard", rowG)):
                    n = TILE0[f"{name}{i}"]
                    claim(n)
                    mm(psum(n)[:, :], pick, src[:, d, :], start=True, stop=True).then_inc(tile_done, 1)

            def weigh(i):
                h, d = i // 2, i % 2
                pe.wait_ge(sig("weights_m"), i + 1)
                for name in ("num", "den"):
                    n = TILE0[f"{name}{i}"]
                    claim(n)
                    for q, j in enumerate(range(NB) if d == 0 else range(NB - 1, -1, -1)):
                        cols = slice(j * P, S) if d == 0 else slice(0, j * P + P)
                        lhs = VA[:, j, h * P:h * P + P] if name == "num" else ones
                        last = mm(psum(n)[:, cols], lhs, PM[:, i % 2, j, cols], start=(q == 0), stop=(q == NB - 1))
                    last.then_inc(tile_done, 1)

            pe.wait_ge(sig("qk_ready"), 4)
            pe.wait_ge(sig("rows_ready"), 1)
            for i in range(9):
                if i < 8:
                    spread_rows(i)
                    if i % 2 == 0:
                        score_tiles(i // 2, (0, 1))
                if i > 0:
                    weigh(i - 1)
                if i < 8 and i % 2 == 0:
                    score_tiles(i // 2, (2, 3))

            def head_sums(name, stage):
                for h in range(4):
                    n = TILE0[name] + h
                    claim(n)
                    pe.wait_ge(sig("head_sq"), 4 * stage + h + 1)
                    mm(psum(n)[:, :], ones, sq[:, h % 2, :], start=True, stop=True).then_inc(tile_done, 1)
            head_sums("norm_a", 0)

            for cc in range(2):
                for lev in range(10):
                    if lev > 0:
                        pe.wait_ge(sig("level_qk"), cc * 9 + lev)
                    for hh in range(2):
                        rows = slice(64 * hh, 64 * hh + 64)
                        q_, k_ = (qkB[rows, 0, cc], qkB[rows, 1, cc]) if lev == 0 else \
                            (qkL[rows, lev % 2, 0], qkL[rows, lev % 2, 1])
                        for half in range(2 if lev == 9 else 1):
                            n = TILE0[f"lev{cc}_{lev}"] + (2 * hh + half if lev == 9 else hh)
                            claim(n)
                            if lev == 9:
                                for j in (2 * half, 2 * half + 1):
                                    last = mm(psum(n)[:, (j % 2) * 256:(j % 2) * 256 + 256], k_[:, j * P:j * P + P],
                                              q_[:, 256 * (1 - half):256 * (1 - half) + 256], start=True, stop=True)
                            else:
                                for j in range(NB):
                                    i = j ^ 1 if lev == 8 else j
                                    last = mm(psum(n)[:, j * P:j * P + P], k_[:, j * P:j * P + P],
                                              q_[:, i * P:i * P + P], start=True, stop=True)
                            last.then_inc(tile_done, 1)
                for hh in range(2):
                    n = TILE0[f"o{cc}"] + hh
                    claim(n)
                    gone_wait(pe, TILE0[f"lev{cc}_7"] + hh)
                    gone_wait(pe, TILE0[f"lev{cc}_8"] + hh)
                    gone_wait(pe, TILE0[f"lev{cc}_9"] + 2 * hh)
                    gone_wait(pe, TILE0[f"lev{cc}_9"] + 2 * hh + 1)
                    val = [VB[:, j, (2 * cc + hh) * P:(2 * cc + hh) * P + P] for j in range(NB)]
                    for j in range(NB):
                        mm(psum(n)[:, j * P:j * P + P], val[j], Pd[:, hh, j, :], start=(j == 0), stop=False)
                    for j in range(NB):
                        mm(psum(n)[:, (j ^ 1) * P:(j ^ 1) * P + P], val[j], P1[:, hh, j, :], start=False, stop=False)
                    for j in range(NB):
                        to = slice(256, 512) if j < 2 else slice(0, 256)
                        last = mm(psum(n)[:, to], val[j], P2[:, hh, j, :], start=False, stop=(j == NB - 1))
                    last.then_inc(tile_done, 1)
            head_sums("norm_b", 1)
            project("w_out", actH, actL, ready=lambda k: pe.wait_ge(sig("y_ready"), k + 1))

            row_sums(TILE0["post0"], "post0")
            feed_forward(0, "ffn_pre")
            row_sums(TILE0["post1"], "post1")

            def cross_attention(l):
                norm = f"xa{l}"
                project(f"xq{l}", hnH, hnL, ready=lambda k: wait_hn(norm, k),
                        after={0: lambda: row_sums(TILE0[f"row_sum_x{l}"], norm)})
                base = TILE0[f"xatt{l}"]

                def scores(h):
                    for pair in range(2):
                        n = xtile(base, "s", h, pair)
                        claim(n)
                        gone_wait(pe, TILE0[f"xq{l}"] + 2 * h + 1)
                        for q in range(2):
                            tok = slice((2 * pair + q) * P, (2 * pair + q) * P + P)
                            for k in range(2):
                                last = mm(psum(n)[:, q * MEM:q * MEM + MEM], qX[:, 2 * h + k, tok],
                                          KT[l][:, 2 * h + k, :], start=(k == 0), stop=(k == 1))
                        last.then_inc(tile_done, 1)

                def turn(h):
                    for pair in range(2):
                        n = xtile(base, "t", h, pair)
                        claim(n)
                        pe.wait_ge(sig("x_probs"), 8 * l + 2 * h + pair + 1)
                        for m in range(2):
                            for q in range(2):
                                last = nc.tensor.transpose(psum(n)[:, m * MEM + q * P:m * MEM + q * P + P],
                                                           EX[:, pair, q, m * P:m * P + P], ident)
                        last.then_inc(tile_done, 1)

                def values(h):
                    gone_wait(pe, xtile(base, "t", h, 1))
                    for f in range(2):
                        n = xtile(base, "o", h, f)
                        claim(n)
                        for m in range(2):
                            last = mm(psum(n)[:, :], VM[l][:, m, h * 256 + f * P:h * 256 + f * P + P],
                                      PX[:, h % 2, m, :], start=(m == 0), stop=(m == 1))
                        last.then_inc(tile_done, 1)
                scores(0)
                for h in range(4):
                    if h < 3:
                        scores(h + 1)
                    if h > 0:
                        values(h - 1)
                    turn(h)
                values(3)
                project(f"xo{l}", actH, actL, ready=lambda k: gone_wait(pe, xtile(base, "o", k // 2, k % 2)))

            project("pc_in", hnH, hnL, ready=lambda k: wait_hn("mix2_0", k),
                    after={1: lambda: row_sums(TILE0["row_sum3"], "mix2_0"),
                           6: lambda: row_sums(TILE0["mem_sums"], "mem", MEM)})
            for l in range(2):
                project(f"mem_k{l}", memH[l], memL[l], cols=MEM, ready=lambda k: wait_hn(f"mem{l}", k))
                for g in range(2):
                    project_natural(f"mem_v{l}", memH[l], memL[l], KD, 2, TILE0[f"mem_v{l}"] + 2 * g,
                                    UNIT0[f"mem_v{l}"] + 4 * g, 4)
                if l == 0:
                    for g in range(4):
                        n = TILE0["pool"] + g
                        pe.wait_ge(sig("pooled"), 4)
                        claim(n)
                        mm(psum(n)[:, :], pwt[:, g, :], pooled[:, g, :], start=True, stop=True).then_inc(tile_done, 1)

            def out_pair(i, half):
                u = UNIT0["pc_out"] + 3 * half + i
                pe.wait_ge(split, u + 1)
                for q in range(2):
                    n = pc_tile(2 * i + q)
                    if half == 0:
                        claim(n)
                    for k in range(4):
                        if i == 0 and q == 0:
                            pe.wait_ge(sig("conv_out" if half else "pool_out"), k + 1)
                        cut = slice((4 * q + k) * P, (4 * q + k) * P + P)
                        last = three(psum(n)[:, :], wH[:, u % RING, cut], wL[:, u % RING, cut], actH[:, 4 * half + k, :],
                                     actL[:, 4 + k, :] if half else poolL[:, k, :], half == 0 and k == 0,
                                     half == 1 and k == 3)
                last.then_inc(unit_done, 1)
            out_pair(0, 0)
            out_pair(1, 0)
            n = TILE0["ln_mean"]
            pe.wait_ge(sig("ln_sum"), 1)
            claim(n)
            mm(psum(n)[:, :], ones, ssq[:, :], start=True, stop=True).then_inc(tile_done, 1)
            out_pair(2, 0)
            row_sums(TILE0["ln_var"], "ln")
            for i in range(3):
                out_pair(i, 1)
            for m in (6, 7):
                n, u = pc_tile(m), UNIT0["pc_out"] + m
                pe.wait_ge(split, u + 1)
                claim(n)
                for k in range(KD):
                    cut = slice(k * P, k * P + P)
                    last = three(psum(n)[:, :], wH[:, u % RING, cut], wL[:, u % RING, cut], actH[:, k, :],
                                 poolL[:, k, :] if k < 4 else actL[:, k, :], k == 0, k == KD - 1)
                last.then_inc(unit_done, 1)
            cross_attention(0)
            feed_forward(1, "ffn2_0")

            n, u = TILE0["k_pe"], UNIT0["k_pe"]
            pe.wait_ge(split, u + 1)
            claim(n)
            for b in range(NB):
                for k in range(KD):
                    wait_hn("mix2_1", k)
                    tok = slice(b * P, b * P + P)
                    cut = slice(k * 32, k * 32 + 32)
                    last = three(psum(n)[:, b * 32:b * 32 + 32], hnH[:, k, tok], hnL[:, k, tok], wH[:, u % RING, cut],
                                 wL[:, u % RING, cut], k == 0, k == KD - 1)
            last.then_inc(unit_done, 1)
            row_sums(TILE0["row_sum6"], "mix2_1")
            col_sums(TILE0["col_sum6"], "mix2_1")
            project("w_dq", hnH, hnL)
            for i, name in enumerate(("q_sum", "kv_sum")):
                n = TILE0[name]
                pe.wait_ge(sig("lora_added"), (3, 5)[i])
                claim(n)
                mm(psum(n)[:, :], ones, sq[:, i, :], start=True, stop=True).then_inc(tile_done, 1)
                claim(n + 1)
                for b in range(NB):
                    last = mm(psum(n + 1)[:, b:b + 1], sq[:, i, b * P:b * P + P], ones[:, 0:1], start=True, stop=True)
                last.then_inc(tile_done, 1)

            def turn_positions(b):
                n = turn_tile(b)
                pe.wait_ge(sig("q_rotated"), b + 1)
                claim(n)
                for g in range(4):
                    last = nc.tensor.transpose(psum(n)[:, g * P:g * P + P], qpr[:, b % 2, g * P:g * P + P], ident)
                last.then_inc(tile_done, 1)

            pe.wait_ge(sig("c_ready"), 5)
            for name, per, kd, c0 in (("q_nope", 2, 3, 0), ("q_pe", 0, 3, 0), ("k_nope", 4, 2, 3), ("mla_v", 0, 2, 3)):
                if name == "q_pe":
                    project_natural(name, cH, cL, kd, NB, TILE0[name], UNIT0[name], 2)
                    continue
                if name == "mla_v":
                    n = TILE0["k_turn"]
                    pe.wait_ge(sig("k_rotated"), 1)
                    claim(n)
                    for b in range(NB):
                        last = nc.tensor.transpose(psum(n)[0:32, b * P:b * P + P], kpr[:, b, :], ident)
                    last.then_inc(tile_done, 1)
                    turn_positions(0)
                    turn_positions(1)
                    for g in range(2):
                        project_natural(name, cH[:, c0:c0 + 2, :], cL[:, c0:c0 + 2, :], kd, NB, TILE0[name] + 4 * g,
                                        UNIT0[name] + g, 1)
                    continue
                for i in range(COUNT[name]):
                    u = UNIT0[name] + i
                    pe.wait_ge(split, u + 1)
                    for q in range(per):
                        n = TILE0[name] + per * i + q
                        claim(n)
                        for k in range(kd):
                            cut = slice((q * kd + k) * P, (q * kd + k) * P + P)
                            last = three(psum(n)[:, :], wH[:, u % RING, cut], wL[:, u % RING, cut],
                                         cH[:, c0 + k, :], cL[:, c0 + k, :], k == 0, k == kd - 1)
                    last.then_inc(unit_done, 1)
            turn_positions(2)
            turn_positions(3)
            gone_wait(pe, TILE0["mla_v"] + 7)
            gone_wait(pe, turn_tile(2))
            gone_wait(pe, turn_tile(3))

            def att_scores(h):
                for b in range(NB):
                    n = mtile("s", h, b)
                    claim(n)
                    w = (b + 1) * P
                    mm(psum(n)[:, 0:w], QC[0:96, h, b * P:b * P + P], KC[0:96, h, 0:w], start=True, stop=False)
                    mm(psum(n)[:, b * P:w], identR[:, :], neg_futureR[:, :], start=False, stop=True).then_inc(tile_done, 1)

            def att_turn(h):
                for b in range(NB):
                    n = mtile("t", h, b)
                    claim(n)
                    pe.wait_ge(sig("m_probs"), 4 * h + b + 1)
                    for j in range(b + 1):
                        last = nc.tensor.transpose(psum(n)[:, j * P:j * P + P], EM[:, h % 2, b, j * P:j * P + P], ident)
                    last.then_inc(tile_done, 1)

            def att_values(h):
                n = mtile("o", h, 0)
                claim(n)
                for b in (0, 1, 2, 3):
                    gone_wait(pe, mtile("t", h, b))
                rows = slice(64 * (h % 2), 64 * (h % 2) + 64)
                for j in range(NB):
                    last = mm(psum(n)[rows, j * P:], VL[:, j, h * 64:h * 64 + 64], PX2[:, h % 2, j, j * P:],
                              start=(j == 0), stop=(j == NB - 1))
                last.then_inc(tile_done, 1)

            pe.wait_ge(sig("mask_ready"), 2)
            for i in range(MLA_HEADS + 2):
                if i < MLA_HEADS:
                    att_scores(i)
                if i >= 2:
                    att_values(i - 2)
                if 1 <= i <= MLA_HEADS:
                    att_turn(i - 1)
            oH_, oL_ = (oHL[:, :, :].rearrange("p (a two) s -> p a two s", two=2)[:, :, i, :] for i in range(2))
            project("mla_o", oH_, oL_, ready=lambda k: gone_wait(pe, mtile("o", 2 * k + 1, 0)))
            cross_attention(1)
            feed_forward(2, "ffn2_1")
            row_sums(TILE0["row_sum_end"], "final")

        @block.scalar
        def _(act):
            step, nsq = [0], [0]
            run = nc.scalar.activation

            def link(ins):
                step[0] += 1
                ins.then_inc(a_step, 1)
                act.wait_ge(a_step, step[0])

            def square(src, cols=S, dst=None):
                if dst is None:
                    if nsq[0] >= 2:
                        act.wait_ge(sq_used, nsq[0] - 1)
                    dst = sq[:, nsq[0] % 2, 0:cols]
                run(dst, src, ACT.Square).then_inc(sq_ready, 1)
                nsq[0] += 1

            def high(dst, src, gain):
                run(dst, src, ACT.Copy, scale=gain).then_inc(hi_ready, 1)

            def norm_chunk(gain, c_):
                square(XT[:, c_, :])
                high(hnH[:, c_, :], XT[:, c_, :], v(gain, c_))

            def inverse_root(n, dst, tmp, width, cols=S, signal=None, rows=P):
                nc.scalar.preload_act_table_set("natural_log_exp_and_others")
                tile_wait(act, n)
                free(run(tmp, psum(n)[0:rows, 0:cols], ACT.Ln, bias=v("eps"), scale=1.0 / width), n)
                gone_wait(act, n)
                run(dst, tmp, ACT.Exp, scale=-0.5).then_inc(signal, 1)

            def row_root(n, width=D):
                inverse_root(n, rstd[:, :], lnb[:, :], width, signal=rstd_ready)

            def feed_forward(f):
                base = TILE0[f"row_sum_f{f}"]
                row_root(base)
                for t, chunks in enumerate(THIRDS):
                    for j in range(chunks):
                        q = sum(THIRDS[:t]) + j
                        i, s_ = f * NF + q, q % 2
                        g = 4 + i
                        gone_wait(act, TILE0[f"ff{f}_gu{t}"] + 2 * j)
                        mid = 2 if f == 0 else 1
                        run(cva[:, s_, :], gpad[:, s_, mid:mid + S], ACT.Identity, bias=v(f"fconv_b{f}", q),
                            scale=v(f"fconv_w{f}", 3 * q + 1)).then_inc(sig("conv_mid"), 1)
                        act.wait_ge(sig("conv_done"), g + 1)
                        run(cva[:, s_, :], cva[:, s_, :], ACT.Gelu_apprx_tanh if f == 0 else ACT.Silu)\
                            .then_inc(sig("gate_done"), 1)
                        if j == 0 and t > 0:
                            act.wait_ge(unit_done, LAST[f"ff{f}_d{t - 1}"])
                        act.wait_ge(sig("hval_ready"), i + 1)
                        run(actH[:, j, :], hval[:, s_, :], ACT.Copy).then_inc(sig("hid_hi"), 1)
                    if t == 0 and f == 0:
                        for m in range(KD):
                            n = TILE0["ff0_d0"] + m
                            tile_wait(act, n)
                            free(run(MIX[:, m, :], psum(n)[:, :], ACT.Copy), n)

            act.dma_start(VT[:, :], vecs).then_inc(vecs_in, 16)
            act.dma_start(CT[:, :], consts).then_inc(tables_in, 16)
            act.dma_start(MASK[:, :, :], masks).then_inc(tables_in, 16)
            act.dma_start(W2[:, :, :], gla_w2).then_inc(tables_in, 16)
            act.wait_ge(vecs_in, 16)

            for c_ in range(KD):
                act.wait_ge(x_in[c_], 16)
                norm_chunk("mix_pre", c_)
            inverse_root(TILE0["col_sum1"], rcol[:, :], lncol[:, :], D, NB, sig("rcol_ready"))
            row_root(TILE0["row_sum1"])
            act.wait_ge(sig("gates_in"), 1)
            link(run(absf[:, :, :], gate_in[:, :, 8:16], ACT.Abs))
            link(run(lnf[:, :, :], absf[:, :, :], ACT.Exp, scale=-1.0))
            run(lnf[:, :, :], lnf[:, :, :], ACT.Ln, bias=v("one")).then_inc(sig("softplus_f"), 1)
            for i in range(4):
                gone_wait(act, TILE0["a_qk"] + i)
                run(cvm[:, i % 2, :], cpad[:, i % 2, 2:2 + S], ACT.Identity, bias=v("mconv_b", i),
                    scale=v("mconv_w", 3 * i + 1)).then_inc(sig("conv_mid"), 1)
                act.wait_ge(sig("conv_done"), i + 1)
                run(qkA[:, i, :], cvm[:, i % 2, :], ACT.Silu).then_inc(sig("qk_ready"), 1)
            for i in range(4):
                n = TILE0["log_a"] + i
                tile_wait(act, n)
                if i > 0:
                    act.wait_ge(sig("log_a_used"), i)
                free(run(zb[:, :], psum(n)[:, :], ACT.Identity, bias=v("gla_b", i)), n)
                gone_wait(act, n)
                link(run(zc[:, :], zb[:, :], ACT.Abs))
                link(run(zc[:, :], zc[:, :], ACT.Exp, scale=-1.0))
                run(zc[:, :], zc[:, :], ACT.Ln, bias=v("one")).then_inc(sig("softplus_a"), 1)
            for i, dst in enumerate((rowA, rowB)):
                n = TILE0["gate_rows"] + i
                tile_wait(act, n)
                free(run(dst[:, :], psum(n)[0:8, :], ACT.Copy), n)
            for name, dst in (("a_v", VA), ("b_v", VB)):
                for b in range(NB):
                    n = TILE0[name] + b
                    tile_wait(act, n)
                    free(run(dst[:, b, :], psum(n)[:, :], ACT.Copy, scale=rcol[:, b:b + 1]), n)
            for i in range(4):
                gone_wait(act, TILE0["a_o"] + i)
                run(gateO[:, i, :], gateO[:, i, :], ACT.Sigmoid).then_inc(sig("gate_act"), 1)
            for i in range(4):
                gone_wait(act, TILE0["b_r"] + i)
                run(gateR[:, i, :], gateR[:, i, :], ACT.Silu).then_inc(sig("gate_act"), 1)

            nc.scalar.preload_act_table_set("natural_log_exp_and_others")

            def take_scores(h, js):
                for j in js:
                    n = s_tile(h, j)
                    tile_wait(act, n)
                    free(run(ST[:, j, :], psum(n)[:, :], ACT.Copy, scale=0.125), n)

            def invert_m(i):
                gone_wait(act, TILE0[f"den{i}"])
                link(run(den[:, i % 2, :], den[:, i % 2, :], ACT.Ln))
                run(den[:, i % 2, :], den[:, i % 2, :], ACT.Exp, scale=-1.0).then_inc(sig("den_inverse"), 1)

            for i in range(8):
                h, d = i // 2, i % 2
                if i > 0:
                    act.wait_ge(sig("weights_m"), i)
                if d == 0:
                    take_scores(h, (0, 1))
                n = TILE0[f"max{i}"]
                act.wait_ge(sig("masked"), i + 1)
                for j in (range(NB - 1, -1, -1) if d == 0 else range(NB)):
                    diag = slice(j * P, j * P + P)
                    rest = slice(j * P + P, S) if d == 0 else slice(0, j * P)
                    own = aN[:, j, h + 4 * d:h + 4 * d + 1]
                    run(DT[:, j, diag], tmpM[:, diag], ACT.Exp, bias=own, scale=-1.0)
                    if rest.start < rest.stop:
                        last = run(DT[:, j, rest], psum(n)[:, rest], ACT.Exp, bias=own, scale=-1.0)
                free(last, n)
                if d == 0:
                    take_scores(h, (2, 3))
                n = TILE0[f"guard{i}"]
                tile_wait(act, n)
                if i >= 2:
                    gone_wait(act, TILE0[f"den{i - 2}"])
                free(run(guard[:, i % 2, :], psum(n)[:, :], ACT.Exp, scale=-1.0), n)
                if i >= 2:
                    invert_m(i - 2)
            invert_m(6)
            invert_m(7)

            def head_norms(name, stage, chunk0):
                def finish(h):
                    act.wait_ge(sig("head_out"), 4 * stage + h + 1)
                    run(actH[:, chunk0 + h, :], ht[:, h % 2, :], ACT.Copy).then_inc(sig("y_hi"), 1)
                for h in range(4):
                    act.wait_ge(sig("head_ready"), 4 * stage + h + 1)
                    if h >= 2:
                        tile_wait(act, TILE0[name] + h - 2)
                    run(sq[:, h % 2, :], Y[:, h, :], ACT.Square).then_inc(sig("head_sq"), 1)
                    if h >= 2:
                        act.wait_ge(sig("head_out"), 4 * stage + h - 1)
                    inverse_root(TILE0[name] + h, hr[:, h % 2, :], lnb[:, :], P, signal=sig("head_root"))
                    if h >= 1:
                        finish(h - 1)
                finish(3)
            head_norms("norm_a", 0, 0)

            for cc in range(2):
                for lev in range(1, 10):
                    i = cc * 9 + lev
                    act.wait_ge(sig("level_arg"), i)
                    run(arg[:, lev % 2, :, :], arg[:, lev % 2, :, :], ACT.Exp, scale=1.0 / 16)\
                        .then_inc(sig("level_exp"), 1)
                if cc > 0:
                    tile_wait(act, TILE0[f"o{cc - 1}"] + 1)
                for hh in range(2):
                    n = TILE0[f"lev{cc}_8"] + hh
                    tile_wait(act, n)
                    free(run(P1[:, hh, :, :], psum(n)[:, :], ACT.Copy), n)
                for q in range(4):
                    n = TILE0[f"lev{cc}_9"] + q
                    tile_wait(act, n)
                    free(run(P2[:, q // 2, 2 * (q % 2):2 * (q % 2) + 2, :], psum(n)[:, :], ACT.Copy), n)
            head_norms("norm_b", 1, 4)

            def post_chunk(c_):
                square(MIX[:, c_, :])
            for m in range(KD):
                n = TILE0["w_out"] + m
                tile_wait(act, n)
                free(run(MIX[:, m, :], psum(n)[:, :], ACT.Copy), n)
                gone_wait(act, n)
                post_chunk(m)
            row_root(TILE0["post0"])
            for c_ in range(KD):
                act.wait_ge(sig("x_new"), c_ + 1)
                square(XT[:, c_, :], dst=MIX[:, c_, :])
                high(hnH[:, c_, :], XT[:, c_, :], v("ffn_pre", c_))
            act.dma_start(memT[:, :, :], mem_t.rearrange("(k p) m -> p k m", p=P)).then_inc(mem_in, 16)
            act.dma_start(posI[:, :], positions).then_inc(mem_in, 16)
            act.dma_start(pwt[:, :, :], pool_w.rearrange("g c d -> c g d")).then_inc(mem_in, 16)
            feed_forward(0)
            for m in range(KD):
                gone_wait(act, TILE0["ff0_d2"] + m)
                post_chunk(m)
            row_root(TILE0["post1"])
            for c_ in range(KD):
                act.wait_ge(sig("x_new"), KD + c_ + 1)
                square(XT[:, c_, :], dst=MIX[:, c_, :])
                high(hnH[:, c_, :], XT[:, c_, :], v("mix2_0", c_))

            act.wait_ge(mem_in, 48)
            row_root(TILE0["row_sum3"])
            for c_ in range(KD):
                square(memT[:, c_, :], MEM)

            def memory_high(i):
                u = UNIT0["mem_k0"] + i
                act.wait_ge(loaded[u % RING], 16 * (u // RING + 1))
                act.wait_ge(unit_done, u - RING + 1)
                run(wH[:, u % RING, :], raw[:, u % RING, :], ACT.Copy).then_inc(sig("memory_hi"), 1)
            for i in range(4):
                gone_wait(act, TILE0["pc_in"] + 8 + i)
                run(sigb[:, i % 2, :], sigb[:, i % 2, :], ACT.Sigmoid).then_inc(sig("glu_gate"), 1)
                if i == 0:
                    inverse_root(TILE0["mem_sums"], rmem[:, :], lnb[:, 0:MEM], D, MEM, sig("mem_root"))
                if i >= 2:
                    for c_ in range(KD):
                        act.wait_ge(sig("mem_normed"), c_ + 1)
                        high(memH[i - 2][:, c_, :], memT[:, c_, :], v(f"mem{i - 2}", c_))
                memory_high(i)
            def pool_take(g):
                n = TILE0["pool"] + g
                act.wait_ge(unit_done, LAST["mem_v0"])
                tile_wait(act, n)
                if g >= 2:
                    act.wait_ge(sig("pool_out"), g - 1)
                free(run(ybuf[:, g % 2, :], psum(n)[:, :], ACT.Copy, scale=v("pool_scale", g)), n)
                gone_wait(act, n)
                run(actH[:, g, :], ybuf[:, g % 2, :], ACT.Copy).then_inc(sig("pool_hi"), 1)

            def memory_take(i):
                l, i = i // 16, i % 16
                if i < KD:
                    n = TILE0[f"mem_k{l}"] + i
                    tile_wait(act, n)
                    free(run(KT[l][:, i, :], psum(n)[:, 0:MEM], ACT.Copy), n)
                elif i % 4 == 3:
                    half = (i - KD) // 4
                    for b in range(2):
                        n = TILE0[f"mem_v{l}"] + 2 * half + b
                        tile_wait(act, n)
                        free(run(VM[l][:, b, half * S:half * S + S], psum(n)[:, :], ACT.Copy), n)
            for i in range(32):
                memory_take(i)
                if i in (16, 18, 20, 22):
                    pool_take((i - 16) // 2)
                if i + RING < 32:
                    memory_high(i + RING)
            act.wait_ge(unit_done, LAST["mem_v1"])

            for c_ in range(4):
                act.wait_ge(sig("centred"), c_ + 1)
                square(cvb[:, c_, :])
            row_root(TILE0["ln_var"], S)
            for c_ in range(4):
                act.wait_ge(sig("scaled"), c_ + 1)
                if c_ >= 2:
                    act.wait_ge(sig("conv_out"), c_ - 1)
                link(run(ybuf[:, c_ % 2, :], cvb[:, c_, :], ACT.Silu, bias=v("ln_b", c_), scale=v("ln_g", c_)))
                run(actH[:, 4 + c_, :], ybuf[:, c_ % 2, :], ACT.Copy).then_inc(sig("conv_hi"), 1)
            for c_ in range(KD):
                gone_wait(act, pc_tile(c_))
                norm_chunk("xa0", c_)

            def cross_attention(l, next_norm):
                base = TILE0[f"xatt{l}"]
                row_root(TILE0[f"row_sum_x{l}"])

                def rows(h):
                    for pair in range(2):
                        n = xtile(base, "t", h, pair)
                        tile_wait(act, n)
                        if h >= 2:
                            tile_wait(act, xtile(base, "o", h - 2, 1))
                        free(run(PX[:, h % 2, :, pair * MEM:pair * MEM + MEM],
                                 psum(n)[:, :].rearrange("p (m q) -> p m q", m=2), ACT.Copy), n)

                def output_high(h):
                    for f in range(2):
                        tile_wait(act, xtile(base, "o", h, f))
                        run(actH[:, 2 * h + f, :], psum(xtile(base, "o", h, f))[:, :], ACT.Copy)\
                            .then_inc(sig("x_hi"), 1)
                for h in range(4):
                    for pair in range(2):
                        n = xtile(base, "s", h, pair)
                        act.wait_ge(sig("x_max"), 8 * l + 2 * h + pair + 1)
                        if h >= 1:
                            tile_wait(act, xtile(base, "t", h - 1, pair))
                        for q in range(2):
                            last = run(EX[:, pair, q, :], psum(n)[:, q * MEM:q * MEM + MEM], ACT.Exp,
                                       bias=xst[:, pair, 2 + q:3 + q], scale=1.0 / 16,
                                       accum_out=xst[:, pair, 4 + q:5 + q])
                        free(last, n)
                    if h >= 2:
                        output_high(h - 2)
                    if h >= 1:
                        rows(h - 1)
                output_high(2)
                rows(3)
                output_high(3)
                for c_ in range(KD):
                    gone_wait(act, TILE0[f"xo{l}"] + c_)
                    norm_chunk(next_norm, c_)

            cross_attention(0, "ffn2_0")
            feed_forward(1)
            for c_ in range(KD):
                gone_wait(act, TILE0["ff1_d2"] + c_)
                norm_chunk("mix2_1", c_)

            act.wait_ge(sig("angle"), 1)
            run(sinT[:, :, :], angB[:, :, :], ACT.Sin).then_inc(sig("turned"), 1)
            act.wait_ge(sig("angle"), 2)
            run(cosT[:, :, :], angC[:, :, :], ACT.Sin).then_inc(sig("turned"), 1)
            row_root(TILE0["row_sum6"])
            inverse_root(TILE0["col_sum6"], rcol[:, :], lncol[:, :], D, NB, sig("rcol_ready"))
            act.wait_ge(sig("rcol_ready"), 2)
            n = TILE0["k_pe"]
            tile_wait(act, n)
            for b in range(NB):
                last = run(kpn[:, b, :], psum(n)[:, b * 32:b * 32 + 32], ACT.Copy, scale=rcol[:, b:b + 1])
            free(last, n)
            for i in range(5):
                gone_wait(act, TILE0["w_dq"] + i)
                if i >= 2:
                    act.wait_ge(sig("lora_added"), i - 1)
                run(qpr[:, i % 2, :], qpn[:, i % 2, :], ACT.Square).then_inc(sig("lora_sq"), 1)
                run(cH[:, i, :], qpn[:, i % 2, :], ACT.Copy, scale=v("q_norm", i) if i < 3 else v("kv_norm", i - 3))\
                    .then_inc(sig("c_hi"), 1)
            inverse_root(TILE0["q_sum"], rq[:, :], lnb[:, :], 384, signal=sig("lora_root"))
            inverse_root(TILE0["q_sum"] + 1, rcq[:, 0:4], lncol[:, :], 384, NB, sig("lora_root"))
            inverse_root(TILE0["kv_sum"], rstd[:, :], lnb[:, :], 256, signal=rstd_ready)
            inverse_root(TILE0["kv_sum"] + 1, rcq[:, 4:8], lncol[:, :], 256, NB, sig("lora_root"))
            act.wait_ge(sig("lora_root"), 3)
            for b in range(NB):
                n = TILE0["q_pe"] + b
                tile_wait(act, n)
                if b >= 2:
                    act.wait_ge(sig("q_rotated"), b - 1)
                else:
                    act.wait_ge(sig("c_ready"), 5)
                free(run(qpn[:, b % 2, :], psum(n)[:, :], ACT.Copy, scale=rcq[:, b:b + 1]), n)

            def position_rows(b):
                n = turn_tile(b)
                tile_wait(act, n)
                for j in range(4):
                    last = run(QC[64:96, j:MLA_HEADS:4, b * P:b * P + P],
                               psum(n)[32 * j:32 * j + 32, :].rearrange("p (g t) -> p g t", g=4), ACT.Copy)
                free(last, n)
            n = TILE0["k_turn"]
            tile_wait(act, n)
            run(KC[64:96, 8:16, :], psum(n)[0:32, :].unsqueeze(1).broadcast_to([32, 8, S]), ACT.Copy)\
                .then_inc(sig("k_rows"), 1)
            for b in range(2):
                position_rows(b)
            for i in range(8):
                n = TILE0["mla_v"] + i
                tile_wait(act, n)
                b = i % 4
                free(run(VL[:, b, (i // 4) * S:(i // 4) * S + S], psum(n)[:, :], ACT.Copy, scale=rcq[:, 4 + b:5 + b]), n)
            position_rows(2)

            scale = (64 + 32) ** -0.5

            def att_rows(h):
                for b in (0, 2):
                    n = mtile("t", h, b)
                    tile_wait(act, n)
                    if h >= 2:
                        tile_wait(act, mtile("o", h - 2, 0))
                    free(run(PX2[:, h % 2, 0:b + 1, b * P:b * P + P],
                             psum(n)[:, 0:(b + 1) * P].rearrange("p (j q) -> p j q", q=P), ACT.Copy), n)

            def att_high(h):
                n = mtile("o", h, 0)
                tile_wait(act, n)
                rows = slice(64 * (h % 2), 64 * (h % 2) + 64)
                run(oHL[rows, h // 2 * 2, :], psum(n)[rows, :], ACT.Copy).then_inc(sig("m_hi"), 1)

            for i in range(MLA_HEADS):
                act.wait_ge(sig("m_max"), i + 1)
                for b in range(NB):
                    n = mtile("s", i, b)
                    if i >= 2:
                        tile_wait(act, mtile("t", i - 2, b))
                    w = (b + 1) * P
                    free(run(EM[:, i % 2, b, 0:w], psum(n)[:, 0:w], ACT.Exp, bias=mst[:, i % 2, 4 + b:5 + b], scale=scale,
                             accum_out=mst[:, i % 2, 8 + b:9 + b]), n)
                if i >= 2:
                    att_high(i - 2)
                if i >= 1:
                    att_rows(i - 1)
            att_high(MLA_HEADS - 2)
            att_rows(MLA_HEADS - 1)
            att_high(MLA_HEADS - 1)
            for c_ in range(KD):
                gone_wait(act, TILE0["mla_o"] + c_)
                norm_chunk("xa1", c_)
            cross_attention(1, "ffn2_1")
            feed_forward(2)
            for c_ in range(KD):
                gone_wait(act, TILE0["ff2_d2"] + c_)
                square(XT[:, c_, :])
            row_root(TILE0["row_sum_end"])
            for c_ in range(KD):
                act.wait_ge(sig("final"), c_ + 1)
                act.dma_start(out[c_ * P:c_ * P + P, :], MIX[:, c_, :]).then_inc(out_done, 16)

        @block.vector
        def _(dve):
            step, nsq, nhn, nroot, nconv, posts = [0], [0], [0], [0], [0], [0]
            tt, ts, stt = nc.vector.tensor_tensor, nc.vector.tensor_scalar, nc.vector.scalar_tensor_tensor

            def link(ins):
                step[0] += 1
                ins.then_inc(v_step, 1)
                dve.wait_ge(v_step, step[0])

            def add_squares(first, cols=S, src=None):
                dve.wait_ge(sq_ready, nsq[0] + 1)
                s_ = sq[:, nsq[0] % 2, 0:cols] if src is None else src
                if first:
                    ins = nc.vector.tensor_copy(ssq[:, 0:cols], s_)
                else:
                    ins = tt(ssq[:, 0:cols], ssq[:, 0:cols], s_, ALU.add)
                ins.then_inc(sq_used, 1)
                nsq[0] += 1
                dve.wait_ge(sq_used, nsq[0])

            def low(dst, src, gain, hi):
                dve.wait_ge(hi_ready, nhn[0] + 1)
                stt(dst, src, gain, hi.bitcast(F32), ALU.mult, ALU.subtract).then_inc(hn_ready, 1)
                nhn[0] += 1

            def norm_chunk(gain, c_):
                add_squares(c_ == 0)
                if gain != "final":
                    low(hnL[:, c_, :], XT[:, c_, :], v(gain, c_), hnH[:, c_, :])

            def root_wait():
                nroot[0] += 1
                dve.wait_ge(rstd_ready, nroot[0])

            def scaled(dst, n, rows=slice(0, P)):
                tile_wait(dve, n)
                free(tt(dst, psum(n)[rows, :], rstd[rows, :], ALU.mult), n)

            def convolve(pad, acc, left, right, w, q):
                nconv[0] += 1
                dve.wait_ge(sig("conv_mid"), nconv[0])
                link(stt(acc, pad[:, left:left + S], v(w, 3 * q), acc, ALU.mult, ALU.add))
                stt(acc, pad[:, right:right + S], v(w, 3 * q + 2), acc, ALU.mult, ALU.add).then_inc(sig("conv_done"), 1)

            def norm_next(f, next_norm, c_):
                if f == 0:
                    add_squares(c_ == 0)
                else:
                    norm_chunk(next_norm, c_)

            def feed_forward(f, next_norm):
                root_wait()
                left, right = (1, 3) if f == 0 else (0, 2)
                for s_ in range(2):
                    nc.vector.memset(gpad[:, s_, 0:2], 0.0)
                    link(nc.vector.memset(gpad[:, s_, 2 + S:4 + S], 0.0))
                for t, chunks in enumerate(THIRDS):
                    for j in range(chunks):
                        q = sum(THIRDS[:t]) + j
                        i, s_ = f * NF + q, q % 2
                        n = TILE0[f"ff{f}_gu{t}"] + 2 * j
                        scaled(gpad[:, s_, 2:2 + S], n)
                        scaled(ups[:, s_, :], n + 1)
                        convolve(gpad[:, s_, :], cva[:, s_, :], left, right, f"fconv_w{f}", q)
                        dve.wait_ge(sig("gate_done"), i + 1)
                        tt(hval[:, s_, :], cva[:, s_, :], ups[:, s_, :], ALU.mult).then_inc(sig("hval_ready"), 1)
                        dve.wait_ge(sig("hid_hi"), i + 1)
                        tt(actL[:, j, :], hval[:, s_, :], actH[:, j, :].bitcast(F32), ALU.subtract)\
                            .then_inc(sig("hid_ready"), 1)
                    acc = MIX if f == 0 else XT
                    for m in range(KD):
                        n = TILE0[f"ff{f}_d{t}"] + m
                        if f == 0 and t == 0:
                            continue
                        tile_wait(dve, n)
                        if f == 0 and t == 1:
                            gone_wait(dve, TILE0["ff0_d0"] + m)
                        free(tt(acc[:, m, :], psum(n)[:, :], acc[:, m, :], ALU.add), n)
                        if t == 2 and m > 0:
                            norm_next(f, next_norm, m - 1)
                norm_next(f, next_norm, KD - 1)

            def post_norm(gain, next_norm):
                root_wait()
                for c_ in range(KD):
                    posts[0] += 1
                    dve.wait_ge(sig("post_scaled"), posts[0])
                    stt(XT[:, c_, :], MIX[:, c_, :], v(gain, c_), XT[:, c_, :], ALU.mult, ALU.add)\
                        .then_inc(sig("x_new"), 1)
                    if c_ > 0:
                        low(hnL[:, c_ - 1, :], XT[:, c_ - 1, :], v(next_norm, c_ - 1), hnH[:, c_ - 1, :])
                low(hnL[:, KD - 1, :], XT[:, KD - 1, :], v(next_norm, KD - 1), hnH[:, KD - 1, :])
                for c_ in range(KD):
                    add_squares(c_ == 0, src=MIX[:, c_, :])

            link(nc.vector.memset(ones512[:, :], 1.0))
            for s_ in range(2):
                link(nc.vector.memset(cpad[:, s_, 0:2], 0.0))
                link(nc.vector.memset(cpad[:, s_, 2 + S:4 + S], 0.0))
            link(nc.vector.memset(cumF[:, :, 0:1], 0.0))
            dve.wait_ge(vecs_in, 16)
            for c_ in range(KD):
                dve.wait_ge(x_in[c_], 16)
                norm_chunk("mix_pre", c_)
            dve.wait_ge(tables_in, 16 * 3)
            nc.vector.tensor_copy(identR[:, :], ident).then_inc(sig("mask_ready"), 1)
            nc.vector.tensor_copy(neg_futureR[:, :], neg_future).then_inc(sig("mask_ready"), 1)
            dve.wait_ge(sig("rcol_ready"), 1)
            n = TILE0["gates"]
            tile_wait(dve, n)
            for b in range(NB):
                last = stt(gate_in[:, b, :], psum(n)[:, b * 16:b * 16 + 16], rcol[:, b:b + 1],
                           VT[:, VEC["gate_b"]:VEC["gate_b"] + 16], ALU.mult, ALU.add)
            free(last, n)
            gone_wait(dve, n)
            nc.vector.tensor_copy(bN[:, :, :], gate_in[:, :, 0:8]).then_inc(sig("gates_in"), 1)
            root_wait()
            scaled(lrT[:, :], TILE0["lr"], slice(0, 32))
            gone_wait(dve, TILE0["lr"])
            dve.wait_ge(sig("softplus_f"), 1)
            stt(logf[:, :, :], gate_in[:, :, 8:16], 0.0, lnf[:, :, :], ALU.min, ALU.subtract)\
                .then_inc(sig("logf_ready"), 1)
            for i in range(4):
                n = TILE0["a_qk"] + i
                scaled(cpad[:, i % 2, 2:2 + S], n)
                convolve(cpad[:, i % 2, :], cvm[:, i % 2, :], 1, 3, "mconv_w", i)
            n = TILE0["cum"]
            tile_wait(dve, n)
            link(nc.vector.tensor_copy(bN[:, :, :], psum(n)[:, 0:32].rearrange("p (b h) -> p b h", b=NB)))
            free(tt(aN[:, :, :], gate_in[:, :, 0:8], bN[:, :, :], ALU.subtract), n)
            for i in range(4):
                n = TILE0["b_qk"] + i
                tile_wait(dve, n)
                free(stt(qkB[:, i // 2, i % 2, :], psum(n)[:, :], 0.125 if i < 2 else 1.0, rstd[:, :], ALU.mult,
                         ALU.mult), n)
            for i in range(4):
                dve.wait_ge(sig("softplus_a"), i + 1)
                stt(zc[:, :], zb[:, :], 0.0, zc[:, :], ALU.min, ALU.subtract).then_inc(sig("log_a_made"), 1)
                dve.wait_ge(sig("log_a_made"), i + 1)
                nc.vector.tensor_tensor_scan(cumF[:, i, 1:1 + S], ones512[:, :], zc[:, :], 0.0, ALU.mult, ALU.add)\
                    .then_inc(sig("log_a_used"), 1)
            for i in range(2):
                gone_wait(dve, TILE0["gate_rows"] + i)
            scan = nc.vector.tensor_tensor_scan
            link(scan(rowM[:, 0, :], rowA[:, :], rowA[:, :], 0.0, ALU.max, ALU.max))
            link(scan(rowM[:, 1, ::-1], rowA[:, ::-1], rowA[:, ::-1], 0.0, ALU.max, ALU.max))
            tt(rowG[:, :, :], rowM[:, :, :], rowB[:, :].unsqueeze(1).broadcast_to([8, 2, S]), ALU.add)\
                .then_inc(sig("rows_ready"), 1)
            for i in range(4):
                scaled(gateO[:, i, :], TILE0["a_o"] + i)
            for i in range(4):
                scaled(gateR[:, i, :], TILE0["b_r"] + i)

            def mask_m(i):
                n = TILE0[f"max{i}"]
                tile_wait(dve, n)
                mask = past if i % 2 == 0 else future
                tt(tmpM[:, :].rearrange("p (b t) -> p b t", b=NB), psum(n)[:, :].rearrange("p (b t) -> p b t", b=NB),
                   mask.unsqueeze(1).broadcast_to([P, NB, P]), ALU.add).then_inc(sig("masked"), 1)

            def denominator(i):
                n = TILE0[f"den{i}"]
                tile_wait(dve, n)
                gone_wait(dve, TILE0[f"guard{i}"])
                link(tt(den[:, i % 2, :], psum(n)[:, :], guard[:, i % 2, :], ALU.max))
                free(stt(den[:, i % 2, :], psum(n)[:, :], -1.0, den[:, i % 2, :], ALU.mult, ALU.max), n)

            def output_m(i):
                h, d = i // 2, i % 2
                dve.wait_ge(sig("den_inverse"), i + 1)
                n = TILE0[f"num{i}"]
                free(tt(yd[:, :] if d else Y[:, h, :], psum(n)[:, :], den[:, i % 2, :], ALU.mult), n)
                gone_wait(dve, n)
                if d:
                    tt(Y[:, h, :], Y[:, h, :], yd[:, :], ALU.add).then_inc(sig("head_ready"), 1)

            mask_m(0)
            for i in range(10):
                if i < 8:
                    h, d = i // 2, i % 2
                    gone_wait(dve, TILE0[f"max{i}"])
                    gone_wait(dve, s_tile(h, 3))
                    for j in range(NB):
                        cols = slice(j * P, S) if d == 0 else slice(0, j * P + P)
                        last = tt(PM[:, i % 2, j, cols], ST[:, j, cols], DT[:, j, cols], ALU.mult)
                    last.then_inc(sig("weights_m"), 1)
                if i < 7:
                    mask_m(i + 1)
                if i >= 2:
                    output_m(i - 2)
                if 1 <= i < 9:
                    denominator(i - 1)

            def head_norms(stage, chunk0, gain, gate):
                def finish(h):
                    dve.wait_ge(sig("y_hi"), 4 * stage + h + 1)
                    tt(actL[:, chunk0 + h, :], ht[:, h % 2, :], actH[:, chunk0 + h, :].bitcast(F32), ALU.subtract)\
                        .then_inc(sig("y_ready"), 1)
                for h in range(4):
                    dve.wait_ge(sig("head_root"), 4 * stage + h + 1)
                    if h >= 2:
                        dve.wait_ge(sig("y_ready"), 4 * stage + h - 1)
                    link(stt(ht[:, h % 2, :], Y[:, h, :], v(gain, h), hr[:, h % 2, :], ALU.mult, ALU.mult))
                    dve.wait_ge(sig("gate_act"), 4 * stage + h + 1)
                    tt(ht[:, h % 2, :], ht[:, h % 2, :], gate[:, h, :], ALU.mult).then_inc(sig("head_out"), 1)
                    if h >= 1:
                        finish(h - 1)
                finish(3)
            head_norms(0, 0, "mnorm", gateO)

            for cc in range(2):
                fw, bw = cumF[:, cc], cumF[:, 2 + cc]

                def level_arg(lev):
                    half = 2 ** (lev - 1)
                    s_ = lev % 2
                    used = cc * 9 + (lev - 2 if lev > 2 else 0)
                    if used > 0:
                        dve.wait_ge(sig("level_qk"), used)

                    def halves(a):
                        return a.rearrange("p (n two h) -> p n two h", two=2, h=half)
                    at_, after = halves(fw[:, 0:S]), halves(fw[:, 1:1 + S])
                    bat = halves(bw[:, 0:S])
                    q_, k_ = halves(arg[:, s_, 0, :]), halves(arg[:, s_, 1, :])
                    wide = [P, S // (2 * half), half]
                    mid, bmid = at_[:, :, 1, 0:1].broadcast_to(wide), bat[:, :, 1, 0:1].broadcast_to(wide)
                    tt(q_[:, :, 1, :], after[:, :, 1, :], mid, ALU.subtract)
                    tt(k_[:, :, 0, :], mid, after[:, :, 0, :], ALU.subtract)
                    tt(q_[:, :, 0, :], bmid, bat[:, :, 0, :], ALU.subtract)
                    tt(k_[:, :, 1, :], bat[:, :, 1, :], bmid, ALU.subtract).then_inc(sig("level_arg"), 1)

                def level_apply(lev):
                    dve.wait_ge(sig("level_exp"), cc * 9 + lev)
                    tt(qkL[:, lev % 2, :, :], arg[:, lev % 2, :, :], qkB[:, :, cc, :], ALU.mult)\
                        .then_inc(sig("level_qk"), 1)

                def level_take(lev):
                    for hh in range(2):
                        n = TILE0[f"lev{cc}_{lev}"] + hh
                        tile_wait(dve, n)
                        src = psum(n)[:, :].rearrange("p (b t) -> p b t", b=NB)
                        if lev == 0:
                            free(tt(Pd[:, hh, :, :], src, twice.unsqueeze(1).broadcast_to([P, NB, P]), ALU.mult), n)
                        elif lev < 8:
                            gone_wait(dve, TILE0[f"lev{cc}_{lev - 1}"] + hh)
                            free(nc.vector.copy_predicated(
                                Pd[:, hh, :, :], MASK[:, lev - 1, :].unsqueeze(1).broadcast_to([P, NB, P]), src), n)
                if cc > 0:
                    tile_wait(dve, TILE0[f"o{cc - 1}"] + 1)
                level_arg(1)
                for lev in range(1, 10):
                    if lev < 9:
                        level_arg(lev + 1)
                    if lev >= 2:
                        level_take(lev - 2)
                    level_apply(lev)
                for hh in range(2):
                    n = TILE0[f"o{cc}"] + hh
                    tile_wait(dve, n)
                    free(nc.vector.tensor_copy(Y[:, 2 * cc + hh, :], psum(n)[:, :]), n)
                    gone_wait(dve, n)
                    nc.vector.tensor_copy(tmpY[:, :], Y[:, 2 * cc + hh, 0:1]).then_inc(sig("head_ready"), 1)
            head_norms(1, 4, "gnorm", gateR)
            for c_ in range(KD):
                add_squares(c_ == 0)
            post_norm("mix_post", "ffn_pre")
            feed_forward(0, None)
            post_norm("ffn_post", "mix2_0")

            root_wait()
            for i in range(4):
                nc.vector.memset(upad[:, i, 0:PADU], 0.0)
                nc.vector.memset(glp[:, i, 0:32], 0.0)
            scaled(upad[:, 0, PADU:], TILE0["pc_in"])
            gone_wait(dve, TILE0["pc_in"])
            dve.wait_ge(mem_in, 48)
            for c_ in range(KD):
                add_squares(c_ == 0, MEM)
            for i in range(1, 4):
                scaled(upad[:, i, PADU:], TILE0["pc_in"] + i)
            for i in range(4):
                scaled(glp[:, i, 30:30 + S], TILE0["pc_in"] + 4 + i)

            def memory_low(l):
                for c_ in range(KD):
                    low(memL[l][:, c_, :], memT[:, c_, :], v(f"mem{l}", c_), memH[l][:, c_, :])
            for i in range(4):
                if i >= 2:
                    dve.wait_ge(sig("glu_gate"), i - 1)
                scaled(sigb[:, i % 2, :], TILE0["pc_in"] + 8 + i)
                if i > 0:
                    dve.wait_ge(sig("glu_gate"), i)
                    link(tt(glp[:, i - 1, 30:30 + S], glp[:, i - 1, 30:30 + S], sigb[:, (i - 1) % 2, :], ALU.mult))
                if i == 1:
                    dve.wait_ge(sig("mem_root"), 1)
                    for c_ in range(KD):
                        tt(memT[:, c_, :], memT[:, c_, :], rmem[:, :], ALU.mult).then_inc(sig("mem_normed"), 1)
                if i == 2:
                    memory_low(0)
            dve.wait_ge(sig("glu_gate"), 4)
            link(tt(glp[:, 3, 30:30 + S], glp[:, 3, 30:30 + S], sigb[:, 1, :], ALU.mult))
            memory_low(1)
            dve.wait_ge(unit_done, LAST["pc_in"])
            for g, w in enumerate(POOL_WINDOWS):
                src, shift, bufs = upad[:, g, :], 1, [wina, winb]
                while shift < w:
                    dst = bufs[0]
                    lo = 2 * shift - 1
                    link(tt(dst[:, lo:], src[:, lo:], src[:, lo - shift:S + PADU - shift], ALU.add))
                    src, shift, bufs = dst, 2 * shift, bufs[::-1]
                link(stt(pooled[:, g, :], src[:, PADU:], 1.0 / w, upad[:, g, PADU:], ALU.mult, ALU.subtract))
                link(tt(meanb[:, 0:16], src[:, PADU:PADU + 16], CT[:, CONST["inv_count"] + 16 * g:
                        CONST["inv_count"] + 16 * g + 16], ALU.mult))
                tt(pooled[:, g, 0:16], meanb[:, 0:16], upad[:, g, PADU:PADU + 16], ALU.subtract)\
                    .then_inc(sig("pooled"), 1)
            for k in range(CONV_K):
                for c_ in range(4):
                    tap = glp[:, c_, k:k + S]
                    w = v("dw_w", c_ * CONV_K + k)
                    if k == 0:
                        ins = ts(cvb[:, c_, :], tap, w, v("dw_b", c_), ALU.mult, ALU.add)
                    else:
                        dve.wait_ge(sig("conv31"), 4 * (k - 1) + c_ + 1)
                        ins = stt(cvb[:, c_, :], tap, w, cvb[:, c_, :], ALU.mult, ALU.add)
                    ins.then_inc(sig("conv31"), 1)
                if k in POOL_LOW_AT:
                    g = POOL_LOW_AT.index(k)
                    dve.wait_ge(sig("pool_hi"), g + 1)
                    tt(poolL[:, g, :], ybuf[:, g % 2, :], actH[:, g, :].bitcast(F32), ALU.subtract)\
                        .then_inc(sig("pool_out"), 1)
            dve.wait_ge(sig("conv31"), 4 * CONV_K)
            link(tt(ssq[:, :], cvb[:, 0, :], cvb[:, 1, :], ALU.add))
            link(tt(ssq[:, :], ssq[:, :], cvb[:, 2, :], ALU.add))
            tt(ssq[:, :], ssq[:, :], cvb[:, 3, :], ALU.add).then_inc(sig("ln_sum"), 1)

            n = TILE0["ln_mean"]
            tile_wait(dve, n)
            free(ts(meanb[:, :], psum(n)[:, :], 1.0 / S, None, ALU.mult), n)
            gone_wait(dve, n)
            for c_ in range(4):
                tt(cvb[:, c_, :], cvb[:, c_, :], meanb[:, :], ALU.subtract).then_inc(sig("centred"), 1)
            for c_ in range(4):
                add_squares(c_ == 0)
            root_wait()
            for c_ in range(4):
                tt(cvb[:, c_, :], cvb[:, c_, :], rstd[:, :], ALU.mult).then_inc(sig("scaled"), 1)
            for c_ in range(4):
                dve.wait_ge(sig("conv_hi"), c_ + 1)
                tt(actL[:, 4 + c_, :], ybuf[:, c_ % 2, :], actH[:, 4 + c_, :].bitcast(F32), ALU.subtract)\
                    .then_inc(sig("conv_out"), 1)

            def add_to_x(name, next_norm):
                for m in range(KD):
                    n = pc_tile(m) if name == "pc_out" else TILE0[name] + m
                    tile_wait(dve, n)
                    free(tt(XT[:, m, :], psum(n)[:, :], XT[:, m, :], ALU.add), n)
                    if m > 0:
                        norm_chunk(next_norm, m - 1)
                norm_chunk(next_norm, KD - 1)
            add_to_x("pc_out", "xa0")

            def cross_attention(l, next_norm):
                base = TILE0[f"xatt{l}"]
                root_wait()
                for i in range(KD):
                    scaled(qX[:, i, :], TILE0[f"xq{l}"] + i)

                def output_low(h):
                    for f in range(2):
                        dve.wait_ge(sig("x_hi"), 8 * l + 2 * h + f + 1)
                        n = xtile(base, "o", h, f)
                        free(tt(actL[:, 2 * h + f, :], psum(n)[:, :], actH[:, 2 * h + f, :].bitcast(F32),
                                ALU.subtract), n)
                for h in range(4):
                    for pair in range(2):
                        n = xtile(base, "s", h, pair)
                        tile_wait(dve, n)
                        link(nc.vector.reduce_max(xst[:, pair, 0:2], psum(n)[:, :].rearrange("p (q m) -> p q m", q=2),
                                                  AX.X))
                        ts(xst[:, pair, 2:4], xst[:, pair, 0:2], -1.0 / 16, None, ALU.mult).then_inc(sig("x_max"), 1)
                    for pair in range(2):
                        gone_wait(dve, xtile(base, "s", h, pair))
                        link(nc.vector.reciprocal(xst[:, pair, 6:8], xst[:, pair, 4:6]))
                        for q in range(2):
                            last = ts(EX[:, pair, q, :], EX[:, pair, q, :], xst[:, pair, 6 + q:7 + q], None, ALU.mult)
                        last.then_inc(sig("x_probs"), 1)
                    if h >= 2:
                        output_low(h - 2)
                output_low(2)
                output_low(3)
                add_to_x(f"xo{l}", next_norm)

            cross_attention(0, "ffn2_0")
            feed_forward(1, "mix2_1")

            link(nc.vector.tensor_copy(posF[:, :], posI[:, :]))
            freq = CT[:, CONST["inv_freq"]:CONST["inv_freq"] + 16].unsqueeze(1).broadcast_to([P, NB, 16])
            link(tt(angA[:, :, :], freq, posF[:, :].unsqueeze(2).broadcast_to([P, NB, 16]), ALU.mult))
            link(ts(angB[:, :, :], angA[:, :, :], 1.0 / TWO_PI, ROUND, ALU.mult, ALU.add))
            link(ts(angB[:, :, :], angB[:, :, :], ROUND, None, ALU.subtract))
            for part in (TWO_PI_A, TWO_PI_B, TWO_PI_C):
                link(stt(angA[:, :, :], angB[:, :, :], -part, angA[:, :, :], ALU.mult, ALU.add))
            link(ts(angC[:, :, :], angA[:, :, :], TWO_PI / 4, TWO_PI / 2, ALU.add, ALU.is_gt))
            link(stt(angC[:, :, :], angC[:, :, :], -TWO_PI, angA[:, :, :], ALU.mult, ALU.add))
            link(ts(angC[:, :, :], angC[:, :, :], TWO_PI / 4, None, ALU.add))
            ts(angB[:, :, :], angA[:, :, :], 3.1415925, -3.1415925, ALU.min, ALU.max).then_inc(sig("angle"), 1)
            ts(angC[:, :, :], angC[:, :, :], 3.1415925, -3.1415925, ALU.min, ALU.max).then_inc(sig("angle"), 1)
            root_wait()
            for i in range(5):
                g_ = v("q_norm", i) if i < 3 else v("kv_norm", i - 3)
                n = TILE0["w_dq"] + i
                scaled(qpn[:, i % 2, :], n)
                gone_wait(dve, n)
                dve.wait_ge(sig("lora_sq"), i + 1)
                dst, src = sq[:, i // 3, :], qpr[:, i % 2, :]
                if i in (0, 3):
                    ins = nc.vector.tensor_copy(dst, src)
                else:
                    ins = tt(dst, dst, src, ALU.add)
                ins.then_inc(sig("lora_added"), 1)
                dve.wait_ge(sig("lora_added"), i + 1)
                dve.wait_ge(sig("c_hi"), i + 1)
                stt(cL[:, i, :], qpn[:, i % 2, :], g_, cH[:, i, :].bitcast(F32), ALU.mult, ALU.subtract)\
                    .then_inc(sig("c_ready"), 1)

            def contents(name, dst, root):
                for i in range(8):
                    n = TILE0[name] + i
                    tile_wait(dve, n)
                    tt(dst[0:64, 2 * i, :], psum(n)[0:64, :], root[0:64, :], ALU.mult)
                    free(tt(dst[0:64, 2 * i + 1, :], psum(n)[64:P, :], root[64:P, :], ALU.mult), n)
            dve.wait_ge(sig("lora_root"), 1)
            contents("q_nope", QC, rq)

            def rotate(dst, src, b, heads):
                w = [P, heads, 16]
                cos, sin = cosT[:, b:b + 1, :].broadcast_to(w), sinT[:, b:b + 1, :].broadcast_to(w)
                x1, x2 = src[:, :, 0:16], src[:, :, 16:32]
                t = [z.rearrange("p (h c) -> p h c", c=16) for z in
                     (ssq[:, 0:16 * heads], ssq[:, 256:256 + 16 * heads], lnv[:, 0:16 * heads],
                      lnv[:, 256:256 + 16 * heads])]
                tt(t[0], x1, cos, ALU.mult)
                tt(t[1], x2, sin, ALU.mult)
                tt(t[2], x1, sin, ALU.mult)
                link(tt(t[3], x2, cos, ALU.mult))
                tt(dst[:, :, 0:16], t[0], t[1], ALU.subtract)
                return tt(dst[:, :, 16:32], t[2], t[3], ALU.add)
            dve.wait_ge(sig("turned"), 2)
            gone_wait(dve, TILE0["k_pe"])
            for b in range(NB):
                last = rotate(kpr[:, b:b + 1, :], kpn[:, b:b + 1, :], b, 1)
                if b < NB - 1:
                    link(last)
            last.then_inc(sig("k_rotated"), 1)
            dve.wait_ge(sig("k_rotated"), 1)
            for b in range(NB):
                gone_wait(dve, TILE0["q_pe"] + b)
                if b == 2:
                    root_wait()
                    contents("k_nope", KC, rstd)
                if b >= 2:
                    tile_wait(dve, turn_tile(b - 2))
                if b == 3:
                    n = TILE0["k_turn"]
                    tile_wait(dve, n)
                    dve.wait_ge(sig("k_rows"), 1)
                    free(nc.vector.tensor_copy(KC[64:96, 0:8, :],
                                               psum(n)[0:32, :].unsqueeze(1).broadcast_to([32, 8, S])), n)
                rotate(qpr[:, b % 2, :].rearrange("p (h c) -> p h c", c=32),
                       qpn[:, b % 2, :].rearrange("p (h c) -> p h c", c=32), b, MLA_HEADS).then_inc(sig("q_rotated"), 1)
                dve.wait_ge(sig("q_rotated"), b + 1)
            n = turn_tile(3)
            tile_wait(dve, n)
            for j in range(4):
                last = nc.vector.tensor_copy(QC[64:96, j:MLA_HEADS:4, 3 * P:S],
                                             psum(n)[32 * j:32 * j + 32, :].rearrange("p (g t) -> p g t", g=4))
            free(last, n)

            scale = (64 + 32) ** -0.5

            def att_low(h):
                dve.wait_ge(sig("m_hi"), h + 1)
                n = mtile("o", h, 0)
                rows = slice(64 * (h % 2), 64 * (h % 2) + 64)
                free(tt(oHL[rows, h // 2 * 2 + 1, :], psum(n)[rows, :], oHL[rows, h // 2 * 2, :].bitcast(F32),
                        ALU.subtract), n)

            def att_rows(h):
                for b in (1, 3):
                    n = mtile("t", h, b)
                    tile_wait(dve, n)
                    if h >= 2:
                        tile_wait(dve, mtile("o", h - 2, 0))
                    free(nc.vector.tensor_copy(PX2[:, h % 2, 0:b + 1, b * P:b * P + P],
                                               psum(n)[:, 0:(b + 1) * P].rearrange("p (j q) -> p j q", q=P)), n)

            for i in range(MLA_HEADS):
                s_ = i % 2
                for b in range(NB):
                    n = mtile("s", i, b)
                    tile_wait(dve, n)
                    last = nc.vector.reduce_max(mst[:, s_, b:b + 1], psum(n)[:, 0:(b + 1) * P], AX.X)
                link(last)
                ts(mst[:, s_, 4:8], mst[:, s_, 0:4], -scale, None, ALU.mult).then_inc(sig("m_max"), 1)
                if i >= 2:
                    att_low(i - 2)
                if i >= 1:
                    att_rows(i - 1)
                for b in range(NB):
                    gone_wait(dve, mtile("s", i, b))
                link(nc.vector.reciprocal(mst[:, s_, 12:16], mst[:, s_, 8:12]))
                for b in range(NB):
                    w = (b + 1) * P
                    ts(EM[:, s_, b, 0:w], EM[:, s_, b, 0:w], mst[:, s_, 12 + b:13 + b], None, ALU.mult)\
                        .then_inc(sig("m_probs"), 1)
            att_low(MLA_HEADS - 2)
            att_rows(MLA_HEADS - 1)
            att_low(MLA_HEADS - 1)
            add_to_x("mla_o", "xa1")
            cross_attention(1, "ffn2_1")
            feed_forward(2, "final")
            root_wait()
            for c_ in range(KD):
                stt(MIX[:, c_, :], XT[:, c_, :], v("final", c_), rstd[:, :], ALU.mult, ALU.mult)\
                    .then_inc(sig("final"), 1)


def columns(a):
    return a.reshape(-1, P).T


def stationary(w):
    k, n = w.shape
    return w.reshape(k // P, P, n // P, P).transpose(2, 1, 0, 3).reshape(n // P, P, k)


def moving(w):
    k, n = w.shape
    units = []
    for g in range(n // S):
        chunks = [w[c * P:c * P + P, g * S:g * S + S] for c in range(k // P)]
        for i in range(0, len(chunks), 2):
            units.append(np.concatenate(chunks[i:i + 2], axis=1))
    return units


def lay_weights(a):
    w_in = a["w_in"][0]
    widths = (512, 512, 512, 16, 256, 256, 512, 512, 32)
    a_qk, a_v, a_o, gates, b_q, b_k, b_v, b_r, b_lr = np.split(w_in, np.cumsum(widths)[:-1], axis=1)
    gates = gates.reshape(D, 4, 4)[:, [0, 2, 1, 3]].reshape(D, 16)
    small = np.concatenate([gates, b_lr], axis=1)
    kpe = a["mla_w_dq_dkv_2"][0][:, 640:672]
    uq = a["mla_w_uq_2"][0].reshape(384, MLA_HEADS, 96)
    ukv = a["mla_w_ukv_2"][0].reshape(256, MLA_HEADS, 128)

    def narrow(w):
        return [w.reshape(KD, P, -1).transpose(1, 0, 2).reshape(P, -1)]

    def grouped(w, per):
        st = stationary(w)
        return [np.concatenate(list(st[i:i + per]), axis=1) for i in range(0, len(st), per)]
    whole = stationary(a["pc_w_out_2"][0])
    pc_out = [np.concatenate([whole[2 * i][:, cut], whole[2 * i + 1][:, cut]], axis=1)
              for cut in (slice(0, 4 * P), slice(4 * P, 8 * P)) for i in range(3)] + [whole[6], whole[7]]
    groups = {
        "lr_gates": narrow(small), "a_qk": stationary(a_qk), "b_qk": stationary(np.concatenate([b_q, b_k], axis=1)),
        "a_v": moving(a_v), "b_v": moving(b_v), "a_o": stationary(a_o), "b_r": stationary(b_r),
        "w_out": stationary(a["w_out"][0]), "pc_in": stationary(a["pc_w_in_2"][0]),
        "pc_out": pc_out, "k_pe": narrow(kpe),
        "w_dq": stationary(a["mla_w_dq_dkv_2"][0][:, :640]),
        "q_nope": grouped(uq[:, :, :64].reshape(384, 1024), 2), "q_pe": moving(uq[:, :, 64:].reshape(384, 512)),
        "k_nope": grouped(ukv[:, :, :64].reshape(256, 1024), 4), "mla_v": moving(ukv[:, :, 64:].reshape(256, 1024)),
        "mla_o": stationary(a["mla_w_o_2"][0]),
    }
    for l in range(2):
        groups[f"mem_k{l}"] = stationary(a["xa_wkv_2"][l][:, :D])
        groups[f"mem_v{l}"] = moving(a["xa_wkv_2"][l][:, D:])
        groups[f"xq{l}"] = stationary(a["xa_wq_2"][l])
        groups[f"xo{l}"] = stationary(a["xa_wo_2"][l])
    layers = [(a["ffn_w_gate"][0], a["ffn_w_up"][0], a["ffn_w_down"][0])]
    for l in range(2):
        up = a["ffn_w_up_2"][l]
        layers.append((up[:, FF:], up[:, :FF], a["ffn_w_down_2"][l]))
    for i, (gate, up, down) in enumerate(layers):
        pairs = np.stack([stationary(gate), stationary(up)], axis=1).reshape(2 * NF, P, D)
        at = 0
        for t, c in enumerate(THIRDS):
            groups[f"ff{i}_gu{t}"] = pairs[2 * at:2 * (at + c)]
            groups[f"ff{i}_d{t}"] = stationary(down[at * P:(at + c) * P])
            at += c
    laid = np.zeros((NUNITS, P, UNIT), np.float32)
    for name, count, width in UNITS:
        assert len(groups[name]) == count, name
        for i, w in enumerate(groups[name]):
            laid[UNIT0[name] + i, :, :w.shape[1]] = w
    return laid


def lay_vectors(a):
    cols = {
        "mix_pre": a["norm_mix_pre"][0], "mix_post": a["norm_mix_post"][0], "ffn_pre": a["norm_ffn_pre"][0],
        "ffn_post": a["norm_ffn_post"][0], "mix2_0": a["norm_mix_g_2"][0], "mix2_1": a["norm_mix_g_2"][1],
        "xa0": a["norm_xa_g_2"][0], "xa1": a["norm_xa_g_2"][1], "mem0": a["norm_mem_g_2"][0],
        "mem1": a["norm_mem_g_2"][1], "ffn2_0": a["norm_ffn_g_2"][0], "ffn2_1": a["norm_ffn_g_2"][1],
        "final": a["final_norm_g_2"], "mconv_b": a["mlstm_conv_b"][0], "mnorm": a["mlstm_norm"][0],
        "gla_b": a["gla_b"][0], "gnorm": a["gla_norm"][0], "fconv_b0": a["ffn_conv_b"][0],
        "fconv_b1": a["ffn_conv_b_2"][0], "fconv_b2": a["ffn_conv_b_2"][1], "pool_scale": a["pool_scale_2"][0],
        "dw_b": a["conv_dw_b_2"][0], "ln_g": a["conv_ln_g_2"][0], "ln_b": a["conv_ln_b_2"][0],
        "q_norm": a["mla_q_norm_g_2"][0], "kv_norm": a["mla_kv_norm_g_2"][0],
    }
    laid = np.zeros((P, NVEC), np.float32)
    for name, w in cols.items():
        c = columns(w)
        laid[:, VEC[name]:VEC[name] + c.shape[1]] = c
    for name, w in (("mconv_w", a["mlstm_conv_w"][0]), ("fconv_w0", a["ffn_conv_w"][0]),
                    ("fconv_w1", a["ffn_conv_w_2"][0]), ("fconv_w2", a["ffn_conv_w_2"][1]),
                    ("dw_w", a["conv_dw_w_2"][0])):
        taps, width = w.shape
        c = w.reshape(taps, width // P, P).transpose(2, 1, 0).reshape(P, -1)
        laid[:, VEC[name]:VEC[name] + c.shape[1]] = c
    laid[:, VEC["gate_b"]:VEC["gate_b"] + 16] = a["mlstm_gate_b"][0].reshape(4, 4)[[0, 2, 1, 3]].reshape(16)
    laid[:, VEC["eps"]] = 1e-6
    laid[:, VEC["one"]] = 1.0
    return laid


def constants():
    p, f = np.arange(P)[:, None], np.arange(P)[None, :]
    laid = np.zeros((P, NCONST), np.float32)

    def put(name, w):
        laid[:, CONST[name]:CONST[name] + w.shape[1]] = w
    put("ident", (p == f) * 1.0)
    put("ones", np.ones((P, P)))
    put("past", (f < p) * BIG)
    put("future", (f > p) * BIG)
    put("upto", (p <= f) * 1.0)
    put("since", (p >= f) * 1.0)
    put("twice", (p == f) * 2.0)
    put("neg_future", (f > p) * -BIG)
    counts = [np.minimum(np.arange(16) + 1, w).astype(np.float32) for w in POOL_WINDOWS]
    put("inv_count", np.tile(np.concatenate([np.float32(1.0) / c for c in counts]), (P, 1)))
    inv = np.float32(1.0) / (np.float32(10000.0) ** (np.arange(0, 32, 2, dtype=np.float32) / np.float32(32)))
    put("inv_freq", np.tile(inv.astype(np.float32), (P, 1)))
    masks = np.stack([((p // (2 * h) == f // (2 * h)) & (p // h != f // h)) for h in HALVES], axis=1).astype(np.int32)
    return laid, masks


def kernel(**inputs):
    import concourse.bacc as bacc
    from concourse.bass_utils import run_bass_kernel_spmd

    a = {k: np.asarray(w) for k, w in inputs.items()}
    consts, masks = constants()
    w2 = np.zeros((32, 2, 256), np.float32)
    w2[0:16, 0], w2[16:32, 1] = a["gla_w2"][0, 0], a["gla_w2"][0, 1]
    arrays = {
        "x_t": np.ascontiguousarray(a["x"][0].T), "mem_t": np.ascontiguousarray(a["mem_2"][0].T),
        "positions": np.ascontiguousarray(a["positions_2"][0].reshape(NB, P).T),
        "weights": lay_weights(a), "pool_w": np.ascontiguousarray(a["pool_w_2"][0]), "gla_w2": w2,
        "vecs": lay_vectors(a), "consts": consts, "masks": masks,
    }
    nc = bacc.Bacc("TRN2", target_bir_lowering=False, num_devices=1, dynamic_dma_scratch_size=1024)
    args = {n: nc.dram_tensor(n, w.shape, mybir.dt.from_np(w.dtype), kind="ExternalInput").ap()
            for n, w in arrays.items()}
    out = nc.dram_tensor("out", (D, S), F32, kind="ExternalOutput").ap()
    program(nc, out=out, **args)
    result = run_bass_kernel_spmd(nc, [arrays], core_ids=[0])
    return np.ascontiguousarray(result.results[0]["out"].T).reshape(1, S, D)
```
